# Optimizing a Trainium2 kernel written in Bass

```python
import jax, jax.numpy as jnp
from jax import lax
import numpy as np

D_MODEL = 2048
BATCH = 1
SEQ = 512
DEPTH = 1
DEC_BATCH = 1
DEC_SEQ = 32
PAST_LEN = 128

CHUNK = 64
Q_BLOCK = 128
EPS = 1e-6
NEG_INF = -1e30
N_MOD = 6
MLA_HEADS = 8
QK_NOPE = 128
QK_ROPE = 64
V_HEAD = 128
KV_LORA = 512
ROPE_THETA = 10000.0
FOX_HEADS = 8
FOX_HEAD_DIM = 128
FORGET_BIAS_INIT = 2.0
PEER_HEADS = 8
N_KEYS = 128
N_EXPERTS = N_KEYS * N_KEYS
PEER_QDIM = 256
PEER_TOPK = 16
PEER_BLOCK = 128

MLA_Q_COLS = MLA_HEADS * (QK_NOPE + QK_ROPE)
FOX_COLS = FOX_HEADS * FOX_HEAD_DIM
SPLIT_0 = MLA_Q_COLS
SPLIT_1 = SPLIT_0 + KV_LORA
SPLIT_2 = SPLIT_1 + QK_ROPE
SPLIT_3 = SPLIT_2 + 3 * FOX_COLS
SPLIT_4 = SPLIT_3 + FOX_HEADS
SPLIT_5 = SPLIT_4 + D_MODEL
IN_COLS = SPLIT_5 + D_MODEL

kernel_name = "mla_fox_peer_streaming_encoder_step"

def rms_norm(x, g):
    x32 = x.astype(jnp.float32)
    y = x32 * lax.rsqrt(jnp.mean(x32 * x32, axis=-1, keepdims=True) + EPS)
    return (y * g.astype(jnp.float32)).astype(x.dtype)

def modulate(x, g, shift, scale):
    return rms_norm(x, g) * (1 + scale[:, None, :]) + shift[:, None, :]

def rope(x, pos):
    half = QK_ROPE // 2
    inv = 1.0 / (ROPE_THETA ** (jnp.arange(0, QK_ROPE, 2, dtype=jnp.float32) / QK_ROPE))
    ang = pos.astype(jnp.float32)[:, None] * inv[None, :]
    cos = jnp.cos(ang)[None, :, None, :]
    sin = jnp.sin(ang)[None, :, None, :]
    x32 = x.astype(jnp.float32)
    x1, x2 = x32[..., :half], x32[..., half:]
    return jnp.concatenate([x1 * cos - x2 * sin, x1 * sin + x2 * cos], axis=-1).astype(x.dtype)

def block_attention(q, k, v, q_pos, k_pos, chunk_causal, f_q=None, f_k=None):
    b, sq, h, dk = q.shape
    scale = dk ** -0.5

    def attend(args):
        qb, pb, fb = args
        s = jnp.einsum('bqhd,bkhd->bhqk', qb, k).astype(jnp.float32) * scale
        if f_k is not None:
            s = s + (jnp.swapaxes(fb, 1, 2)[..., :, None] - jnp.swapaxes(f_k, 1, 2)[..., None, :])
        if chunk_causal:
            ok = (pb[:, None] // CHUNK) >= (k_pos[None, :] // CHUNK)
        else:
            ok = pb[:, None] >= k_pos[None, :]
        s = jnp.where(ok, s, NEG_INF)
        p = jax.nn.softmax(s, axis=-1).astype(v.dtype)
        return jnp.einsum('bhqk,bkhd->bqhd', p, v)

    if sq > Q_BLOCK and sq % Q_BLOCK == 0:
        nb = sq // Q_BLOCK
        to_blocks = lambda a: jnp.moveaxis(a.reshape((b, nb, Q_BLOCK) + a.shape[2:]), 1, 0)
        fb = None if f_q is None else to_blocks(f_q)
        out = lax.map(attend, (to_blocks(q), q_pos.reshape(nb, Q_BLOCK), fb))
        return jnp.moveaxis(out, 0, 1).reshape(b, sq, h, -1)
    return attend((q, q_pos, f_q))

def mla_mixer(q_cols, ckv, kr, pos, cache_lat, cache_kr, kv_norm_g, w_ukv):
    b, s, _ = q_cols.shape
    q = q_cols.reshape(b, s, MLA_HEADS, QK_NOPE + QK_ROPE)
    q = jnp.concatenate([q[..., :QK_NOPE], rope(q[..., QK_NOPE:], pos)], axis=-1)
    lat = rms_norm(ckv, kv_norm_g)
    k_r = rope(kr[:, :, None, :], pos)[:, :, 0, :]
    lat_all = jnp.concatenate([cache_lat, lat], axis=1)
    kr_all = jnp.concatenate([cache_kr, k_r], axis=1)
    n_keys = lat_all.shape[1]
    kv = jnp.einsum('blc,ce->ble', lat_all, w_ukv).reshape(b, n_keys, MLA_HEADS, QK_NOPE + V_HEAD)
    k_nope, v = kv[..., :QK_NOPE], kv[..., QK_NOPE:]
    k = jnp.concatenate([k_nope, jnp.broadcast_to(kr_all[:, :, None, :], (b, n_keys, MLA_HEADS, QK_ROPE))], axis=-1)
    k_pos = jnp.arange(n_keys, dtype=jnp.int32)
    o = block_attention(q, k, v, pos, k_pos, True)
    return o.reshape(b, s, MLA_HEADS * V_HEAD), lat, k_r

def fox_mixer(qkv, f_logit, f_bias, pos, cache_k, cache_v, cache_logf):
    b, s, _ = qkv.shape
    past = cache_k.shape[1]
    qkv = qkv.reshape(b, s, 3, FOX_HEADS, FOX_HEAD_DIM)
    q, k, v = qkv[:, :, 0], qkv[:, :, 1], qkv[:, :, 2]
    logf = jax.nn.log_sigmoid(f_logit.astype(jnp.float32) + f_bias.astype(jnp.float32))
    k_all = jnp.concatenate([cache_k, k], axis=1)
    v_all = jnp.concatenate([cache_v, v], axis=1)
    f_all = jnp.cumsum(jnp.concatenate([cache_logf.astype(jnp.float32), logf], axis=1), axis=1)
    k_pos = jnp.arange(past + s, dtype=jnp.int32)
    o = block_attention(q, k_all, v_all, pos, k_pos, False, f_all[:, past:], f_all)
    return o.reshape(b, s, FOX_COLS), k, v, logf

def peer_ffn(h, w_q, keys1, keys2, u_tab, v_tab):
    b, s, d = h.shape
    t = b * s
    hf = h.reshape(t, d)
    q = (hf @ w_q).reshape(t, PEER_HEADS, PEER_QDIM).astype(jnp.float32)
    half = PEER_QDIM // 2
    s1 = jnp.einsum('thd,nd->thn', q[..., :half], keys1.astype(jnp.float32))
    s2 = jnp.einsum('thd,nd->thn', q[..., half:], keys2.astype(jnp.float32))
    v1, i1 = lax.top_k(s1, PEER_TOPK)
    v2, i2 = lax.top_k(s2, PEER_TOPK)
    cand = (v1[..., :, None] + v2[..., None, :]).reshape(t, PEER_HEADS, PEER_TOPK * PEER_TOPK)
    cidx = (i1[..., :, None] * N_KEYS + i2[..., None, :]).reshape(t, PEER_HEADS, PEER_TOPK * PEER_TOPK)
    sc, sel = lax.top_k(cand, PEER_TOPK)
    expert = jnp.take_along_axis(cidx, sel, axis=-1)
    gate = jax.nn.softmax(sc, axis=-1)
    pad = (-t) % PEER_BLOCK
    nb = (t + pad) // PEER_BLOCK
    hb = jnp.pad(hf, ((0, pad), (0, 0))).reshape(nb, PEER_BLOCK, d)
    eb = jnp.pad(expert, ((0, pad), (0, 0), (0, 0))).reshape(nb, PEER_BLOCK, PEER_HEADS, PEER_TOPK)
    gb = jnp.pad(gate, ((0, pad), (0, 0), (0, 0))).reshape(nb, PEER_BLOCK, PEER_HEADS, PEER_TOPK)

    def expert_block(args):
        hx, ex, gx = args
        a = jnp.einsum('td,thkd->thk', hx, u_tab[ex]).astype(jnp.float32)
        w = (gx * jax.nn.gelu(a, approximate=False)).astype(hx.dtype)
        return jnp.einsum('thk,thkd->td', w, v_tab[ex])

    out = lax.map(expert_block, (hb, eb, gb)).reshape(nb * PEER_BLOCK, d)[:t]
    return out.reshape(b, s, d)

def trunk_layer(x, c, cache_lat, cache_kr, cache_k, cache_v, cache_logf,
                w_ada, b_ada, norm1_g, w_in, fox_fbias, kv_norm_g, w_ukv, w_o_mla, w_o_fox,
                w_out, norm2_g, peer_wq, peer_keys1, peer_keys2, peer_u, peer_v):
    b, s, _ = x.shape
    past = cache_lat.shape[1]
    pos = past + jnp.arange(s, dtype=jnp.int32)
    mod = jax.nn.silu(c) @ w_ada + b_ada
    shift1, scale1, gate1, shift2, scale2, gate2 = jnp.split(mod, N_MOD, axis=-1)
    h = modulate(x, norm1_g, shift1, scale1)
    proj = h @ w_in
    q_mla, ckv, kr, qkv_fox, f_logit, g_mla, g_fox = jnp.split(
        proj, [SPLIT_0, SPLIT_1, SPLIT_2, SPLIT_3, SPLIT_4, SPLIT_5], axis=-1)
    o_mla, lat_new, kr_new = mla_mixer(q_mla, ckv, kr, pos, cache_lat, cache_kr, kv_norm_g, w_ukv)
    o_fox, k_new, v_new, logf_new = fox_mixer(qkv_fox, f_logit, fox_fbias, pos, cache_k, cache_v, cache_logf)
    merged = jax.nn.sigmoid(g_mla) * (o_mla @ w_o_mla) + jax.nn.sigmoid(g_fox) * (o_fox @ w_o_fox)
    x = x + gate1[:, None, :] * (merged @ w_out)
    h2 = modulate(x, norm2_g, shift2, scale2)
    x = x + gate2[:, None, :] * peer_ffn(h2, peer_wq, peer_keys1, peer_keys2, peer_u, peer_v)
    return x, (lat_new, kr_new, k_new, v_new, logf_new)

def setup_inputs(seed: int = 0) -> dict:
    key = jax.random.key(seed)
    ks = jax.random.split(key, 32)
    nrm = lambda k, shape, sc: jax.random.normal(k, shape, jnp.float32) * sc
    d = D_MODEL
    return {
        'x_prompt': nrm(ks[0], (BATCH, SEQ, d), 1.0),
        'x_sample': nrm(ks[1], (DEC_BATCH, DEC_SEQ, d), 1.0),
        'c_prompt': nrm(ks[2], (BATCH, d), 1.0),
        'c_sample': nrm(ks[3], (DEC_BATCH, d), 1.0),
        'cache_mla_latent': nrm(ks[4], (DEPTH, DEC_BATCH, PAST_LEN, KV_LORA), 1.0),
        'cache_mla_krope': nrm(ks[5], (DEPTH, DEC_BATCH, PAST_LEN, QK_ROPE), 1.0),
        'cache_fox_k': nrm(ks[6], (DEPTH, DEC_BATCH, PAST_LEN, FOX_HEADS, FOX_HEAD_DIM), 1.0),
        'cache_fox_v': nrm(ks[7], (DEPTH, DEC_BATCH, PAST_LEN, FOX_HEADS, FOX_HEAD_DIM), 1.0),
        'cache_fox_logf': jax.nn.log_sigmoid(nrm(ks[8], (DEPTH, DEC_BATCH, PAST_LEN, FOX_HEADS), 1.0) + FORGET_BIAS_INIT),
        'w_ada': nrm(ks[9], (DEPTH, d, N_MOD * d), 0.5 * d ** -0.5),
        'b_ada': nrm(ks[10], (DEPTH, N_MOD * d), 0.02),
        'norm1_g': 1.0 + nrm(ks[11], (DEPTH, d), 0.02),
        'w_in': nrm(ks[12], (DEPTH, d, IN_COLS), d ** -0.5),
        'fox_fbias': FORGET_BIAS_INIT + nrm(ks[13], (DEPTH, FOX_HEADS), 0.5),
        'kv_norm_g': 1.0 + nrm(ks[14], (DEPTH, KV_LORA), 0.02),
        'w_ukv': nrm(ks[15], (DEPTH, KV_LORA, MLA_HEADS * (QK_NOPE + V_HEAD)), KV_LORA ** -0.5),
        'w_o_mla': nrm(ks[16], (DEPTH, MLA_HEADS * V_HEAD, d), (MLA_HEADS * V_HEAD) ** -0.5),
        'w_o_fox': nrm(ks[17], (DEPTH, FOX_COLS, d), FOX_COLS ** -0.5),
        'w_out': nrm(ks[18], (DEPTH, d, d), d ** -0.5),
        'norm2_g': 1.0 + nrm(ks[19], (DEPTH, d), 0.02),
        'peer_wq': nrm(ks[20], (DEPTH, d, PEER_HEADS * PEER_QDIM), d ** -0.5),
        'peer_keys1': nrm(ks[21], (DEPTH, N_KEYS, PEER_QDIM // 2), (PEER_QDIM // 2) ** -0.5),
        'peer_keys2': nrm(ks[22], (DEPTH, N_KEYS, PEER_QDIM // 2), (PEER_QDIM // 2) ** -0.5),
        'peer_u': nrm(ks[23], (DEPTH, N_EXPERTS, d), d ** -0.5),
        'peer_v': nrm(ks[24], (DEPTH, N_EXPERTS, d), 1.0),
        'final_g': 1.0 + nrm(ks[25], (d,), 0.02),
    }

def reference(x_prompt, x_sample, c_prompt, c_sample, cache_mla_latent, cache_mla_krope,
              cache_fox_k, cache_fox_v, cache_fox_logf, w_ada, b_ada, norm1_g, w_in, fox_fbias,
              kv_norm_g, w_ukv, w_o_mla, w_o_fox, w_out, norm2_g, peer_wq, peer_keys1, peer_keys2,
              peer_u, peer_v, final_g):
    xp, xs = x_prompt, x_sample
    bp = xp.shape[0]
    states_p, states_s = [], []
    for l in range(DEPTH):
        w = (w_ada[l], b_ada[l], norm1_g[l], w_in[l], fox_fbias[l], kv_norm_g[l], w_ukv[l],
             w_o_mla[l], w_o_fox[l], w_out[l], norm2_g[l], peer_wq[l], peer_keys1[l],
             peer_keys2[l], peer_u[l], peer_v[l])
        xp, st_p = trunk_layer(xp, c_prompt,
                               jnp.zeros((bp, 0, KV_LORA), xp.dtype),
                               jnp.zeros((bp, 0, QK_ROPE), xp.dtype),
                               jnp.zeros((bp, 0, FOX_HEADS, FOX_HEAD_DIM), xp.dtype),
                               jnp.zeros((bp, 0, FOX_HEADS, FOX_HEAD_DIM), xp.dtype),
                               jnp.zeros((bp, 0, FOX_HEADS), jnp.float32), *w)
        xs, st_s = trunk_layer(xs, c_sample, cache_mla_latent[l], cache_mla_krope[l],
                               cache_fox_k[l], cache_fox_v[l], cache_fox_logf[l], *w)
        states_p.append(st_p)
        states_s.append(st_s)
    sp = [jnp.stack([st[i] for st in states_p]) for i in range(5)]
    ss = [jnp.stack([st[i] for st in states_s]) for i in range(5)]
    y_prompt = rms_norm(xp, final_g)
    y_sample = rms_norm(xs, final_g)
    return (y_prompt, y_sample, sp[0], sp[1], sp[2], sp[3], sp[4], ss[0], ss[1], ss[2], ss[3], ss[4])


_drawn_inputs = setup_inputs


def setup_inputs(seed=0):
    import zlib

    import numpy as np

    out = dict(_drawn_inputs(seed))
    spreads = {}
    factors = {'cache_mla_krope': 2.912,
     'cache_fox_logf': 20.399,
     'norm1_g': 2.987,
     'kv_norm_g': 2.995,
     'final_g': 7.396,
     'norm2_g': 2.872}
    for name, (base, spread) in spreads.items():
        noise = np.random.default_rng([zlib.crc32(name.encode()), seed]).standard_normal(out[name].shape)
        drawn = base * np.exp(spread * noise) if base else spread * noise
        out[name] = __import__('jax').numpy.asarray(drawn.astype(out[name].dtype))
    for name, factor in factors.items():
        out[name] = (out[name] * factor).astype(out[name].dtype)
    return out
```

```python
import numpy as np
import concourse.bass as bass
from concourse import mybir
from contextlib import ExitStack

D, TP, TS, PAST = 2048, 512, 32, 128
T = TP + TS
P = 128
KC = D // P
NH, HD, ROPE, LORA = 8, 128, 64, 512
NKEY = T + PAST
QT = TP // P
NT = QT + 1
HALF = T // 2
KHALF = NKEY // 2
CHUNK = 64
EPS = 1e-6
NEG = -1e30
SC_MLA = float(HD + ROPE) ** -0.5
SC_FOX = float(HD) ** -0.5
PH, NK, TOPK = 8, 128, 16
SLOTS = PH * TOPK
RING = 4
FB = 8
GR = 4

N_MOD = 6 * KC
ADA_A = 2 * KC
CKV, KRF, FOXV, MLAV = 4, 1, 8, 2
B_CKV = ADA_A
B_KRF = B_CKV + CKV
B_MLAV = B_KRF + KRF
B_MLA = B_MLAV + MLAV
B_FOXV = B_MLA + 4 * NH
B_FOX = B_FOXV + FOXV
B_MERGE = B_FOX + 4 * NH
B_OUT = B_MERGE + 4 * KC
B_WQ = B_OUT + 2 * KC
NB = B_WQ + KC

S_AT = [(2, 0), (3, 0), (2, 128), (4, 0), (3, 256)]
S_W = [128 * (t + 1) for t in range(QT)] + [TS + PAST]
P_AT = [0, 128, 384, 768, 1280]
P_W = P_AT[-1] + S_W[-1]
PT_AT = [0, 512, 896, 1152]
PT_S = 1280
PT_W = PT_S + 2 * TS


def rows(t):
    return P if t < QT else TS


def const_layout():
    names = [("ident", P), ("stack", P), ("band", TP), ("mask_mla", P), ("mask_fox", P), ("iota", TOPK),
             ("cos", T), ("sin", T), ("ones", P), ("zeros", P)]
    at, out = 0, {}
    for n, w in names:
        out[n] = (at, w)
        at += w
    return out, at


def build(nc, wstream, x_t, c_t, b_ada, g1, g2, kvg, final_g, fbias, lat_cache, kr_cache, kf_cache, vf_cache,
          logf_cache, keys, peer_u, peer_v, aug_ones, consts, outs):
    F32, U32 = mybir.dt.float32, mybir.dt.uint32
    ACT, ALU, AX = mybir.ActivationFunctionType, mybir.AluOpType, mybir.AxisListType
    (y_p, y_s, lat_p, kr_p, kf_p, vf_p, lf_p, lat_s, kr_s, kf_s, vf_s, lf_s) = outs
    clay, cw = const_layout()
    aug_q_dram = nc.dram_tensor("aug_q", (NH, 2, T), F32).ap()
    aug_k_dram = nc.dram_tensor("aug_k", (NH, 2, NKEY), F32).ap()

    with ExitStack() as ctx:
        def sb(name, shape, dt=F32):
            return ctx.enter_context(nc.sbuf_tensor(name, shape, dt))

        def sem(name):
            return ctx.enter_context(nc.semaphore(name))

        ring = sb("ring", [P, RING, D])
        hreg = sb("hreg", [P, KC, T])
        oreg = sb("oreg", [P, KC, T])
        CW_A = 6 * NH * HD
        offs = {}
        at = 0
        for n, w in [("v", CW_A), ("latT", 4 * NKEY), ("qn", T), ("qr", T), ("kn", NKEY), ("rope_x", NKEY),
                     ("vh", 6 * HD), ("prob", P_W), ("probT", PT_W), ("ktok", NT * HD)]:
            offs[n] = at
            at += w
        arena_w = 8 * D
        assert at <= arena_w
        arena = sb("arena", [P, arena_w])

        def area(name, w, p=P):
            return arena[0:p, offs[name]:offs[name] + w]

        v_tok = area("v", CW_A).rearrange("p (t c) -> p t c", t=6)
        lat_tok = arena[:, 0:NT * LORA].rearrange("p (t c) -> p t c", t=NT)
        latT = area("latT", 4 * NKEY).rearrange("p (k t) -> p k t", k=4)
        kf_past = area("latT", NH * PAST).rearrange("p (h t) -> p h t", h=NH)
        qn = area("qn", T)
        qr = area("qr", T, ROPE)
        kn = area("kn", NKEY)
        rope_x = area("rope_x", HALF, ROPE)
        rope_r = arena[0:ROPE, offs["rope_x"] + HALF:offs["rope_x"] + 2 * HALF]
        aug_q = area("qr", T, 2)
        aug_k = area("rope_x", NKEY, 2)
        vh = area("vh", 6 * HD).rearrange("p (t d) -> p t d", t=6)
        prob = area("prob", P_W)
        probT = area("probT", PT_W)
        ktok = area("ktok", NT * HD).rearrange("p (t d) -> p t d", t=NT)
        merged = arena[:, 0:KC * T].rearrange("p (k t) -> p k t", k=KC)
        sg = arena[:, KC * T:KC * T + 4 * HALF].rearrange("p (n t) -> p n t", n=4)
        s_all = arena[:, 0:NT * D].rearrange("p (t n) -> p t n", t=NT)
        vring = arena[:, 0:GR * D].rearrange("p (r n) -> p r n", r=GR)
        g2b = arena[:, 4 * D:5 * D]
        wk = arena[:, NT * D:NT * D + 2 * D]
        qn_peer = wk[:, 0:T]
        junk = wk[:, 0:D].bitcast(mybir.dt.bfloat16)
        dot_junk, sq_junk = junk[:, 0:D], junk[:, D:2 * D]
        h2_tok = wk[:, D:2 * D]
        y_row = arena[:, 7 * D:8 * D]
        roff = [0]

        def route(name_w, pat=None, dt=None, **kw):
            w = name_w
            x = ring[:, roff[0] // D, roff[0] % D:roff[0] % D + w]
            roff[0] += w
            if dt is not None:
                x = x.bitcast(dt)
            return x.rearrange(pat, **kw) if pat else x

        top_v = route(256, "p (q k) -> p q k", q=2 * PH)
        top_i = route(256, "p (q k) -> p q k", U32, q=2 * PH)
        top_if = route(256, "p (q k) -> p q k", q=2 * PH)
        sel_f = route(256, "p (s h k) -> p s h k", s=2, h=PH)
        sc_v = route(128, "p (h k) -> p h k", h=PH)
        sc_d = route(128, "p (h k) -> p h k", h=PH)
        ex_f = route(128, "p (h k) -> p h k", h=PH)
        sel = route(128, "p (h k) -> p h k", U32, h=PH)
        sel_a = route(128, "p (h k) -> p h k", U32, h=PH)
        sel_b = route(128, "p (h k) -> p h k", U32, h=PH)
        sc_s = route(128)[:, 0:PH]
        roff[0] = D
        gate_all = route(NT * SLOTS, "p (t s) -> p t s", t=NT)
        exp_all = route(NT * SLOTS, "p (t s) -> p t s", U32, t=NT)
        fgb = sb("fgb", [P, D])

        krT = sb("krT", [ROPE, NKEY])
        cst = sb("cst", [P, cw])
        cn = {n: cst[:, a:a + w] for n, (a, w) in clay.items()}
        ident = cn["ident"]
        kvgb = sb("kvgb", [P, LORA])
        keyT = sb("keyT", [P, 2, NK])
        cT = sb("cT", [P, KC, 2])
        bad = sb("bad", [P, N_MOD])
        g1T = sb("g1T", [P, KC])
        g2T = sb("g2T", [P, KC])
        mod = sb("mod", [P, N_MOD, 2])
        cf = sb("cf", [P, KC, 2])
        rstd = sb("rstd", [P, T])
        stat = sb("stat", [P, 4, NT])
        fb = sb("fb", [P, NH])
        fw = sb("fw", [P, 6, NT * NH])
        logf = sb("logf", [P, 6, NH])
        frow = area("probT", 2 * NKEY, NH).rearrange("p (r t) -> p r t", r=2)
        diag = sb("diag", [P, GR, P])
        dots = sb("dots", [P, FB])
        idx8 = sb("idx8", [P, 4, GR], U32)
        NS = TP * SLOTS // P + TS * SLOTS // P
        experts = sb("experts", [P, NS], U32)
        gates = sb("gates", [P, NS])
        wts = sb("wts", [P, NS])
        pb = [ctx.enter_context(nc.psum_tensor(f"pb{i}", [P, 512], F32)) for i in range(8)]

        w_in = [sem(f"w_in{r}") for r in range(RING)]
        w_used = [sem(f"w_used{r}") for r in range(RING)]
        small_in = sem("small_in")
        x_in = sem("x_in")
        x_in2 = sem("x_in2")
        cache_in = sem("cache_in")
        kfp_in = sem("kfp_in")
        vfp_in = sem("vfp_in")
        out_s = sem("out_s")
        sq_ok, ssq_ok, var_ok, rstd_ok = sem("sq_ok"), sem("ssq_ok"), sem("var_ok"), sem("rstd_ok")
        silu_ok = sem("silu_ok")
        ada_ok = sem("ada_ok")
        ada_free = [sem(f"ada_free{j}") for j in range(4)]
        cf_ok, hn_ok, h_ok = sem("cf_ok"), sem("hn_ok"), sem("h_ok")
        tokm = sem("tokm")
        tokm_ev = sem("tokm_ev")
        lat_ss, lat_rs, lat_ok = sem("lat_ss"), sem("lat_rs"), sem("lat_ok")
        latT_ps, latT_ok = sem("latT_ps"), sem("latT_ok")
        lat_out = sem("lat_out")
        v_out = sem("v_out")
        f_ps, f_z, f_l, logf_ok, cum_ps, frow_ok, aug_st = (sem("f_ps"), sem("f_z"), sem("f_l"), sem("logf_ok"),
                                                            sem("cum_ps"), sem("frow_ok"), sem("aug_st"))
        proj = sem("proj")
        proj_free = [sem(f"proj_free{b}") for b in range(2)]
        rope_in, rope_ok = sem("rope_in"), sem("rope_ok")
        krt_ps, krt_ok = sem("krt_ps"), sem("krt_ok")
        s_ok, mx_ok, exp_ok, prob_ok = sem("s_ok"), sem("mx_ok"), sem("exp_ok"), sem("prob_ok")
        pt_ps, pt_ok, pv_ok, o_ok, vh_ok = sem("pt_ps"), sem("pt_ok"), sem("pv_ok"), sem("o_ok"), sem("vh_ok")
        aug_in, kt_ps, kt_ok, kt_out = sem("aug_in"), sem("kt_ps"), sem("kt_ok"), sem("kt_out")
        mg_ps, sig_ok = sem("mg_ps"), sem("sig_ok")
        mg_free = [sem(f"mg_free{b}") for b in range(2)]
        x2_ok = sem("x2_ok")
        q_ok, sc_ps, sc_ok = sem("q_ok"), sem("sc_ps"), sem("sc_ok")
        smx_in, smx_ok, route_ok = sem("smx_in"), sem("smx_ok"), sem("route_ok")
        u_in = [sem(f"u_in{r}") for r in range(GR)]
        u_used = [sem(f"u_used{r}") for r in range(GR)]
        v_in = [sem(f"v_in{r}") for r in range(GR)]
        v_used = [sem(f"v_used{r}") for r in range(GR)]
        dg_ok = [sem(f"dg_ok{r}") for r in range(GR)]
        idx_ok = [sem("idx_u_ok"), sem("idx_v_ok")]
        s_clear = sem("s_clear")
        pool_on = sem("pool_on")
        ht_ps, ht_ok = sem("ht_ps"), sem("ht_ok")
        dot_ok, gelu_ok, wt_ok = sem("dot_ok"), sem("gelu_ok"), sem("wt_ok")
        g2_ps, g2_ok = sem("g2_ps"), sem("g2_ok")
        acc_ok, acc_free, x2t_ps, y_pre, y_ss, y_rs, y_ok, y_out, y_rs2 = (
            sem("acc_ok"), sem("acc_free"), sem("x2t_ps"), sem("y_pre"), sem("y_ss"), sem("y_rs"), sem("y_ok"), sem("y_out"), sem("y_rs2"))
        block = ctx.enter_context(nc.Block())

        UB_MLA = 2
        UB_FOX = UB_MLA + 6 * NH
        UB_OUT = UB_FOX + 4 * NH
        UB_WQ = UB_OUT + 2 * KC
        AD_A = KC // 2
        NSMALL = 11

        @block.sync
        def _(sp):
            with sp.Fori(0, NB // RING) as i:
                for r in range(RING):
                    sp.wait_ge(w_used[r], i + 1)
                    sp.dma_start(ring[:, r, :], wstream[i * RING + r]).then_inc(w_in[r], 16)
            for b in range(NB // RING * RING, NB):
                sp.wait_ge(w_used[b % RING], b // RING + 1)
                sp.dma_start(ring[:, b % RING, :], wstream[b]).then_inc(w_in[b % RING], 16)

        @block.tensor
        def _(pe):
            def mm(out, lhsT, rhs, start=True, stop=True):
                return nc.tensor.matmul(out, lhsT, rhs, start=start, stop=stop)

            def tr(out, in_):
                p = in_.shape[0]
                return nc.tensor.transpose(out, in_, ident[0:p, 0:p])

            def blk(base, j, i=0, per=4):
                b = base + j
                pe.wait_ge(w_in[b % RING], 16 * (b // RING + 1) + 16 * (per // RING) * i)
                return b % RING

            def used(ins, slot):
                ins.then_inc(w_used[slot], 1)

            def ada(base, j, i, region, before, ps):
                s = blk(base, j, i)
                pe.wait_ge(ada_free[region], before + i + 1)
                for k in range(KC):
                    last = mm(ps, ring[:, s, k * P:(k + 1) * P], cT[:, k, :], k == 0, k == KC - 1)
                last.then_inc(ada_ok, 1)
                return s

            def sumsq():
                for hf in range(2):
                    for k in range(KC):
                        last = mm(pb[hf][:, 0:HALF], cn["ones"], hreg[:, k, hf * HALF:(hf + 1) * HALF], k == 0, k == KC - 1)
                    last.then_inc(ssq_ok, 1)

            pe.wait_ge(small_in, 16 * NSMALL)
            pe.wait_ge(sq_ok, 1)
            sumsq()
            pe.wait_ge(silu_ok, 1)
            with pe.Fori(0, ADA_A // 4) as i:
                for j in range(4):
                    s = blk(0, j, i)
                    pe.wait_ge(ada_free[j], i + 1)
                    for k in range(KC):
                        last = mm(pb[2 + j][:, 0:2], ring[:, s, k * P:(k + 1) * P], cT[:, k, :], k == 0, k == KC - 1)
                    last.then_inc(ada_ok, 1)
                    pe.drain().then_inc(w_used[s], 1)
            pe.wait_ge(h_ok, 1)

            def token_major(base, nblk, bank0, tiles, lhs, kper, first):
                for c in range(nblk):
                    s = blk(base, c)
                    for kk in range(kper):
                        k = c * kper + kk
                        for t in tiles:
                            m = rows(t) if t < 5 else P
                            last = mm(pb[bank0 + t][0:m, :], lhs(k, t), ring[:, s, kk * 512:(kk + 1) * 512],
                                      k == 0, k == nblk * kper - 1)
                    used(last, s)

            def h_tile(k, t):
                return hreg[:, k, t * P:t * P + rows(t)]

            token_major(B_CKV, CKV, 0, range(NT), h_tile, 4, 0)
            pe.drain().then_inc(tokm, 1)
            s = blk(B_KRF, 0)
            for hf in range(2):
                for k in range(KC):
                    last = mm(pb[5 + hf][0:ROPE, 0:HALF], ring[:, s, k * ROPE:(k + 1) * ROPE],
                              hreg[:, k, hf * HALF:(hf + 1) * HALF], k == 0, k == KC - 1)
                last.then_inc(proj, 1)
            for t in range(NT):
                for k in range(KC):
                    last = mm(pb[7][0:rows(t), t * NH:(t + 1) * NH], h_tile(k, t),
                              ring[:, s, KC * ROPE + k * NH:KC * ROPE + (k + 1) * NH], k == 0, k == KC - 1)
            last.then_inc(f_ps, 1)
            pe.drain().then_inc(w_used[s], 1)
            for t in range(NT):
                pe.wait_ge(lat_ok, t + 1)
                m = rows(t)
                for c in range(4):
                    last = tr(pb[t][:, c * P:c * P + m], lat_tok[0:m, t, c * P:(c + 1) * P])
                last.then_inc(latT_ps, 1)
            pe.wait_ge(logf_ok, 1)
            band = cn["band"]
            pe.wait_ge(rope_in, 2)
            for t in range(QT):
                mm(pb[5][0:NH, t * P:TP], logf[:, t, :], band[:, 0:TP - t * P], t == 0, t == QT - 1)
            mm(pb[6][0:NH, 0:PAST + TS], logf[:, 5, :], band[:, 0:PAST + TS], True, False)
            mm(pb[6][0:NH, PAST:PAST + TS], logf[0:TS, 4, :], band[0:TS, 0:TS], False, True).then_inc(cum_ps, 1)
            pe.wait_ge(latT_ok, NT)
            pe.wait_ge(cache_in, 16)
            pe.wait_ge(frow_ok, 1)

            def lat_tile(k, t):
                a = t * P if t < 5 else T
                return latT[:, k, a:a + (rows(t) if t < 5 else P)]

            for n in range(MLAV):
                if n:
                    pe.wait_ge(tokm_ev, 6)
                token_major(B_MLAV + n, 1, 0, range(6), lat_tile, 4, 0)
                pe.drain().then_inc(tokm, 1)
            pe.wait_ge(rope_ok, 2)
            pe.wait_ge(f_z, 1)
            for t in range(NT):
                last = tr(pb[7][0:rows(t), t * ROPE:(t + 1) * ROPE], krT[:, t * P:t * P + rows(t)])
            last.then_inc(krt_ps, 1)
            pe.wait_ge(tokm_ev, 12)
            pe.wait_ge(krt_ok, 1)

            def project(s, lhs, m, src, width, unit0, i, per, n0=0):
                for hf in range(2):
                    u = unit0 + hf
                    pe.wait_ge(proj_free[hf], u // 2 + (per // 2) * i)
                    for k in range(src.shape[1]):
                        last = mm(pb[hf][0:m, 0:width], lhs(k), src[:, k, hf * width:(hf + 1) * width],
                                  k == 0, k == src.shape[1] - 1)
                    last.then_inc(proj, 1)
                return last

            def scores_mla(g):
                pe.wait_ge(rope_ok, 2 + 2 * (g + 1))
                pe.wait_ge(proj_free[1], UB_MLA // 2 + 3 * (g + 1))
                pe.wait_ge(proj_free[0], UB_MLA // 2 + 3 * (g + 1))
                for t in range(NT):
                    m, (b, c) = rows(t), S_AT[t]
                    q = slice(t * P, t * P + m)
                    ks = slice(0, S_W[t]) if t < QT else slice(TP, NKEY)
                    mm(pb[b][0:m, c:c + S_W[t]], qn[:, q], kn[:, ks], True, False)
                    last = mm(pb[b][0:m, c:c + S_W[t]], qr[:, q], krT[:, ks], False, True)
                last.then_inc(s_ok, 1)

            def scores_fox(g, h):
                pe.wait_ge(proj_free[1], UB_FOX // 2 + 2 * (h + 1))
                pe.wait_ge(proj_free[0], UB_FOX // 2 + 2 * (h + 1))
                pe.wait_ge(aug_in, 32 * (h + 1))
                for t in range(NT):
                    m, (b, c) = rows(t), S_AT[t]
                    q = slice(t * P, t * P + m)
                    if t < QT:
                        mm(pb[b][0:m, c:c + S_W[t]], qn[:, q], kn[:, 0:S_W[t]], True, False)
                        last = mm(pb[b][0:m, c:c + S_W[t]], aug_q[:, q], aug_k[:, 0:S_W[t]], False, True)
                    else:
                        mm(pb[b][0:m, c:c + TS], qn[:, q], kn[:, TP:T], True, False)
                        mm(pb[b][0:m, c:c + TS], aug_q[:, q], aug_k[:, TP:T], False, True)
                        mm(pb[b][0:m, c + TS:c + TS + PAST], qn[:, q], kf_past[:, h, :], True, False)
                        last = mm(pb[b][0:m, c + TS:c + TS + PAST], aug_q[:, q], aug_k[:, T:NKEY], False, True)
                last.then_inc(s_ok, 1)

            def weighted_values(g, ada_read):
                pe.wait_ge(prob_ok, g + 1)
                pe.wait_ge(o_ok, g)

                def pt(bank, col, kt):
                    for t in range(kt, QT):
                        last = tr(pb[bank][:, col + (t - kt) * P:col + (t - kt + 1) * P],
                                  prob[:, P_AT[t] + kt * P:P_AT[t] + (kt + 1) * P])
                    return last
                pt(5, 0, 0).then_inc(pt_ps, 1)
                pt(6, 0, 1)
                pt(6, 384, 3).then_inc(pt_ps, 1)
                pe.wait_ge(pt_ok, 3 * g + 1)
                pt(5, 0, 2)
                a = P_AT[QT]
                tr(pb[5][0:TS, 256:256 + TS], prob[0:TS, a:a + TS])
                tr(pb[5][:, 256 + TS:256 + 2 * TS], prob[0:TS, a + TS:a + TS + PAST]).then_inc(pt_ps, 1)
                pe.wait_ge(vh_ok, g + 1)
                pe.wait_ge(pt_ok, 3 * g + 3)
                pe.wait_ge(ada_free[0], ada_read + 1)
                for kt in range(QT):
                    mm(pb[7][:, kt * P:TP], vh[:, kt, :], probT[:, PT_AT[kt]:PT_AT[kt] + TP - kt * P],
                       kt == 0, kt == QT - 1)
                so = pb[5][:, 440:440 + TS]
                mm(so, vh[0:TS, 4, :], probT[0:TS, PT_S:PT_S + TS], True, False)
                mm(so, vh[:, 5, :], probT[:, PT_S + TS:PT_S + 2 * TS], False, True).then_inc(pv_ok, 1)

            def prev(i):
                return 0 if isinstance(i, int) and i == 0 else i - 1

            def ada_pair(base, i, before, o_read):
                pe.wait_ge(o_ok, o_read)
                for j in range(2):
                    s = ada(base, 2 + j, i, 0, before, pb[7][:, 2 * j:2 * j + 2])
                    pe.drain().then_inc(w_used[s], 1)

            def proj_mla(i):
                s = blk(B_MLA, 0, i)
                last = project(s, lambda k: ring[:, s, k * P:(k + 1) * P], P, hreg, HALF, UB_MLA, i, 6)
                pe.drain().then_inc(w_used[s], 1)
                s2 = blk(B_MLA, 1, i)
                project(s2, lambda k: ring[:, s2, k * ROPE:(k + 1) * ROPE], ROPE, hreg, HALF, UB_MLA + 2, i, 6)
                project(s2, lambda k: ring[:, s2, KC * ROPE + k * P:KC * ROPE + (k + 1) * P], P, latT, KHALF, UB_MLA + 4, i, 6)
                pe.drain().then_inc(w_used[s2], 1)
                ada_pair(B_MLA, i, AD_A, prev(i))

            proj_mla(0)
            scores_mla(0)
            with pe.Fori(1, NH) as i:
                proj_mla(i)
                weighted_values(i - 1, AD_A + i + 1)
                scores_mla(i)
            weighted_values(NH - 1, AD_A + NH)

            pe.wait_ge(mx_ok, NH)
            pe.wait_ge(exp_ok, NH)
            pe.wait_ge(o_ok, NH)
            for n in range(2):
                if n:
                    pe.wait_ge(tokm_ev, 12 + NT)
                token_major(B_FOXV + 4 * n, 4, 0, range(NT), h_tile, 4, 0)
                pe.drain().then_inc(tokm, 1)
            pe.wait_ge(tokm_ev, 12 + 2 * NT)
            pe.wait_ge(kfp_in, 16)

            def proj_fox(i):
                s = blk(B_FOX, 0, i)
                project(s, lambda k: ring[:, s, k * P:(k + 1) * P], P, hreg, HALF, UB_FOX, i, 4)
                pe.drain().then_inc(w_used[s], 1)
                s2 = blk(B_FOX, 1, i)
                project(s2, lambda k: ring[:, s2, k * P:(k + 1) * P], P, hreg, HALF, UB_FOX + 2, i, 4)
                pe.drain().then_inc(w_used[s2], 1)
                ada_pair(B_FOX, i, AD_A + NH, prev(i) + NH)

            def keys_out(h):
                pe.wait_ge(o_ok, NH + h)
                for t in range(NT):
                    m = rows(t)
                    o = pb[5][0:m, t * P:(t + 1) * P] if t < QT else pb[6][0:m, 0:P]
                    last = tr(o, kn[:, t * P:t * P + m])
                last.then_inc(kt_ps, 1)

            proj_fox(0)
            scores_fox(NH, 0)
            pe.wait_ge(pt_ok, 3 * NH)
            keys_out(0)
            with pe.Fori(1, NH) as i:
                proj_fox(i)
                pe.wait_ge(kt_ok, i)
                weighted_values(NH - 1 + i, AD_A + NH + i + 1)
                scores_fox(NH + i, i)
                pe.wait_ge(pt_ok, 3 * NH + 3 * i)
                keys_out(i)
            pe.wait_ge(kt_ok, NH)
            weighted_values(2 * NH - 1, AD_A + 2 * NH)
            pe.wait_ge(exp_ok, 2 * NH)
            pe.wait_ge(o_ok, 2 * NH)

            with pe.Fori(0, KC) as i:
                sm = blk(B_MERGE, 0, i)
                sf = blk(B_MERGE, 1, i)
                so = blk(B_MERGE, 2, i)
                for hf in range(2):
                    cols = slice(hf * HALF, (hf + 1) * HALF)
                    pe.wait_ge(mg_free[hf], i + 1)
                    if hf:
                        s3 = ada(B_MERGE, 3, i, 0, AD_A + 2 * NH, pb[4][:, 0:2])
                        pe.drain().then_inc(w_used[s3], 1)
                    for q, s, off, src, k0, kn_ in [(1, sf, 0, hreg, 0, KC), (2, so, 0, oreg, 0, NH),
                                                    (3, so, NH * P, oreg, NH, NH), (0, sm, 0, hreg, 0, KC)]:
                        if hf and q == 0:
                            pe.wait_ge(ada_free[0], AD_A + 2 * NH + i + 2)
                        for k in range(kn_):
                            last = mm(pb[4 * hf + q][:, 0:HALF], ring[:, s, off + k * P:off + (k + 1) * P],
                                      src[:, k0 + k, cols], k == 0, k == kn_ - 1)
                    last.then_inc(mg_ps, 1)
                pe.drain().then_inc(w_used[sm], 1)
                pe.drain().then_inc(w_used[sf], 1)
                pe.drain().then_inc(w_used[so], 1)
            for b in range(2):
                pe.wait_ge(mg_free[b], KC + 1)
            pe.wait_ge(x_in2, 16)
            with pe.Fori(0, KC // 2) as i:
                for j in range(2):
                    s = blk(B_OUT, j, i)
                    project(s, lambda k: ring[:, s, k * P:(k + 1) * P], P, merged, HALF, UB_OUT + 2 * j, i, 4)
                    pe.drain().then_inc(w_used[s], 1)
                for j in range(2):
                    s3 = ada(B_OUT, 2 + j, i, j, AD_A + (2 * NH + KC if j == 0 else 0), pb[2 + j][:, 0:2])
                    pe.drain().then_inc(w_used[s3], 1)
            pe.wait_ge(sq_ok, 2)
            for b in range(2):
                pe.wait_ge(proj_free[b], UB_WQ // 2)
            sumsq()
            pe.wait_ge(h_ok, 2)
            with pe.Fori(0, KC // 4) as i:
                for j in range(4):
                    s = blk(B_WQ, j, i)
                    project(s, lambda k: ring[:, s, k * P:(k + 1) * P], P, hreg, HALF, UB_WQ + 2 * j, i, 8)
                    pe.drain().then_inc(w_used[s], 1)
                    pe.wait_ge(q_ok, 4 * i + j + 1)
                    pe.wait_ge(sc_ok, 4 * i + j + 1)
                    for t in range(NT):
                        m = rows(t)
                        o = pb[2][0:m, t * P:(t + 1) * P] if t < QT else pb[3][0:m, 0:P]
                        last = mm(o, qn_peer[:, t * P:t * P + m], keyT[:, j % 2, :])
                    last.then_inc(sc_ps, 1)

            def gate2_rows(g):
                for k in range(KC):
                    c = 4 + k // 4
                    last = mm(pb[c][:, (k % 4) * P:(k % 4 + 1) * P],
                              mod[:, 5 * KC + k, g:g + 1].to_broadcast([P, P]), ident)
                last.then_inc(g2_ps, 1)

            def tokens_of(src, t, m, s):
                for k in range(KC):
                    last = tr(pb[4 + k // 4][0:m, (k % 4) * P:(k % 4 + 1) * P], src[:, k, t * P:t * P + m])
                last.then_inc(s, 1)

            def values_begin():
                for c in range(4):
                    mm(pb[c][:, :], cn["zeros"], oreg[:, 0, 0:512], True, False)

            def values_loop(trip0, trips):
                with pe.Fori(trip0, trip0 + trips) as i:
                    for e in range(FB):
                        r, lap = e % GR, e // GR
                        pe.wait_ge(v_in[r], 32 * i + 16 * (lap + 1))
                        pe.wait_ge(dg_ok[r], 2 * i + lap + 1)
                        for c in range(4):
                            last = mm(pb[c][:, :], diag[:, r, :], vring[:, r, c * 512:(c + 1) * 512], False, False)
                        last.then_inc(v_used[r], 1)

            pe.wait_ge(sc_ok, KC + 1)
            gate2_rows(0)
            pe.wait_ge(g2_ok, 1)
            tokens_of(hreg, 0, P, ht_ps)
            for t in range(NT):
                pe.wait_ge(ht_ok, t + 1)
                pe.wait_ge(dot_ok, t + 1)
                if t + 1 < NT:
                    tokens_of(hreg, t + 1, rows(t + 1), ht_ps)
                if t:
                    pe.wait_ge(acc_free, t)
                values_begin()
                trips = SLOTS // FB if t < QT else TS * SLOTS // P // FB
                values_loop(t * (SLOTS // FB), trips)
                if t + 1 < NT:
                    pe.wait_ge(ht_ok, t + 2)
                for c in range(4):
                    last = mm(pb[c][:, :], cn["zeros"], oreg[:, 0, 0:512], False, True)
                last.then_inc(acc_ok, 1)
                if t == QT:
                    gate2_rows(1)
                    pe.wait_ge(g2_ok, 2)
                tokens_of(oreg, t, rows(t), x2t_ps)
                pe.wait_ge(acc_free, t + 1)

        @block.scalar
        def _(act):
            def a(out, in_, fn=ACT.Copy, **kw):
                return nc.scalar.activation(out, in_, fn, **kw)

            act.dma_start(cst[:, :], consts).then_inc(small_in, 16)
            act.dma_start(cT[:, :, :], c_t).then_inc(small_in, 16)
            act.dma_start(oreg[:, :, :], x_t).then_inc(x_in, 16)
            act.dma_start(bad[:, :], b_ada).then_inc(small_in, 16)
            act.dma_start(g1T[:, :], g1).then_inc(small_in, 16)
            act.dma_start(g2T[:, :], g2).then_inc(small_in, 16)
            act.dma_start(kvgb[:, :], kvg.to_broadcast([P, LORA])).then_inc(small_in, 16)
            act.dma_start(fb[:, :], fbias.to_broadcast([P, NH])).then_inc(small_in, 16)
            act.dma_start(keyT[:, :, :], keys).then_inc(small_in, 16)
            act.dma_start(fgb[:, :], final_g.to_broadcast([P, D])).then_inc(small_in, 16)
            act.dma_start(logf[:, 5, :], logf_cache).then_inc(small_in, 16)
            act.dma_start(krT[:, T:NKEY], kr_cache).then_inc(small_in, 16)
            act.dma_start(latT[:, :, T:NKEY], lat_cache).then_inc(cache_in, 16)
            act.wait_ge(small_in, 16 * NSMALL)
            a(cT[:, :, :], cT[:, :, :], ACT.Silu).then_inc(silu_ok, 1)

            def norm(n, scale0):
                act.wait_ge(var_ok, n + 1)
                a(rstd[:, :], rstd[:, :], ACT.Sqrt).then_inc(rstd_ok, 1)
                with act.Fori(0, KC) as k:
                    act.wait_ge(hn_ok, n * KC + k + 1)
                    act.wait_ge(cf_ok, n + 1)
                    for g, cols in enumerate((slice(0, TP), slice(TP, T))):
                        a(hreg[:, k, cols], hreg[:, k, cols], ACT.Identity, scale=cf[:, k, g:g + 1],
                          bias=mod[:, scale0 + k, g:g + 1])
                act.drain().then_inc(h_ok, 1)

            norm(0, 0)
            act.wait_ge(tokm, 1)
            for t in range(NT):
                m = rows(t)
                a(lat_tok[0:m, t, :], pb[t][0:m, :], ACT.Square, accum_out=stat[0:m, 0, t:t + 1])
            act.drain().then_inc(lat_ss, 1)

            def rope_copy(bank, unit, kf, u):
                act.wait_ge(proj, u)
                act.wait_ge(rope_ok, kf)
                a(rope_x, pb[bank][0:ROPE, 0:HALF])
                a(rope_r[0:32, :], pb[bank][32:64, 0:HALF])
                a(rope_r[32:64, :], pb[bank][0:32, 0:HALF])
                return act.drain()

            for hf in range(2):
                rope_copy(5 + hf, hf, hf, hf + 1).then_inc(rope_in, 1)
            act.wait_ge(lat_rs, 1)
            a(stat[:, 1, :], stat[:, 1, :], ACT.Sqrt)
            act.drain().then_inc(lat_rs, 1)
            act.wait_ge(f_z, 1)
            a(fw[:, 2, :], fw[:, 1, :], ACT.Exp, scale=-1.0)
            act.drain()
            a(fw[:, 3, :], fw[:, 2, :], ACT.Ln, bias=1.0)
            act.drain().then_inc(f_l, 1)
            for t in range(NT):
                act.wait_ge(latT_ps, t + 1)
                m = rows(t)
                a(latT[:, :, t * P:t * P + m], pb[t][:, :].rearrange("p (c t) -> p c t", c=4)[:, :, 0:m]).then_inc(latT_ok, 1)
            act.wait_ge(lat_out, 32)
            for n in range(2):
                act.wait_ge(tokm, 2 + n)
                for t in range(6):
                    m = rows(t) if t < 5 else P
                    a(v_tok[0:m, t, n * 512:(n + 1) * 512], pb[t][0:m, :]).then_inc(tokm_ev, 1)
            act.wait_ge(krt_ps, 1)
            a(ktok[:, 0:QT, 0:ROPE], pb[7][:, 0:QT * ROPE].rearrange("p (t d) -> p t d", d=ROPE))
            a(ktok[0:TS, QT, 0:ROPE], pb[7][0:TS, QT * ROPE:NT * ROPE])
            act.drain().then_inc(krt_ok, 1)
            act.sem_inc(proj_free[0], 1)
            act.sem_inc(proj_free[1], 1)

            def softmax_exp(g, scale):
                act.wait_ge(mx_ok, g + 1)
                for t in range(NT):
                    m, (b, c) = rows(t), S_AT[t]
                    a(prob[0:m, P_AT[t]:P_AT[t] + S_W[t]], pb[b][0:m, c:c + S_W[t]], ACT.Exp,
                      bias=stat[0:m, 2, t:t + 1], scale=scale, accum_out=stat[0:m, 3, t:t + 1])
                act.drain().then_inc(exp_ok, 1)

            def copy_pt(g):
                act.wait_ge(pt_ps, 3 * g + 1)
                act.wait_ge(pv_ok, g)
                act.wait_ge(aug_st, 64)
                a(probT[:, 0:512], pb[5][:, :]).then_inc(pt_ok, 1)
                act.wait_ge(pt_ps, 3 * g + 2)
                a(probT[:, PT_AT[1]:PT_AT[1] + 384], pb[6][:, 0:384])
                a(probT[:, PT_AT[3]:PT_AT[3] + 128], pb[6][:, 384:512]).then_inc(pt_ok, 1)
                act.wait_ge(pt_ps, 3 * g + 3)
                a(probT[:, PT_AT[2]:PT_AT[2] + 256], pb[5][:, 0:256])
                a(probT[0:TS, PT_S:PT_S + TS], pb[5][0:TS, 256:256 + TS])
                a(probT[:, PT_S + TS:PT_S + 2 * TS], pb[5][:, 256 + TS:256 + 2 * TS]).then_inc(pt_ok, 1)

            def copy_o(g):
                act.wait_ge(pv_ok, g + 1)
                a(oreg[:, bass.ds(g, 1), 0:TP], pb[7][:, :].rearrange("p (o t) -> p o t", o=1))
                a(oreg[:, bass.ds(g, 1), TP:T], pb[5][:, 440:440 + TS].rearrange("p (o t) -> p o t", o=1))
                act.drain().then_inc(o_ok, 1)

            def evict_mla(i):
                act.wait_ge(s_ok, i)
                for hf in range(2):
                    act.wait_ge(proj, UB_MLA + hf + 1 + 6 * i)
                    a(qn[:, hf * HALF:(hf + 1) * HALF], pb[hf][:, 0:HALF]).then_inc(proj_free[hf], 1)
                for hf in range(2):
                    rope_copy(hf, 0, 2 + 2 * i + hf, UB_MLA + 2 + hf + 1 + 6 * i)
                    act.drain().then_inc(proj_free[hf], 1)
                    act.drain().then_inc(rope_in, 1)
                for hf in range(2):
                    act.wait_ge(proj, UB_MLA + 4 + hf + 1 + 6 * i)
                    a(kn[:, hf * KHALF:(hf + 1) * KHALF], pb[hf][:, 0:KHALF]).then_inc(proj_free[hf], 1)

            evict_mla(0)
            softmax_exp(0, SC_MLA)
            with act.Fori(1, NH) as i:
                evict_mla(i)
                copy_pt(i - 1)
                copy_o(i - 1)
                softmax_exp(i, SC_MLA)
            copy_pt(NH - 1)
            copy_o(NH - 1)
            act.wait_ge(vh_ok, NH)
            for n in range(2):
                act.wait_ge(tokm, 4 + n)
                for t in range(NT):
                    m = rows(t)
                    a(v_tok[0:m, t, n * 512:(n + 1) * 512], pb[t][0:m, :]).then_inc(tokm_ev, 1)

            def evict_fox(i):
                act.wait_ge(s_ok, NH + i)
                act.wait_ge(kt_ps, i)
                for hf in range(2):
                    act.wait_ge(proj, UB_FOX + hf + 1 + 4 * i)
                    a(qn[:, hf * HALF:(hf + 1) * HALF], pb[hf][:, 0:HALF], scale=SC_FOX).then_inc(proj_free[hf], 1)
                for hf in range(2):
                    act.wait_ge(proj, UB_FOX + 2 + hf + 1 + 4 * i)
                    a(kn[:, hf * HALF:(hf + 1) * HALF], pb[hf][:, 0:HALF]).then_inc(proj_free[hf], 1)

            def copy_keys(i):
                act.wait_ge(kt_ps, i + 1)
                act.wait_ge(kt_out, 32 * i)
                act.wait_ge(out_s, 16 * 4)
                a(ktok[:, 0:QT, :], pb[5][:, :].rearrange("p (t d) -> p t d", t=QT))
                a(ktok[0:TS, QT, :], pb[6][0:TS, 0:P])
                act.drain().then_inc(kt_ok, 1)

            evict_fox(0)
            softmax_exp(NH, 1.0)
            copy_keys(0)
            with act.Fori(1, NH) as i:
                evict_fox(i)
                copy_pt(NH - 1 + i)
                copy_o(NH - 1 + i)
                softmax_exp(NH + i, 1.0)
                copy_keys(i)
            copy_pt(2 * NH - 1)
            copy_o(2 * NH - 1)
            act.wait_ge(vh_ok, 2 * NH)
            act.wait_ge(kt_out, 32 * NH)
            act.wait_ge(v_out, 32)
            with act.Fori(0, KC) as i:
                for hf in range(2):
                    act.wait_ge(mg_ps, 2 * i + hf + 1)
                    act.wait_ge(mg_free[hf], i + 1)
                    a(sg[:, 2 * hf, :], pb[4 * hf][:, 0:HALF], ACT.Sigmoid)
                    a(sg[:, 2 * hf + 1, :], pb[4 * hf + 1][:, 0:HALF], ACT.Sigmoid)
                    act.drain().then_inc(sig_ok, 1)
            act.wait_ge(mg_ps, 2 * KC)
            act.dma_start(oreg[:, :, :], x_t).then_inc(x_in2, 16)
            norm(1, 3 * KC)
            act.wait_ge(s_clear, 1)
            with act.Fori(0, KC // 4) as i:
                for j in range(4):
                    n = 4 * i + j
                    for hf in range(2):
                        act.wait_ge(proj, UB_WQ + 2 * j + hf + 1 + 8 * i)
                        a(qn_peer[:, hf * HALF:(hf + 1) * HALF], pb[hf][:, 0:HALF]).then_inc(proj_free[hf], 1)
                    act.drain().then_inc(q_ok, 1)
                    act.wait_ge(sc_ps, n + 1)
                    a(s_all.rearrange("p t (n k) -> p n t k", k=NK)[:, bass.ds(n, 1), 0:QT, :],
                      pb[2][:, :].rearrange("p (o t k) -> p o t k", o=1, t=QT))
                    a(s_all[0:TS, QT, bass.ds(n * NK, NK)], pb[3][0:TS, 0:P])
                    act.drain().then_inc(sc_ok, 1)
            with act.Fori(0, NT) as t:
                act.wait_ge(smx_in, t + 1)
                a(sc_d, sc_d, ACT.Exp).then_inc(smx_ok, 1)
            act.wait_ge(g2_ps, 1)
            act.wait_ge(route_ok, 1)
            for c in range(4):
                a(g2b[:, c * 512:(c + 1) * 512], pb[4 + c][:, :])
            act.drain().then_inc(g2_ok, 1)

            def copy_h2(t):
                act.wait_ge(ht_ps, t + 1)
                m = rows(t)
                if t:
                    act.wait_ge(dot_ok, t)
                if t < QT:
                    for c in range(4):
                        a(h2_tok[0:m, c * 512:(c + 1) * 512], pb[4 + c][0:m, :])
                else:
                    for g in range(4):
                        for c in range(4):
                            a(h2_tok[32 * g:32 * g + TS, c * 512:(c + 1) * 512], pb[4 + c][0:TS, :])
                act.drain().then_inc(ht_ok, 1)

            def gelu_tile(t):
                act.wait_ge(dot_ok, t + 1)
                c0, w = t * SLOTS, (SLOTS if t < QT else TS)
                a(wts[:, c0:c0 + w], wts[:, c0:c0 + w], ACT.Gelu).then_inc(gelu_ok, 1)
                act.wait_ge(wt_ok, t + 1)

            def diagonals(trip0, trips, base):
                with act.Fori(trip0, trip0 + trips) as i:
                    for e in range(FB):
                        r, lap = e % GR, e // GR
                        act.wait_ge(v_used[r], 2 * i + lap + 1)
                        a(diag[:, r, :], base, scale=wts[:, bass.ds(FB * i + e, 1)]).then_inc(dg_ok[r], 1)

            copy_h2(0)
            for t in range(NT):
                gelu_tile(t)
                if t + 1 < NT:
                    copy_h2(t + 1)
                trips = SLOTS // FB if t < QT else TS * SLOTS // P // FB
                diagonals(t * (SLOTS // FB), trips, ident if t < QT else cn["stack"])
                m = rows(t)
                if t == QT:
                    act.wait_ge(g2_ps, 2)
                    act.wait_ge(y_ok, QT)
                    for c in range(4):
                        a(g2b[:, c * 512:(c + 1) * 512], pb[4 + c][:, :])
                    act.drain().then_inc(g2_ok, 1)
                act.wait_ge(y_pre, t + 1)
                a(sq_junk[0:m, :], y_row[0:m, :], ACT.Square, accum_out=stat[0:m, 0, t:t + 1])
                act.drain().then_inc(y_ss, 1)
                act.wait_ge(y_rs, t + 1)
                a(stat[0:m, 1, t:t + 1], stat[0:m, 1, t:t + 1], ACT.Sqrt).then_inc(y_rs2, 1)
                act.wait_ge(y_ok, t + 1)
                dst = y_p[0, t * P:(t + 1) * P, :] if t < QT else y_s[0, :, :]
                act.dma_start(dst, y_row[0:m, :]).then_inc(y_out, 16)
            act.wait_ge(y_out, 16 * NT)

        @block.vector
        def _(dve):
            v = nc.vector

            def square(src, n, gate):
                v.tensor_tensor(hreg[:, :, :], src[:, :, :], src[:, :, :], ALU.mult)
                dve.drain().then_inc(sq_ok, 1)

            def ada_out(a0, region, idx, ps):
                dve.wait_ge(ada_ok, a0)
                v.tensor_scalar(mod[:, bass.ds(idx, 1), :].rearrange("p o g -> p (o g)"), ps,
                                bad[:, bass.ds(idx, 1)], None, ALU.add).then_inc(ada_free[region], 1)

            def ada_pair_out(a0, idx):
                dve.wait_ge(ada_ok, a0)
                for j in range(2):
                    last = v.tensor_scalar(mod[:, bass.ds(idx + j, 1), :].rearrange("p o g -> p (o g)"), pb[7][:, 2 * j:2 * j + 2],
                                           bad[:, bass.ds(idx + j, 1)], None, ALU.add)
                last.then_inc(ada_free[0], 1)

            def norm(n, src, g, scale0):
                for hf in range(2):
                    dve.wait_ge(ssq_ok, 2 * n + hf + 1)
                    v.tensor_scalar(rstd[:, hf * HALF:(hf + 1) * HALF], pb[hf][:, 0:HALF], 1.0 / D, EPS, ALU.mult, ALU.add)
                dve.drain()
                v.reciprocal(rstd[:, :], rstd[:, :])
                dve.drain().then_inc(var_ok, 1)

            def norm2(n, src, g, scale0):
                dve.wait_ge(rstd_ok, n + 1)
                v.tensor_scalar(cf[:, :, :], mod[:, scale0:scale0 + KC, :], 1.0, None, ALU.add)
                dve.drain()
                v.tensor_tensor(cf[:, :, :], cf[:, :, :], g[:, :].rearrange("p (k o) -> p k o", o=1).to_broadcast([P, KC, 2]), ALU.mult)
                dve.drain().then_inc(cf_ok, 1)
                with dve.Fori(0, KC) as k:
                    v.tensor_tensor(hreg[:, bass.ds(k, 1), :].rearrange("p o t -> p (o t)"),
                                    src[:, bass.ds(k, 1), :].rearrange("p o t -> p (o t)"), rstd[:, :], ALU.mult).then_inc(hn_ok, 1)

            v.memset(stat[:, :, :], 1.0)
            v.memset(logf[:, 0:5, :], 0.0)
            v.memset(fw[:, :, :], 0.0)
            dve.wait_ge(x_in, 16)
            dve.wait_ge(small_in, 16 * NSMALL)
            square(oreg, 0, None)
            norm(0, oreg, g1T, KC)
            with dve.Fori(0, ADA_A // 4) as i:
                for j in range(4):
                    ada_out(4 * i + j + 1, j, 4 * i + j, pb[2 + j][:, 0:2])
            dve.drain()
            norm2(0, oreg, g1T, KC)

            dve.wait_ge(lat_ss, 1)
            v.tensor_scalar(stat[:, 1, :], stat[:, 0, :], 1.0 / LORA, EPS, ALU.mult, ALU.add)
            dve.drain()
            v.reciprocal(stat[:, 1, :], stat[:, 1, :])
            dve.drain().then_inc(lat_rs, 1)

            def rotate(dst, hf, n):
                dve.wait_ge(rope_in, n)
                cols = slice(hf * HALF, (hf + 1) * HALF)
                v.tensor_tensor(rope_x, rope_x, cn["cos"][0:ROPE, cols], ALU.mult)
                v.tensor_tensor(rope_r, rope_r, cn["sin"][0:ROPE, cols], ALU.mult)
                dve.drain()
                v.tensor_tensor(dst[:, cols], rope_x, rope_r, ALU.add)
                dve.drain().then_inc(rope_ok, 1)

            for hf in range(2):
                rotate(krT, hf, hf + 1)
            dve.wait_ge(f_ps, 1)
            for t in range(NT):
                m = rows(t)
                v.tensor_tensor(fw[0:m, 0, t * NH:(t + 1) * NH], pb[7][0:m, t * NH:(t + 1) * NH], fb[0:m, :], ALU.add)
            dve.drain()
            v.tensor_scalar(fw[:, 1, :], fw[:, 0, :], -1.0, None, ALU.mult)
            v.tensor_scalar(fw[:, 4, :], fw[:, 0, :], 0.0, None, ALU.min)
            dve.drain()
            v.tensor_tensor(fw[:, 1, :], fw[:, 1, :], fw[:, 0, :], ALU.max)
            dve.drain().then_inc(f_z, 1)
            dve.wait_ge(lat_rs, 2)
            for t in range(NT):
                m = rows(t)
                v.scalar_tensor_tensor(lat_tok[0:m, t, :], pb[t][0:m, :], stat[0:m, 1, t:t + 1], kvgb[0:m, :],
                                       ALU.mult, ALU.mult).then_inc(lat_ok, 1)
            dve.wait_ge(f_l, 1)
            v.tensor_tensor(fw[:, 5, :], fw[:, 4, :], fw[:, 3, :], ALU.subtract)
            dve.drain()
            for t in range(NT):
                m = rows(t)
                v.tensor_copy(logf[0:m, t, :], fw[0:m, 5, t * NH:(t + 1) * NH])
            dve.drain().then_inc(logf_ok, 1)
            dve.wait_ge(cum_ps, 1)
            for a_, b_, src in ((0, TP, pb[5][0:NH, 0:TP]), (TP, T, pb[6][0:NH, PAST:PAST + TS]), (T, NKEY, pb[6][0:NH, 0:PAST])):
                v.tensor_copy(frow[:, 0, a_:b_], src)
            dve.drain()
            v.tensor_scalar(frow[:, 1, :], frow[:, 0, :], -1.0, None, ALU.mult)
            dve.drain().then_inc(frow_ok, 1)

            def row_max(g, mask, scale):
                dve.wait_ge(s_ok, g + 1)
                for t in range(QT):
                    b, c = S_AT[t]
                    d = pb[b][:, c + t * P:c + (t + 1) * P]
                    v.tensor_tensor(d, d, mask, ALU.add)
                if scale == 1.0:
                    b, c = S_AT[QT]
                    d = pb[b][0:TS, c:c + TS]
                    v.tensor_tensor(d, d, mask[0:TS, 0:TS], ALU.add)
                dve.drain()
                for t in range(NT):
                    m, (b, c) = rows(t), S_AT[t]
                    v.reduce_max(stat[0:m, 2, t:t + 1], pb[b][0:m, c:c + S_W[t]], AX.X)
                dve.drain()
                v.tensor_scalar(stat[:, 2, :], stat[:, 2, :], -scale, None, ALU.mult)
                dve.drain().then_inc(mx_ok, 1)

            def divide(g):
                dve.wait_ge(exp_ok, g + 1)
                v.reciprocal(stat[:, 3, :], stat[:, 3, :])
                dve.drain()
                for t in range(NT):
                    m = rows(t)
                    pr = prob[0:m, P_AT[t]:P_AT[t] + S_W[t]]
                    v.tensor_scalar(pr, pr, stat[0:m, 3, t:t + 1], None, ALU.mult)
                dve.drain().then_inc(prob_ok, 1)

            with dve.Fori(0, NH) as i:
                for hf in range(2):
                    rotate(qr, hf, 2 + 2 * i + hf + 1)
                ada_pair_out(ADA_A + 2 * i + 2, 2 * KC + 2 * i)
                row_max(i, cn["mask_mla"], SC_MLA)
                divide(i)
            with dve.Fori(0, NH) as i:
                ada_pair_out(ADA_A + 2 * NH + 2 * i + 2, 3 * KC + 2 * i)
                row_max(NH + i, cn["mask_fox"], 1.0)
                divide(NH + i)

            dve.wait_ge(o_ok, 2 * NH)
            dve.wait_ge(kt_out, 32 * NH)
            with dve.Fori(0, KC) as i:
                for hf in range(2):
                    if hf:
                        ada_out(ADA_A + 4 * NH + i + 1, 0, 4 * KC + i, pb[4][:, 0:2])
                    dve.wait_ge(sig_ok, 2 * i + hf + 1)
                    s0, s1 = sg[:, 2 * hf, :], sg[:, 2 * hf + 1, :]
                    v.tensor_tensor(s0, s0, pb[4 * hf + 2][:, 0:HALF], ALU.mult)
                    v.tensor_tensor(s1, s1, pb[4 * hf + 3][:, 0:HALF], ALU.mult)
                    dve.drain()
                    v.tensor_tensor(merged[:, bass.ds(i, 1), hf * HALF:(hf + 1) * HALF].rearrange("p o t -> p (o t)"), s0, s1, ALU.add)
                    dve.drain().then_inc(mg_free[hf], 1)
            dve.wait_ge(x_in2, 16)
            with dve.Fori(0, KC // 2) as i:
                for j in range(2):
                    for hf in range(2):
                        dve.wait_ge(proj, UB_OUT + 2 * j + hf + 1 + 4 * i)
                        parts = [(0, HALF, 0)] if hf == 0 else [(HALF, TP, 0), (TP, T, 1)]
                        for a_, b_, g in parts:
                            xr = oreg[:, bass.ds(2 * i + j, 1), a_:b_].rearrange("p o t -> p (o t)")
                            v.scalar_tensor_tensor(xr, pb[hf][:, a_ - hf * HALF:b_ - hf * HALF],
                                                   mod[:, bass.ds(2 * KC + 2 * i + j, 1), g:g + 1].rearrange("p o g -> p (o g)"),
                                                   xr, ALU.mult, ALU.add)
                        dve.drain().then_inc(proj_free[hf], 1)
                for j in range(2):
                    ada_out(ADA_A + 4 * NH + KC + 2 * i + j + 1, j, 5 * KC + 2 * i + j, pb[2 + j][:, 0:2])
            dve.drain()
            square(oreg, 1, None)
            norm(1, oreg, g2T, 4 * KC)
            norm2(1, oreg, g2T, 4 * KC)

            dve.wait_ge(proj_free[1], UB_WQ // 2)
            v.memset(s_all[:, QT, :], 0.0)
            dve.drain().then_inc(s_clear, 1)
            dve.wait_ge(sc_ok, KC + 1)
            with dve.Fori(0, NT) as t:
                v.tensor_copy(wk[:, 0:D], s_all[:, bass.ds(t, 1), :].rearrange("p o n -> p (o n)"))
                dve.drain()

                def top16(src, rep, val, ind):
                    n = len(src)
                    for q in range(n):
                        v.max(val[q][:, 0:8], src[q])
                    dve.drain()
                    for q in range(n):
                        v.max_index(ind[q][:, 0:8], val[q][:, 0:8], src[q])
                        v.match_replace(rep[q], val[q][:, 0:8], src[q], -3.0e38)
                    dve.drain()
                    for q in range(n):
                        v.max(val[q][:, 8:16], rep[q])
                    dve.drain()
                    for q in range(n):
                        v.max_index(ind[q][:, 8:16], val[q][:, 8:16], rep[q])
                    dve.drain()

                src = [wk[:, q * NK:(q + 1) * NK] for q in range(2 * PH)]
                rep = [wk[:, D + q * NK:D + (q + 1) * NK] for q in range(2 * PH)]
                top16(src, rep, [top_v[:, q, :] for q in range(2 * PH)], [top_i[:, q, :] for q in range(2 * PH)])
                v1 = top_v.rearrange("p (h s) k -> p h s k", s=2)
                cand = wk[:, 0:D].rearrange("p (h a b) -> p h a b", h=PH, a=TOPK)
                va = v1[:, :, 0, :].rearrange("p h (k o) -> p h k o", o=1).to_broadcast([P, PH, TOPK, TOPK])
                vb = v1[:, :, 1, :].rearrange("p h (o k) -> p h o k", o=1).to_broadcast([P, PH, TOPK, TOPK])
                v.tensor_tensor(cand, va, vb, ALU.add)
                v.tensor_copy(top_if[:, :, :], top_i[:, :, :])
                dve.drain()
                src = [wk[:, h * 256:(h + 1) * 256] for h in range(PH)]
                rep = [wk[:, D + h * 256:D + (h + 1) * 256] for h in range(PH)]
                top16(src, rep, [sc_v[:, h, :] for h in range(PH)], [sel[:, h, :] for h in range(PH)])
                v.tensor_tensor(sc_d, sc_v[:, :, :], sc_v[:, :, 0:1].to_broadcast([P, PH, TOPK]), ALU.subtract)
                dve.drain().then_inc(smx_in, 1)
                v.tensor_scalar(sel_a[:, :, :], sel[:, :, :], 4, None, ALU.logical_shift_right)
                v.tensor_scalar(sel_b[:, :, :], sel[:, :, :], 15, None, ALU.bitwise_and)
                dve.drain()
                v.tensor_copy(sel_f[:, 0], sel_a[:, :, :])
                v.tensor_copy(sel_f[:, 1], sel_b[:, :, :])
                dve.drain()
                i1 = top_if.rearrange("p (h s) k -> p h s k", s=2)
                iota = cn["iota"].rearrange("p (a b j) -> p a b j", a=1, b=1).to_broadcast([P, PH, TOPK, TOPK])
                for s in range(2):
                    hot = wk[:, s * D:(s + 1) * D].rearrange("p (h k j) -> p h k j", h=PH, k=TOPK)
                    v.tensor_tensor(hot, sel_f[:, s].rearrange("p h (k o) -> p h k o", o=1).to_broadcast([P, PH, TOPK, TOPK]),
                                    iota, ALU.is_equal)
                dve.drain()
                for s in range(2):
                    hot = wk[:, s * D:(s + 1) * D].rearrange("p (h k j) -> p h k j", h=PH, k=TOPK)
                    v.tensor_tensor(hot, hot, i1[:, :, s, :].rearrange("p h (o j) -> p h o j", o=1).to_broadcast([P, PH, TOPK, TOPK]), ALU.mult)
                dve.drain()
                for s in range(2):
                    v.reduce_sum(sel_f[:, s], wk[:, s * D:(s + 1) * D].rearrange("p (h k j) -> p h k j", h=PH, k=TOPK), AX.X)
                dve.drain()
                v.scalar_tensor_tensor(ex_f, sel_f[:, 0], float(NK), sel_f[:, 1], ALU.mult, ALU.add)
                dve.wait_ge(smx_ok, t + 1)
                v.reduce_sum(sc_s[:, :], sc_d, AX.X)
                dve.drain()
                v.reciprocal(sc_s[:, :], sc_s[:, :])
                dve.drain()
                v.tensor_tensor(gate_all[:, bass.ds(t, 1), :].rearrange("p o (h k) -> p (o h) k", h=PH), sc_d,
                                sc_s[:, :].rearrange("p (h o) -> p h o", o=1).to_broadcast([P, PH, TOPK]), ALU.mult)
                v.tensor_copy(exp_all[:, bass.ds(t, 1), :].rearrange("p o (h k) -> p (o h) k", h=PH), ex_f)
                dve.drain()
            v.tensor_copy(experts[:, 0:QT * SLOTS], exp_all[:, 0:QT, :].rearrange("p t s -> p (t s)"))
            v.tensor_copy(gates[:, 0:QT * SLOTS], gate_all[:, 0:QT, :].rearrange("p t s -> p (t s)"))
            for g in range(4):
                v.tensor_copy(experts[32 * g:32 * g + 32, QT * SLOTS:NS], exp_all[0:TS, QT, 32 * g:32 * g + 32])
                v.tensor_copy(gates[32 * g:32 * g + 32, QT * SLOTS:NS], gate_all[0:TS, QT, 32 * g:32 * g + 32])
            dve.drain().then_inc(route_ok, 1)

            def dot_products(t):
                dve.wait_ge(ht_ok, t + 1)
                trips = SLOTS // FB if t < QT else TS * SLOTS // P // FB
                t0 = t * (SLOTS // FB)
                with dve.Fori(t0, t0 + trips) as i:
                    for e in range(FB):
                        r, lap = e % GR, e // GR
                        dve.wait_ge(u_in[r], 32 * i + 16 * (lap + 1))
                        v.tensor_tensor_reduce(out=dot_junk, in0=ring[:, r, :], in1=h2_tok[:, :], scale=1.0, scalar=0.0,
                                               op0=ALU.mult, op1=ALU.add, accum_out=dots[:, e:e + 1])
                        dve.drain().then_inc(u_used[r], 1)
                    dve.drain()
                    v.tensor_copy(wts[:, bass.ds(FB * i, FB)], dots[:, :])
                    dve.drain()
                dve.drain().then_inc(dot_ok, 1)

            def weights(t):
                dve.wait_ge(gelu_ok, t + 1)
                c0, w = t * SLOTS, (SLOTS if t < QT else TS)
                v.tensor_tensor(wts[:, c0:c0 + w], wts[:, c0:c0 + w], gates[:, c0:c0 + w], ALU.mult)
                dve.drain().then_inc(wt_ok, 1)

            def finish(t):
                m = rows(t)
                dve.wait_ge(acc_ok, t + 1)
                dve.wait_ge(x2t_ps, t + 1)
                if t:
                    dve.wait_ge(y_out, 16 * t)
                if t == QT:
                    dve.wait_ge(g2_ok, 2)
                for c in range(4):
                    v.tensor_tensor(y_row[0:m, c * 512:(c + 1) * 512], pb[c][0:m, :], g2b[0:m, c * 512:(c + 1) * 512], ALU.mult)
                dve.drain()
                for c in range(4):
                    v.tensor_tensor(y_row[0:m, c * 512:(c + 1) * 512], y_row[0:m, c * 512:(c + 1) * 512], pb[4 + c][0:m, :], ALU.add)
                dve.drain().then_inc(acc_free, 1)
                dve.drain().then_inc(y_pre, 1)
                dve.wait_ge(y_ss, t + 1)
                st = stat[0:m, 1, t:t + 1]
                v.tensor_scalar(st, stat[0:m, 0, t:t + 1], 1.0 / D, EPS, ALU.mult, ALU.add)
                dve.drain()
                v.reciprocal(st, st)
                dve.drain().then_inc(y_rs, 1)
                dve.wait_ge(y_rs2, t + 1)
                v.scalar_tensor_tensor(y_row[0:m, :], y_row[0:m, :], st, fgb[0:m, :], ALU.mult, ALU.mult).then_inc(y_ok, 1)

            dot_products(0)
            weights(0)
            for t in range(NT):
                if t + 1 < NT:
                    dot_products(t + 1)
                finish(t)
                if t + 1 < NT:
                    weights(t + 1)

        @block.gpsimd
        def _(pool):
            g = nc.gpsimd
            for s in w_used + ada_free + mg_free + u_used + v_used + [sc_ok]:
                pool.sem_inc(s, 1)
            pool.wait_ge(lat_ok, NT)
            pool.dma_start(lat_p[0, 0].rearrange("(t p) c -> p t c", p=P), lat_tok[:, 0:QT, :]).then_inc(lat_out, 16)
            pool.dma_start(lat_s[0, 0], lat_tok[0:TS, QT, :]).then_inc(lat_out, 16)
            pool.wait_ge(logf_ok, 1)
            pool.dma_start(lf_p[0, 0].rearrange("(t p) h -> p t h", p=P), logf[:, 0:QT, :]).then_inc(out_s, 16)
            pool.dma_start(lf_s[0, 0], logf[0:TS, QT, :]).then_inc(out_s, 16)
            pool.wait_ge(frow_ok, 1)
            pool.dma_start(aug_q_dram[:, 0, :], frow[:, 0, 0:T]).then_inc(aug_st, 16)
            pool.dma_start(aug_k_dram[:, 1, :], frow[:, 1, :]).then_inc(aug_st, 16)
            pool.dma_start(aug_q_dram[:, 1, :], aug_ones[:, 0:T]).then_inc(aug_st, 16)
            pool.dma_start(aug_k_dram[:, 0, :], aug_ones).then_inc(aug_st, 16)
            pool.wait_ge(krt_ok, 1)
            pool.dma_start(kr_p[0, 0].rearrange("(t p) d -> p t d", p=P), ktok[:, 0:QT, 0:ROPE]).then_inc(out_s, 16)
            pool.dma_start(kr_s[0, 0], ktok[0:TS, QT, 0:ROPE]).then_inc(out_s, 16)

            def head_values(gh, h):
                pool.wait_ge(pv_ok, gh)
                for t in range(6):
                    m = rows(t) if t < 5 else P
                    g.tensor_copy(vh[0:m, t, :], v_tok[0:m, t, bass.ds(h * HD, HD)])
                pool.drain().then_inc(vh_ok, 1)

            pool.wait_ge(tokm_ev, 12)
            head_values(0, 0)
            with pool.Fori(1, NH) as i:
                head_values(i, i)
            pool.wait_ge(s_ok, NH)
            pool.dma_start(kf_past, kf_cache).then_inc(kfp_in, 16)
            pool.dma_start(v_tok[:, 5, :], vf_cache).then_inc(vfp_in, 16)
            pool.wait_ge(tokm_ev, 12 + 2 * NT)
            pool.dma_start(vf_p[0, 0].rearrange("(t p) h d -> p t (h d)", p=P), v_tok[:, 0:QT, :]).then_inc(v_out, 16)
            pool.dma_start(vf_s[0, 0].rearrange("s h d -> s (h d)"), v_tok[0:TS, QT, :]).then_inc(v_out, 16)
            pool.wait_ge(vfp_in, 16)
            pool.wait_ge(aug_st, 64)
            kfp_o = kf_p[0, 0].rearrange("(t p) h d -> p t h d", p=P)
            with pool.Fori(0, NH) as i:
                pool.wait_ge(s_ok, NH + i)
                pool.sem_inc(pool_on, 1)
                pool.dma_start(aug_q, aug_q_dram[bass.ds(i, 1)].rearrange("o r t -> (o r) t")).then_inc(aug_in, 16)
                pool.dma_start(aug_k, aug_k_dram[bass.ds(i, 1)].rearrange("o r t -> (o r) t")).then_inc(aug_in, 16)
                head_values(NH + i, i)
                pool.wait_ge(kt_ok, i + 1)
                pool.sem_inc(pool_on, 1)
                pool.dma_start(kfp_o[:, :, bass.ds(i, 1), :].rearrange("p t o d -> p t (o d)"), ktok[:, 0:QT, :]).then_inc(kt_out, 16)
                pool.dma_start(kf_s[0, 0, :, bass.ds(i, 1), :].rearrange("s o d -> s (o d)"), ktok[0:TS, QT, :]).then_inc(kt_out, 16)

            pool.wait_ge(route_ok, 1)
            pool.wait_ge(s_clear, 1)
            for r in range(RING):
                pool.wait_ge(w_used[r], (NB - r + RING - 1) // RING + 1)

            def rows_of(table, dst, s_in, s_used, i, which):
                for lap in range(FB // GR):
                    idx = idx8[:, 2 * which + lap, :]
                    g.tensor_copy(idx, experts[:, bass.ds(FB * i + GR * lap, GR)]).then_inc(idx_ok[which], 1)
                    pool.wait_ge(idx_ok[which], 2 * i + lap + 1)
                    for r in range(GR):
                        pool.wait_ge(s_used[r], 2 * i + lap + 1)
                        pool.sem_inc(pool_on, 1)
                        g.indirect_dma_start(out=dst[:, r, :], out_offset=None, in_=table,
                                             in_offset=bass.IndirectOffsetOnAxis(ap=idx[:, r:r + 1], axis=0)).then_inc(s_in[r], 16)

            LAG = SLOTS // FB
            TRIPS = NS // FB
            with pool.Fori(0, LAG) as i:
                rows_of(peer_u, ring, u_in, u_used, i, 0)
            with pool.Fori(LAG, TRIPS) as i:
                rows_of(peer_u, ring, u_in, u_used, i, 0)
                rows_of(peer_v, vring, v_in, v_used, i - LAG, 1)
            with pool.Fori(TRIPS - LAG, TRIPS) as i:
                rows_of(peer_v, vring, v_in, v_used, i, 1)
            pool.wait_ge(out_s, 64)
            pool.wait_ge(v_out, 32)
            pool.wait_ge(kt_out, 32 * NH)
            pool.wait_ge(lat_out, 32)


def kernel(**inp):
    import concourse.bacc as bacc
    from concourse.bass_utils import run_bass_kernel_spmd

    x = {k: np.ascontiguousarray(v) for k, v in inp.items()}

    def feat(a):
        return np.ascontiguousarray(a.T.reshape(-1, P, a.shape[0]).transpose(1, 0, 2))

    def cols(v):
        return np.ascontiguousarray(v.reshape(-1, P).T)

    def block(w):
        return w.reshape(-1, P, w.shape[1]).transpose(1, 0, 2).reshape(P, -1)

    def pad(*parts):
        b = np.zeros((P, D), np.float32)
        at = 0
        for p_ in parts:
            b[:, at:at + p_.shape[1]] = p_
            at += p_.shape[1]
        return b

    w_in, w_ada, ukv = x["w_in"][0], x["w_ada"][0], x["w_ukv"][0]
    q_w = HD + ROPE
    o_lat = NH * q_w
    o_kr = o_lat + LORA
    o_fox = o_kr + ROPE
    o_f = o_fox + 3 * NH * HD
    o_gm = o_f + NH
    o_gf = o_gm + D

    def ada(n):
        return block(w_ada[:, n * P:(n + 1) * P])

    stream = np.empty((NB, P, D), np.float32)
    n = [0]

    def put(b):
        stream[n[0]] = b
        n[0] += 1

    for j in range(ADA_A):
        put(ada(j))
    for c in range(CKV):
        put(block(w_in[c * 512:(c + 1) * 512, o_lat:o_kr]))
    put(pad(block(w_in[:, o_kr:o_fox]), block(w_in[:, o_f:o_gm])))
    ukv_h = ukv.reshape(LORA, NH, 2, HD)
    for c in range(MLAV):
        put(block(ukv_h[:, 4 * c:4 * c + 4, 1].reshape(LORA, 512)))
    for h in range(NH):
        put(block(w_in[:, h * q_w:h * q_w + HD]))
        put(pad(block(w_in[:, h * q_w + HD:(h + 1) * q_w]), block(ukv_h[:, h, 0])))
        put(ada(2 * KC + 2 * h))
        put(ada(2 * KC + 2 * h + 1))
    for c in range(2):
        for r in range(4):
            a = o_fox + 2 * NH * HD + c * 512
            put(block(w_in[r * 512:(r + 1) * 512, a:a + 512]))
    for h in range(NH):
        put(block(w_in[:, o_fox + h * HD:o_fox + (h + 1) * HD]))
        put(block(w_in[:, o_fox + (NH + h) * HD:o_fox + (NH + h + 1) * HD]))
        put(ada(3 * KC + 2 * h))
        put(ada(3 * KC + 2 * h + 1))
    for j in range(KC):
        c = slice(j * P, (j + 1) * P)
        put(block(w_in[:, o_gm + j * P:o_gm + (j + 1) * P]))
        put(block(w_in[:, o_gf + j * P:o_gf + (j + 1) * P]))
        put(pad(block(x["w_o_mla"][0][:, c]), block(x["w_o_fox"][0][:, c])))
        put(ada(4 * KC + j))
    for j in range(KC // 2):
        for q in range(2):
            put(block(x["w_out"][0][:, (2 * j + q) * P:(2 * j + q + 1) * P]))
        for q in range(2):
            put(ada(5 * KC + 2 * j + q))
    for j in range(KC):
        put(block(x["peer_wq"][0][:, j * P:(j + 1) * P]))
    assert n[0] == NB

    lay, cw = const_layout()
    cst = np.zeros((P, cw), np.float32)

    def const(name, a):
        cst[:a.shape[0], lay[name][0]:lay[name][0] + a.shape[1]] = a

    i = np.arange(P)
    const("ident", np.eye(P, dtype=np.float32))
    const("stack", (i[:, None] % TS == i[None, :]).astype(np.float32))
    const("band", (i[:, None] <= np.arange(TP)[None, :]).astype(np.float32))
    const("mask_mla", np.where(i[:, None] // CHUNK >= i[None, :] // CHUNK, 0.0, NEG).astype(np.float32))
    const("mask_fox", np.where(i[:, None] >= i[None, :], 0.0, NEG).astype(np.float32))
    const("iota", np.broadcast_to(np.arange(TOPK, dtype=np.float32), (P, TOPK)))
    const("ones", np.ones((P, P), np.float32))
    inv = (1.0 / (np.float32(10000.0) ** (np.arange(0, ROPE, 2, dtype=np.float32) / ROPE))).astype(np.float32)
    pos = np.concatenate([np.arange(TP), PAST + np.arange(TS)]).astype(np.float32)
    ang = (inv[:, None] * pos[None, :]).astype(np.float32)
    const("cos", np.concatenate([np.cos(ang), np.cos(ang)]))
    const("sin", np.concatenate([-np.sin(ang), np.sin(ang)]))

    arrays = {
        "wstream": stream,
        "x_t": feat(np.concatenate([x["x_prompt"][0], x["x_sample"][0]])),
        "c_t": feat(np.concatenate([x["c_prompt"], x["c_sample"]])),
        "b_ada": cols(x["b_ada"][0]),
        "g1": cols(x["norm1_g"][0]),
        "g2": cols(x["norm2_g"][0]),
        "kvg": x["kv_norm_g"],
        "final_g": x["final_g"][None],
        "fbias": x["fox_fbias"],
        "lat_cache": feat(x["cache_mla_latent"][0, 0]),
        "kr_cache": np.ascontiguousarray(x["cache_mla_krope"][0, 0].T),
        "kf_cache": np.ascontiguousarray(x["cache_fox_k"][0, 0].transpose(2, 1, 0)),
        "vf_cache": x["cache_fox_v"][0, 0].reshape(PAST, NH * HD),
        "logf_cache": x["cache_fox_logf"][0, 0],
        "keys": np.ascontiguousarray(np.stack([x["peer_keys1"][0].T, x["peer_keys2"][0].T], 1)),
        "peer_u": x["peer_u"][0],
        "peer_v": x["peer_v"][0],
        "aug_ones": np.ones((NH, NKEY), np.float32),
        "consts": cst,
    }
    shapes = [(1, TP, D), (1, TS, D)]
    for s in (TP, TS):
        shapes += [(1, 1, s, LORA), (1, 1, s, ROPE), (1, 1, s, NH, HD), (1, 1, s, NH, HD), (1, 1, s, NH)]
    f32 = mybir.dt.float32
    nc = bacc.Bacc("TRN2", target_bir_lowering=False, num_devices=1)
    args = {k: nc.dram_tensor(k, a.shape, f32, kind="ExternalInput").ap() for k, a in arrays.items()}
    outs = [nc.dram_tensor(f"out{j}", s, f32, kind="ExternalOutput").ap() for j, s in enumerate(shapes)]
    build(nc, outs=outs, **args)
    r = run_bass_kernel_spmd(nc, [arrays], core_ids=[0])
    return tuple(r.results[0][f"out{j}"] for j in range(len(shapes)))
```

```python
import numpy as np
import concourse.bass as bass
from concourse import mybir
from contextlib import ExitStack

D, TP, TS, PAST = 2048, 512, 32, 128
T = TP + TS
P = 128
KC = D // P
NH, HD, ROPE, LORA = 8, 128, 64, 512
NKEY = T + PAST
QT = TP // P
NT = QT + 1
HALF = T // 2
KHALF = NKEY // 2
CHUNK = 64
EPS = 1e-6
NEG = -1e30
SC_MLA = float(HD + ROPE) ** -0.5
SC_FOX = float(HD) ** -0.5
PH, NK, TOPK = 8, 128, 16
SLOTS = PH * TOPK
RING = 4
FB = 8
GR = 4

N_MOD = 6 * KC
ADA_A = 2 * KC
CKV, KRF, FOXV, MLAV = 4, 1, 8, 2
B_CKV = ADA_A
B_KRF = B_CKV + CKV
B_MLAV = B_KRF + KRF
B_MLA = B_MLAV + MLAV
B_FOXV = B_MLA + 4 * NH
B_FOX = B_FOXV + FOXV
B_MERGE = B_FOX + 4 * NH
B_OUT = B_MERGE + 4 * KC
B_WQ = B_OUT + 2 * KC
B_UT = B_WQ + KC
DN = 3
TD = DN * P
NB = B_UT + NK * NK // P

S_AT = [(2, 0), (3, 0), (2, 128), (4, 0), (3, 256)]
S_W = [128 * (t + 1) for t in range(QT)] + [TS + PAST]
P_AT = [0, 128, 384, 768, 1280]
P_W = P_AT[-1] + S_W[-1]
PT_AT = [0, 512, 896, 1152]
PT_S = 1280
PT_W = PT_S + 2 * TS


def rows(t):
    return P if t < QT else TS


def const_layout():
    names = [("ident", P), ("stack", P), ("band", TP), ("mask_mla", P), ("mask_fox", P), ("iota", TOPK),
             ("cos", T), ("sin", T), ("ones", P), ("token", NT)]
    at, out = 0, {}
    for n, w in names:
        out[n] = (at, w)
        at += w
    return out, at


def build(nc, wstream, x_t, c_t, b_ada, g1, g2, kvg, final_g, fbias, lat_cache, kr_cache, kf_cache, vf_cache,
          logf_cache, keys, peer_u, peer_v, aug_ones, consts, outs):
    F32, U32 = mybir.dt.float32, mybir.dt.uint32
    ACT, ALU, AX = mybir.ActivationFunctionType, mybir.AluOpType, mybir.AxisListType
    (y_p, y_s, lat_p, kr_p, kf_p, vf_p, lf_p, lat_s, kr_s, kf_s, vf_s, lf_s) = outs
    clay, cw = const_layout()
    aug_q_dram = nc.dram_tensor("aug_q", (NH, 2, T), F32).ap()
    dots_dram = nc.dram_tensor("dots_dram", (NK * NK, TD), F32).ap()
    aug_k_dram = nc.dram_tensor("aug_k", (NH, 2, NKEY), F32).ap()

    with ExitStack() as ctx:
        def sb(name, shape, dt=F32):
            return ctx.enter_context(nc.sbuf_tensor(name, shape, dt))

        def sem(name):
            return ctx.enter_context(nc.semaphore(name))

        ring = sb("ring", [P, RING, D])
        hreg = sb("hreg", [P, KC, T])
        oreg = sb("oreg", [P, KC, T])
        CW_A = 6 * NH * HD
        offs = {}
        at = 0
        for n, w in [("v", CW_A), ("latT", 4 * NKEY), ("qn", T), ("qr", T), ("kn", NKEY), ("rope_x", NKEY),
                     ("vh", 6 * HD), ("prob", P_W), ("probT", PT_W), ("ktok", NT * HD)]:
            offs[n] = at
            at += w
        arena_w = 8 * D
        assert at <= arena_w
        arena = sb("arena", [P, arena_w])

        def area(name, w, p=P):
            return arena[0:p, offs[name]:offs[name] + w]

        v_tok = area("v", CW_A).rearrange("p (t c) -> p t c", t=6)
        lat_tok = arena[:, 0:NT * LORA].rearrange("p (t c) -> p t c", t=NT)
        latT = area("latT", 4 * NKEY).rearrange("p (k t) -> p k t", k=4)
        kf_past = area("latT", NH * PAST).rearrange("p (h t) -> p h t", h=NH)
        qn = area("qn", T)
        qr = area("qr", T, ROPE)
        kn = area("kn", NKEY)
        rope_x = area("rope_x", HALF, ROPE)
        rope_r = arena[0:ROPE, offs["rope_x"] + HALF:offs["rope_x"] + 2 * HALF]
        aug_q = area("qr", T, 2)
        aug_k = area("rope_x", NKEY, 2)
        vh = area("vh", 6 * HD).rearrange("p (t d) -> p t d", t=6)
        prob = area("prob", P_W)
        probT = area("probT", PT_W)
        ktok = area("ktok", NT * HD).rearrange("p (t d) -> p t d", t=NT)
        merged = arena[:, 0:KC * T].rearrange("p (k t) -> p k t", k=KC)
        sg = arena[:, KC * T:KC * T + 4 * HALF].rearrange("p (n t) -> p n t", n=4)
        s_all = arena[:, 0:NT * D].rearrange("p (t n) -> p t n", t=NT)
        vring = arena[:, 0:GR * D].rearrange("p (r n) -> p r n", r=GR)
        g2b = arena[:, 4 * D:5 * D]
        wk = arena[:, NT * D:NT * D + 2 * D]
        qn_peer = wk[:, 0:T]
        h2_tok = [arena[:, 5 * D:6 * D], arena[:, 6 * D:7 * D]]
        accs = [arena[:, 7 * D:8 * D], arena[:, 6 * D:7 * D]]
        sq_junk = arena[:, 5 * D:6 * D]
        roff = [7 * D]

        def route(w, pat, dt=None, **kw):
            x = arena[:, roff[0]:roff[0] + w]
            roff[0] += w
            return (x if dt is None else x.bitcast(dt)).rearrange(pat, **kw)

        top_v = route(256, "p (q k) -> p q k", q=2 * PH)
        top_i = route(256, "p (q k) -> p q k", U32, q=2 * PH)
        top_if = route(256, "p (q k) -> p q k", q=2 * PH)
        sel_f = route(256, "p (s h k) -> p s h k", s=2, h=PH)
        sc_v = route(128, "p (h k) -> p h k", h=PH)
        ex_f = route(128, "p (h k) -> p h k", h=PH)
        sel = route(128, "p (h k) -> p h k", U32, h=PH)
        sel_a = route(128, "p (h k) -> p h k", U32, h=PH)
        sel_b = route(128, "p (h k) -> p h k", U32, h=PH)
        fgb = sb("fgb", [P, D])

        krT = sb("krT", [ROPE, NKEY])
        cst = sb("cst", [P, cw])
        cn = {n: cst[:, a:a + w] for n, (a, w) in clay.items()}
        ident = cn["ident"]
        kvgb = sb("kvgb", [P, LORA])
        keyT = sb("keyT", [P, 2, NK])
        cT = sb("cT", [P, KC, 2])
        bad = sb("bad", [P, N_MOD])
        g1T = sb("g1T", [P, KC])
        g2T = sb("g2T", [P, KC])
        mod = sb("mod", [P, N_MOD, 2])
        cf = sb("cf", [P, KC, 2])
        rstd = sb("rstd", [P, T])
        stat = sb("stat", [P, 4, NT])
        fb = sb("fb", [P, NH])
        fw = sb("fw", [P, 6, NT * NH])
        logf = sb("logf", [P, 6, NH])
        frow = area("probT", 2 * NKEY, NH).rearrange("p (r t) -> p r t", r=2)
        mrow = sb("mrow", [2, 4, P])
        dots = sb("dots", [P, FB])
        idx8 = sb("idx8", [P, 4, GR], U32)
        got = sb("got", [P, 2, GR])
        stage = sb("stage", [P, 2, TD])
        NS = TP * SLOTS // P + TS * SLOTS // P
        SL = NT * SLOTS
        experts = sb("experts", [P, SL], U32)
        at_dot = sb("at_dot", [P, SL], U32)
        gates = sb("gates", [P, SL])
        gsum = sb("gsum", [P, NT * PH])
        wts = sb("wts", [P, NS])
        pb = [ctx.enter_context(nc.psum_tensor(f"pb{i}", [P, 512], F32)) for i in range(8)]

        w_in = [sem(f"w_in{r}") for r in range(RING)]
        w_used = [sem(f"w_used{r}") for r in range(RING)]
        small_in = sem("small_in")
        c_in = sem("c_in")
        x_in = sem("x_in")
        x_in2 = sem("x_in2")
        cache_in = sem("cache_in")
        kfp_in = sem("kfp_in")
        vfp_in = sem("vfp_in")
        out_s = sem("out_s")
        sq_ok, ssq_ok, var_ok, rstd_ok = sem("sq_ok"), sem("ssq_ok"), sem("var_ok"), sem("rstd_ok")
        silu_ok = sem("silu_ok")
        ada_ok, row_ok, col_ps, col_ok = sem("ada_ok"), sem("row_ok"), sem("col_ps"), sem("col_ok")
        cf_ok, hn_ok, h_ok, h_half = sem("cf_ok"), sem("hn_ok"), sem("h_ok"), sem("h_half")
        tokm = sem("tokm")
        tokm_ev = sem("tokm_ev")
        lat_ss, lat_rs, lat_ok = sem("lat_ss"), sem("lat_rs"), sem("lat_ok")
        latT_ps, latT_ok = sem("latT_ps"), sem("latT_ok")
        lat_out = sem("lat_out")
        v_out = sem("v_out")
        f_ps, f_z, f_l, logf_ok, cum_ps, frow_ok, aug_st = (sem("f_ps"), sem("f_z"), sem("f_l"), sem("logf_ok"),
                                                            sem("cum_ps"), sem("frow_ok"), sem("aug_st"))
        proj = sem("proj")
        proj_free = [sem(f"proj_free{b}") for b in range(2)]
        rope_in, rope_ok = sem("rope_in"), sem("rope_ok")
        krt_ps, krt_ok = sem("krt_ps"), sem("krt_ok")
        s_ok, mx_ok, exp_ok, prob_ok = sem("s_ok"), sem("mx_ok"), sem("exp_ok"), sem("prob_ok")
        pt_ps, pt_ok, pv_ok, o_ok, vh_ok = sem("pt_ps"), sem("pt_ok"), sem("pv_ok"), sem("o_ok"), sem("vh_ok")
        aug_in, kt_ps, kt_ok, kt_out = sem("aug_in"), sem("kt_ps"), sem("kt_ok"), sem("kt_out")
        mg_ps, sig_ok = sem("mg_ps"), sem("sig_ok")
        mg_free = [sem(f"mg_free{b}") for b in range(2)]
        x2_ok = sem("x2_ok")
        q_ok, sc_ps, sc_ok = sem("q_ok"), sem("sc_ps"), sem("sc_ok")
        smx_in, smx_ok, route_ok = sem("smx_in"), sem("smx_ok"), sem("route_ok")
        g_in = [sem(f"g_in{r}") for r in range(GR)]
        g_used = [sem(f"g_used{r}") for r in range(GR)]
        a_ps = sem("a_ps")
        a_free = [sem(f"a_free{j}") for j in range(4)]
        a_st = [sem(f"a_st{j}") for j in range(2)]
        ss_in = [sem(f"ss_in{j}") for j in range(2)]
        ss_free = [sem(f"ss_free{j}") for j in range(2)]
        idx_ok = [sem("idx_row_ok"), sem("idx_dot_ok")]
        s_clear = sem("s_clear")
        pool_on = sem("pool_on")
        ht_ps, ht_ok = sem("ht_ps"), sem("ht_ok")
        dot_ok, gelu_ok, wt_ok = sem("dot_ok"), sem("gelu_ok"), sem("wt_ok")
        g2_ps, g2_ok, sum_ps = sem("g2_ps"), sem("g2_ok"), sem("sum_ps")
        acc_ok, acc_free, x2t_ps, y_pre, y_ss, y_rs, y_ok, y_out, y_rs2 = (
            sem("acc_ok"), sem("acc_free"), sem("x2t_ps"), sem("y_pre"), sem("y_ss"), sem("y_rs"), sem("y_ok"), [sem(f"y_out{j}") for j in range(2)], sem("y_rs2"))
        block = ctx.enter_context(nc.Block())

        UB_MLA = 2
        UB_FOX = UB_MLA + 6 * NH
        UB_OUT = UB_FOX + 4 * NH
        UB_WQ = UB_OUT + 2 * KC
        AD_A = KC // 2
        NSMALL = 10

        ORDER = [QT - 1] + list(range(DN)) + [QT]
        D0, D1 = 8, 22
        TRIP, TRIP_S = SLOTS // FB, TS * SLOTS // P // FB

        @block.sync
        def _(sp):
            with sp.Fori(0, NB // RING) as i:
                for r in range(RING):
                    sp.wait_ge(w_used[r], i + 1)
                    sp.dma_start(ring[:, r, :], wstream[i * RING + r]).then_inc(w_in[r], 16)
            for b in range(NB // RING * RING, NB):
                sp.wait_ge(w_used[b % RING], b // RING + 1)
                sp.dma_start(ring[:, b % RING, :], wstream[b]).then_inc(w_in[b % RING], 16)

        @block.tensor
        def _(pe):
            def mm(out, lhsT, rhs, start=True, stop=True):
                return nc.tensor.matmul(out, lhsT, rhs, start=start, stop=stop)

            def tr(out, in_):
                p = in_.shape[0]
                return nc.tensor.transpose(out, in_, ident[0:p, 0:p])

            def blk(base, j, i=0, per=4):
                b = base + j
                pe.wait_ge(w_in[b % RING], 16 * (b // RING + 1) + 16 * (per // RING) * i)
                return b % RING

            def used(ins, slot):
                ins.then_inc(w_used[slot], 1)

            def ada_row(base, j, i, ps):
                s = blk(base, j, i)
                for k in range(KC):
                    last = mm(ps, cT[:, k, :], ring[:, s, k * P:(k + 1) * P], k == 0, k == KC - 1)
                last.then_inc(ada_ok, 1)
                pe.drain().then_inc(w_used[s], 1)

            def ada_cols(n, blocks, batch, ps):
                pe.wait_ge(row_ok, blocks)
                pe.wait_ge(col_ok, batch)
                for j in range(n):
                    last = mm(ps[:, 2 * j:2 * j + 2], mrow[:, j, :], ident[0:2, 0:2])
                last.then_inc(col_ps, 1)

            def sumsq():
                for hf in range(2):
                    for k in range(KC):
                        last = mm(pb[hf][:, 0:HALF], cn["ones"], hreg[:, k, hf * HALF:(hf + 1) * HALF], k == 0, k == KC - 1)
                    last.then_inc(ssq_ok, 1)

            pe.wait_ge(silu_ok, 1)
            pe.wait_ge(small_in, 16 * NSMALL)
            for t0 in (0, ADA_A // 8):
                with pe.Fori(t0, t0 + ADA_A // 8) as i:
                    for j in range(4):
                        ada_row(0, j, i, pb[2 + j][0:2, 0:P])
                    ada_cols(4, 4 * i + 4, i + 1, pb[6])
                if t0 == 0:
                    pe.wait_ge(sq_ok, 1)
                    sumsq()

            def token_major(base, nblk, bank0, tiles, lhs, kper, first):
                for c in range(nblk):
                    s = blk(base, c)
                    for kk in range(kper):
                        k = c * kper + kk
                        if base == B_CKV:
                            pe.wait_ge(h_ok, k + 1)
                        for t in tiles:
                            m = rows(t) if t < 5 else P
                            last = mm(pb[bank0 + t][0:m, :], lhs(k, t), ring[:, s, kk * 512:(kk + 1) * 512],
                                      k == 0, k == nblk * kper - 1)
                    used(last, s)

            def h_tile(k, t):
                return hreg[:, k, t * P:t * P + rows(t)]

            token_major(B_CKV, CKV, 0, range(NT), h_tile, 4, 0)
            pe.drain().then_inc(tokm, 1)
            s = blk(B_KRF, 0)
            for hf in range(2):
                for k in range(KC):
                    last = mm(pb[5 + hf][0:ROPE, 0:HALF], ring[:, s, k * ROPE:(k + 1) * ROPE],
                              hreg[:, k, hf * HALF:(hf + 1) * HALF], k == 0, k == KC - 1)
                last.then_inc(proj, 1)
            for t in range(NT):
                for k in range(KC):
                    last = mm(pb[7][0:rows(t), t * NH:(t + 1) * NH], h_tile(k, t),
                              ring[:, s, KC * ROPE + k * NH:KC * ROPE + (k + 1) * NH], k == 0, k == KC - 1)
            last.then_inc(f_ps, 1)
            pe.drain().then_inc(w_used[s], 1)
            for t in range(NT):
                pe.wait_ge(lat_ok, t + 1)
                m = rows(t)
                for c in range(4):
                    last = tr(pb[t][:, c * P:c * P + m], lat_tok[0:m, t, c * P:(c + 1) * P])
                last.then_inc(latT_ps, 1)
            pe.wait_ge(logf_ok, 1)
            band = cn["band"]
            pe.wait_ge(rope_in, 2)
            for t in range(QT):
                mm(pb[5][0:NH, t * P:TP], logf[:, t, :], band[:, 0:TP - t * P], t == 0, t == QT - 1)
            mm(pb[6][0:NH, 0:PAST + TS], logf[:, 5, :], band[:, 0:PAST + TS], True, False)
            mm(pb[6][0:NH, PAST:PAST + TS], logf[0:TS, 4, :], band[0:TS, 0:TS], False, True).then_inc(cum_ps, 1)
            pe.wait_ge(latT_ok, NT)
            pe.wait_ge(cache_in, 16)
            pe.wait_ge(frow_ok, 1)

            def lat_tile(k, t):
                a = t * P if t < 5 else T
                return latT[:, k, a:a + (rows(t) if t < 5 else P)]

            for n in range(MLAV):
                if n:
                    pe.wait_ge(tokm_ev, 6)
                token_major(B_MLAV + n, 1, 0, range(6), lat_tile, 4, 0)
                pe.drain().then_inc(tokm, 1)
            pe.wait_ge(rope_ok, 2)
            pe.wait_ge(f_z, 1)
            for t in range(NT):
                last = tr(pb[7][0:rows(t), t * ROPE:(t + 1) * ROPE], krT[:, t * P:t * P + rows(t)])
            last.then_inc(krt_ps, 1)
            pe.wait_ge(tokm_ev, 12)
            pe.wait_ge(krt_ok, 1)

            def project(s, lhs, m, src, width, unit0, i, per, n0=0):
                for hf in range(2):
                    u = unit0 + hf
                    pe.wait_ge(proj_free[hf], u // 2 + (per // 2) * i)
                    for k in range(src.shape[1]):
                        last = mm(pb[hf][0:m, 0:width], lhs(k), src[:, k, hf * width:(hf + 1) * width],
                                  k == 0, k == src.shape[1] - 1)
                    last.then_inc(proj, 1)
                return last

            def scores_mla(g):
                pe.wait_ge(rope_ok, 2 + 2 * (g + 1))
                pe.wait_ge(proj_free[1], UB_MLA // 2 + 3 * (g + 1))
                pe.wait_ge(proj_free[0], UB_MLA // 2 + 3 * (g + 1))
                for t in range(NT):
                    m, (b, c) = rows(t), S_AT[t]
                    q = slice(t * P, t * P + m)
                    ks = slice(0, S_W[t]) if t < QT else slice(TP, NKEY)
                    mm(pb[b][0:m, c:c + S_W[t]], qn[:, q], kn[:, ks], True, False)
                    last = mm(pb[b][0:m, c:c + S_W[t]], qr[:, q], krT[:, ks], False, True)
                last.then_inc(s_ok, 1)

            def scores_fox(g, h):
                pe.wait_ge(proj_free[1], UB_FOX // 2 + 2 * (h + 1))
                pe.wait_ge(proj_free[0], UB_FOX // 2 + 2 * (h + 1))
                pe.wait_ge(aug_in, 32 * (h + 1))
                for t in range(NT):
                    m, (b, c) = rows(t), S_AT[t]
                    q = slice(t * P, t * P + m)
                    if t < QT:
                        mm(pb[b][0:m, c:c + S_W[t]], qn[:, q], kn[:, 0:S_W[t]], True, False)
                        last = mm(pb[b][0:m, c:c + S_W[t]], aug_q[:, q], aug_k[:, 0:S_W[t]], False, True)
                    else:
                        mm(pb[b][0:m, c:c + TS], qn[:, q], kn[:, TP:T], True, False)
                        mm(pb[b][0:m, c:c + TS], aug_q[:, q], aug_k[:, TP:T], False, True)
                        mm(pb[b][0:m, c + TS:c + TS + PAST], qn[:, q], kf_past[:, h, :], True, False)
                        last = mm(pb[b][0:m, c + TS:c + TS + PAST], aug_q[:, q], aug_k[:, T:NKEY], False, True)
                last.then_inc(s_ok, 1)

            def weighted_values(g, ada_read):
                pe.wait_ge(prob_ok, g + 1)
                pe.wait_ge(o_ok, g)

                def pt(bank, col, kt):
                    for t in range(kt, QT):
                        last = tr(pb[bank][:, col + (t - kt) * P:col + (t - kt + 1) * P],
                                  prob[:, P_AT[t] + kt * P:P_AT[t] + (kt + 1) * P])
                    return last
                pt(5, 0, 0).then_inc(pt_ps, 1)
                pt(6, 0, 1)
                pt(6, 384, 3).then_inc(pt_ps, 1)
                pe.wait_ge(pt_ok, 3 * g + 1)
                pt(5, 0, 2)
                a = P_AT[QT]
                tr(pb[5][0:TS, 256:256 + TS], prob[0:TS, a:a + TS])
                tr(pb[5][:, 256 + TS:256 + 2 * TS], prob[0:TS, a + TS:a + TS + PAST]).then_inc(pt_ps, 1)
                pe.wait_ge(vh_ok, g + 1)
                pe.wait_ge(pt_ok, 3 * g + 3)
                pe.wait_ge(col_ok, ada_read + 1)
                for kt in range(QT):
                    mm(pb[7][:, kt * P:TP], vh[:, kt, :], probT[:, PT_AT[kt]:PT_AT[kt] + TP - kt * P],
                       kt == 0, kt == QT - 1)
                so = pb[5][:, 440:440 + TS]
                mm(so, vh[0:TS, 4, :], probT[0:TS, PT_S:PT_S + TS], True, False)
                mm(so, vh[:, 5, :], probT[:, PT_S + TS:PT_S + 2 * TS], False, True).then_inc(pv_ok, 1)

            def prev(i):
                return 0 if isinstance(i, int) and i == 0 else i - 1

            def ada_rows2(base, i, o_read, batch):
                pe.wait_ge(o_ok, o_read)
                pe.wait_ge(col_ok, batch)
                for j in range(2):
                    ada_row(base, j, i, pb[7][0:2, j * P:(j + 1) * P])

            def proj_mla(i):
                ada_rows2(B_MLA, i, prev(i), AD_A + i + 1)
                s = blk(B_MLA, 2, i)
                last = project(s, lambda k: ring[:, s, k * P:(k + 1) * P], P, hreg, HALF, UB_MLA, i, 6)
                pe.drain().then_inc(w_used[s], 1)
                s2 = blk(B_MLA, 3, i)
                project(s2, lambda k: ring[:, s2, k * ROPE:(k + 1) * ROPE], ROPE, hreg, HALF, UB_MLA + 2, i, 6)
                project(s2, lambda k: ring[:, s2, KC * ROPE + k * P:KC * ROPE + (k + 1) * P], P, latT, KHALF, UB_MLA + 4, i, 6)
                pe.drain().then_inc(w_used[s2], 1)
                ada_cols(2, ADA_A + 2 * i + 2, AD_A + i + 1, pb[7][:, 256:260])

            proj_mla(0)
            scores_mla(0)
            with pe.Fori(1, NH) as i:
                proj_mla(i)
                weighted_values(i - 1, AD_A + i + 1)
                scores_mla(i)
            weighted_values(NH - 1, AD_A + NH)

            pe.wait_ge(mx_ok, NH)
            pe.wait_ge(exp_ok, NH)
            pe.wait_ge(o_ok, NH)
            for n in range(2):
                if n:
                    pe.wait_ge(tokm_ev, 12 + NT)
                token_major(B_FOXV + 4 * n, 4, 0, range(NT), h_tile, 4, 0)
                pe.drain().then_inc(tokm, 1)
            pe.wait_ge(tokm_ev, 12 + 2 * NT)
            pe.wait_ge(kfp_in, 16)

            def proj_fox(i):
                ada_rows2(B_FOX, i, prev(i) + NH, AD_A + NH + i + 1)
                s = blk(B_FOX, 2, i)
                project(s, lambda k: ring[:, s, k * P:(k + 1) * P], P, hreg, HALF, UB_FOX, i, 4)
                pe.drain().then_inc(w_used[s], 1)
                s2 = blk(B_FOX, 3, i)
                project(s2, lambda k: ring[:, s2, k * P:(k + 1) * P], P, hreg, HALF, UB_FOX + 2, i, 4)
                pe.drain().then_inc(w_used[s2], 1)
                ada_cols(2, ADA_A + 2 * NH + 2 * i + 2, AD_A + NH + i + 1, pb[7][:, 256:260])

            def keys_out(h):
                pe.wait_ge(o_ok, NH + h)
                for t in range(NT):
                    m = rows(t)
                    o = pb[5][0:m, t * P:(t + 1) * P] if t < QT else pb[6][0:m, 0:P]
                    last = tr(o, kn[:, t * P:t * P + m])
                last.then_inc(kt_ps, 1)

            proj_fox(0)
            scores_fox(NH, 0)
            pe.wait_ge(pt_ok, 3 * NH)
            keys_out(0)
            with pe.Fori(1, NH) as i:
                proj_fox(i)
                pe.wait_ge(kt_ok, i)
                weighted_values(NH - 1 + i, AD_A + NH + i + 1)
                scores_fox(NH + i, i)
                pe.wait_ge(pt_ok, 3 * NH + 3 * i)
                keys_out(i)
            pe.wait_ge(kt_ok, NH)
            weighted_values(2 * NH - 1, AD_A + 2 * NH)
            pe.wait_ge(exp_ok, 2 * NH)
            pe.wait_ge(o_ok, 2 * NH)

            with pe.Fori(0, KC) as i:
                sm = blk(B_MERGE, 0, i)
                sf = blk(B_MERGE, 1, i)
                so = blk(B_MERGE, 2, i)
                for hf in range(2):
                    cols = slice(hf * HALF, (hf + 1) * HALF)
                    pe.wait_ge(mg_free[hf], i + 1)
                    if hf:
                        ada_row(B_MERGE, 3, i, pb[4][0:2, 0:P])
                    for q, s, off, src, k0, kn_ in [(1, sf, 0, hreg, 0, KC), (2, so, 0, oreg, 0, NH),
                                                    (3, so, NH * P, oreg, NH, NH), (0, sm, 0, hreg, 0, KC)]:
                        if hf and q == 3:
                            ada_cols(1, ADA_A + 4 * NH + i + 1, AD_A + 2 * NH + i + 1, pb[4][:, 256:258])
                        if hf and q == 0:
                            pe.wait_ge(col_ok, AD_A + 2 * NH + i + 2)
                        for k in range(kn_):
                            last = mm(pb[4 * hf + q][:, 0:HALF], ring[:, s, off + k * P:off + (k + 1) * P],
                                      src[:, k0 + k, cols], k == 0, k == kn_ - 1)
                    last.then_inc(mg_ps, 1)
                pe.drain().then_inc(w_used[sm], 1)
                pe.drain().then_inc(w_used[sf], 1)
                pe.drain().then_inc(w_used[so], 1)
            for b in range(2):
                pe.wait_ge(mg_free[b], KC + 1)
            pe.wait_ge(x_in2, 16)
            with pe.Fori(0, KC // 2) as i:
                for j in range(2):
                    ada_row(B_OUT, j, i, pb[2 + j][0:2, 0:P])
                for j in range(2):
                    s = blk(B_OUT, 2 + j, i)
                    project(s, lambda k: ring[:, s, k * P:(k + 1) * P], P, merged, HALF, UB_OUT + 2 * j, i, 4)
                    pe.drain().then_inc(w_used[s], 1)
                    if j == 0:
                        ada_cols(2, ADA_A + 4 * NH + KC + 2 * i + 2, AD_A + 2 * NH + KC + i + 1, pb[4][:, 0:4])
            pe.wait_ge(sq_ok, 2)
            for b in range(2):
                pe.wait_ge(proj_free[b], UB_WQ // 2)
            sumsq()
            pe.wait_ge(h_ok, 2 * KC)
            with pe.Fori(0, KC // 4) as i:
                for j in range(4):
                    s = blk(B_WQ, j, i)
                    project(s, lambda k: ring[:, s, k * P:(k + 1) * P], P, hreg, HALF, UB_WQ + 2 * j, i, 8)
                    pe.drain().then_inc(w_used[s], 1)
                    pe.wait_ge(q_ok, 4 * i + j + 1)
                    pe.wait_ge(sc_ok, 4 * i + j + 1)
                    for t in range(NT):
                        m = rows(t)
                        o = pb[2][0:m, t * P:(t + 1) * P] if t < QT else pb[3][0:m, 0:P]
                        last = mm(o, qn_peer[:, t * P:t * P + m], keyT[:, j % 2, :])
                    last.then_inc(sc_ps, 1)

            def gate2_rows(g):
                for k in range(KC):
                    c = 4 + k // 4
                    last = mm(pb[c][:, (k % 4) * P:(k % 4 + 1) * P],
                              mod[:, 5 * KC + k, g:g + 1].to_broadcast([P, P]), ident)
                last.then_inc(g2_ps, 1)

            def tokens_of(src, t, m, s):
                for k in range(KC):
                    last = tr(pb[4 + k // 4][0:m, (k % 4) * P:(k % 4 + 1) * P], src[:, k, t * P:t * P + m])
                last.then_inc(s, 1)

            def dense(t0, t1):
                with pe.Fori(t0, t1) as i:
                    for j in range(4):
                        s = blk(B_UT, j, i)
                        pe.wait_ge(a_free[j], i + 1)
                        for k in range(KC):
                            last = mm(pb[j][:, 0:TD], ring[:, s, k * P:(k + 1) * P], hreg[:, k, 0:TD], k == 0, k == KC - 1)
                        last.then_inc(a_ps, 1)
                        pe.drain().then_inc(w_used[s], 1)

            pe.wait_ge(sc_ok, KC + 1)
            dense(0, D0)
            gate2_rows(0)
            pe.wait_ge(g2_ok, 1)
            for n, t in enumerate((QT - 1, QT)):
                tokens_of(hreg, t, rows(t), ht_ps)
                pe.wait_ge(ht_ok, n + 1)
            tokens_of(oreg, QT - 1, P, x2t_ps)
            dense(D0, D1)
            dense(D1, NK // 4)
            for n, t in enumerate(ORDER):
                if n == 0:
                    continue
                pe.wait_ge(acc_free, n)
                if t == QT:
                    gate2_rows(1)
                    pe.wait_ge(g2_ok, 2)
                tokens_of(oreg, t, rows(t), x2t_ps)
            pe.wait_ge(acc_ok, 1)
            for c in range(4):
                last = mm(pb[c][0:TS, :], cn["stack"][:, 0:TS], accs[(NT - 1) % 2][:, c * 512:(c + 1) * 512])
            last.then_inc(sum_ps, 1)

        @block.scalar
        def _(act):
            def a(out, in_, fn=ACT.Copy, **kw):
                return nc.scalar.activation(out, in_, fn, **kw)

            act.dma_start(cT[:, :, :], c_t).then_inc(c_in, 16)
            act.dma_start(cst[:, :], consts).then_inc(small_in, 16)
            act.dma_start(oreg[:, :, :], x_t).then_inc(x_in, 16)
            act.dma_start(bad[:, :], b_ada).then_inc(small_in, 16)
            act.dma_start(g1T[:, :], g1).then_inc(small_in, 16)
            act.dma_start(g2T[:, :], g2).then_inc(small_in, 16)
            act.dma_start(kvgb[:, :], kvg.to_broadcast([P, LORA])).then_inc(small_in, 16)
            act.dma_start(fb[:, :], fbias.to_broadcast([P, NH])).then_inc(small_in, 16)
            act.dma_start(keyT[:, :, :], keys).then_inc(small_in, 16)
            act.dma_start(fgb[:, :], final_g.to_broadcast([P, D])).then_inc(small_in, 16)
            act.dma_start(logf[:, 5, :], logf_cache).then_inc(small_in, 16)
            act.dma_start(krT[:, T:NKEY], kr_cache).then_inc(small_in, 16)
            act.dma_start(latT[:, :, T:NKEY], lat_cache).then_inc(cache_in, 16)
            act.wait_ge(c_in, 16)
            a(cT[:, :, :], cT[:, :, :], ACT.Silu).then_inc(silu_ok, 1)

            def norm(n, scale0):
                act.wait_ge(var_ok, n + 1)
                a(rstd[:, :], rstd[:, :], ACT.Sqrt).then_inc(rstd_ok, 1)
                with act.Fori(0, KC) as k:
                    act.wait_ge(hn_ok, n * KC + k + 1)
                    act.wait_ge(cf_ok, n + 1)
                    for g, cols in enumerate((slice(0, TP), slice(TP, T))):
                        a(hreg[:, k, cols], hreg[:, k, cols], ACT.Identity, scale=cf[:, k, g:g + 1],
                          bias=mod[:, scale0 + k, g:g + 1]).then_inc(*((h_ok, 1) if g else (h_half, 1)))

            def copy_rows(n, blocks, batch, src):
                act.wait_ge(col_ps, batch)
                for j in range(n):
                    act.wait_ge(ada_ok, blocks - n + j + 1 if len(src) > 1 else blocks)
                    a(mrow[:, j, :], src[j] if len(src) > 1 else src[0][:, j * P:(j + 1) * P]).then_inc(row_ok, 1)

            with act.Fori(0, ADA_A // 4) as i:
                copy_rows(4, 4 * i + 4, i + 1, [pb[2 + j][0:2, 0:P] for j in range(4)])
            norm(0, 0)
            act.wait_ge(tokm, 1)
            for t in range(NT):
                m = rows(t)
                a(lat_tok[0:m, t, :], pb[t][0:m, :], ACT.Square, accum_out=stat[0:m, 0, t:t + 1])
            act.drain().then_inc(lat_ss, 1)

            def rope_copy(bank, unit, kf, u):
                act.wait_ge(proj, u)
                act.wait_ge(rope_ok, kf)
                a(rope_x, pb[bank][0:ROPE, 0:HALF])
                a(rope_r[0:32, :], pb[bank][32:64, 0:HALF])
                a(rope_r[32:64, :], pb[bank][0:32, 0:HALF])
                return act.drain()

            for hf in range(2):
                rope_copy(5 + hf, hf, hf, hf + 1).then_inc(rope_in, 1)
            act.wait_ge(lat_rs, 1)
            a(stat[:, 1, :], stat[:, 1, :], ACT.Sqrt)
            act.drain().then_inc(lat_rs, 1)
            act.wait_ge(f_z, 1)
            a(fw[:, 2, :], fw[:, 1, :], ACT.Exp, scale=-1.0)
            act.drain()
            a(fw[:, 3, :], fw[:, 2, :], ACT.Ln, bias=1.0)
            act.drain().then_inc(f_l, 1)
            for t in range(NT):
                act.wait_ge(latT_ps, t + 1)
                m = rows(t)
                a(latT[:, :, t * P:t * P + m], pb[t][:, :].rearrange("p (c t) -> p c t", c=4)[:, :, 0:m]).then_inc(latT_ok, 1)
            act.wait_ge(lat_out, 32)
            for n in range(2):
                act.wait_ge(tokm, 2 + n)
                for t in range(6):
                    m = rows(t) if t < 5 else P
                    a(v_tok[0:m, t, n * 512:(n + 1) * 512], pb[t][0:m, :]).then_inc(tokm_ev, 1)
            act.wait_ge(krt_ps, 1)
            a(ktok[:, 0:QT, 0:ROPE], pb[7][:, 0:QT * ROPE].rearrange("p (t d) -> p t d", d=ROPE))
            a(ktok[0:TS, QT, 0:ROPE], pb[7][0:TS, QT * ROPE:NT * ROPE])
            act.drain().then_inc(krt_ok, 1)
            act.sem_inc(proj_free[0], 1)
            act.sem_inc(proj_free[1], 1)

            def softmax_exp(g, scale):
                act.wait_ge(mx_ok, g + 1)
                for t in range(NT):
                    m, (b, c) = rows(t), S_AT[t]
                    a(prob[0:m, P_AT[t]:P_AT[t] + S_W[t]], pb[b][0:m, c:c + S_W[t]], ACT.Exp,
                      bias=stat[0:m, 2, t:t + 1], scale=scale, accum_out=stat[0:m, 3, t:t + 1])
                act.drain().then_inc(exp_ok, 1)

            def copy_pt(g):
                act.wait_ge(pt_ps, 3 * g + 1)
                act.wait_ge(pv_ok, g)
                act.wait_ge(aug_st, 64)
                a(probT[:, 0:512], pb[5][:, :]).then_inc(pt_ok, 1)
                act.wait_ge(pt_ps, 3 * g + 2)
                a(probT[:, PT_AT[1]:PT_AT[1] + 384], pb[6][:, 0:384])
                a(probT[:, PT_AT[3]:PT_AT[3] + 128], pb[6][:, 384:512]).then_inc(pt_ok, 1)
                act.wait_ge(pt_ps, 3 * g + 3)
                a(probT[:, PT_AT[2]:PT_AT[2] + 256], pb[5][:, 0:256])
                a(probT[0:TS, PT_S:PT_S + TS], pb[5][0:TS, 256:256 + TS])
                a(probT[:, PT_S + TS:PT_S + 2 * TS], pb[5][:, 256 + TS:256 + 2 * TS]).then_inc(pt_ok, 1)

            def copy_o(g):
                act.wait_ge(pv_ok, g + 1)
                a(oreg[:, bass.ds(g, 1), 0:TP], pb[7][:, :].rearrange("p (o t) -> p o t", o=1))
                a(oreg[:, bass.ds(g, 1), TP:T], pb[5][:, 440:440 + TS].rearrange("p (o t) -> p o t", o=1))
                act.drain().then_inc(o_ok, 1)

            def evict_mla(i):
                copy_rows(2, ADA_A + 2 * i + 2, AD_A + i + 1, [pb[7][0:2, 0:2 * P]])
                act.wait_ge(s_ok, i)
                for hf in range(2):
                    act.wait_ge(proj, UB_MLA + hf + 1 + 6 * i)
                    a(qn[:, hf * HALF:(hf + 1) * HALF], pb[hf][:, 0:HALF]).then_inc(proj_free[hf], 1)
                for hf in range(2):
                    rope_copy(hf, 0, 2 + 2 * i + hf, UB_MLA + 2 + hf + 1 + 6 * i)
                    act.drain().then_inc(proj_free[hf], 1)
                    act.drain().then_inc(rope_in, 1)
                for hf in range(2):
                    act.wait_ge(proj, UB_MLA + 4 + hf + 1 + 6 * i)
                    a(kn[:, hf * KHALF:(hf + 1) * KHALF], pb[hf][:, 0:KHALF]).then_inc(proj_free[hf], 1)

            evict_mla(0)
            softmax_exp(0, SC_MLA)
            with act.Fori(1, NH) as i:
                evict_mla(i)
                copy_pt(i - 1)
                copy_o(i - 1)
                softmax_exp(i, SC_MLA)
            copy_pt(NH - 1)
            copy_o(NH - 1)
            act.wait_ge(vh_ok, NH)
            for n in range(2):
                act.wait_ge(tokm, 4 + n)
                for t in range(NT):
                    m = rows(t)
                    a(v_tok[0:m, t, n * 512:(n + 1) * 512], pb[t][0:m, :]).then_inc(tokm_ev, 1)

            def evict_fox(i):
                copy_rows(2, ADA_A + 2 * NH + 2 * i + 2, AD_A + NH + i + 1, [pb[7][0:2, 0:2 * P]])
                act.wait_ge(s_ok, NH + i)
                act.wait_ge(kt_ps, i)
                for hf in range(2):
                    act.wait_ge(proj, UB_FOX + hf + 1 + 4 * i)
                    a(qn[:, hf * HALF:(hf + 1) * HALF], pb[hf][:, 0:HALF], scale=SC_FOX).then_inc(proj_free[hf], 1)
                for hf in range(2):
                    act.wait_ge(proj, UB_FOX + 2 + hf + 1 + 4 * i)
                    a(kn[:, hf * HALF:(hf + 1) * HALF], pb[hf][:, 0:HALF]).then_inc(proj_free[hf], 1)

            def copy_keys(i):
                act.wait_ge(kt_ps, i + 1)
                act.wait_ge(kt_out, 32 * i)
                act.wait_ge(out_s, 16 * 4)
                a(ktok[:, 0:QT, :], pb[5][:, :].rearrange("p (t d) -> p t d", t=QT))
                a(ktok[0:TS, QT, :], pb[6][0:TS, 0:P])
                act.drain().then_inc(kt_ok, 1)

            evict_fox(0)
            softmax_exp(NH, 1.0)
            copy_keys(0)
            with act.Fori(1, NH) as i:
                evict_fox(i)
                copy_pt(NH - 1 + i)
                copy_o(NH - 1 + i)
                softmax_exp(NH + i, 1.0)
                copy_keys(i)
            copy_pt(2 * NH - 1)
            copy_o(2 * NH - 1)
            act.wait_ge(vh_ok, 2 * NH)
            act.wait_ge(kt_out, 32 * NH)
            act.wait_ge(v_out, 32)
            with act.Fori(0, KC) as i:
                for hf in range(2):
                    if hf:
                        copy_rows(1, ADA_A + 4 * NH + i + 1, AD_A + 2 * NH + i + 1, [pb[4][0:2, 0:P]])
                    act.wait_ge(mg_ps, 2 * i + hf + 1)
                    act.wait_ge(mg_free[hf], i + 1)
                    a(sg[:, 2 * hf, :], pb[4 * hf][:, 0:HALF], ACT.Sigmoid)
                    a(sg[:, 2 * hf + 1, :], pb[4 * hf + 1][:, 0:HALF], ACT.Sigmoid)
                    act.drain().then_inc(sig_ok, 1)
            act.wait_ge(mg_ps, 2 * KC)
            act.dma_start(oreg[:, :, :], x_t).then_inc(x_in2, 16)
            with act.Fori(0, KC // 2) as i:
                copy_rows(2, ADA_A + 4 * NH + KC + 2 * i + 2, AD_A + 2 * NH + KC + i + 1, [pb[2 + j][0:2, 0:P] for j in range(2)])
            norm(1, 3 * KC)
            act.wait_ge(s_clear, 1)
            with act.Fori(0, KC // 4) as i:
                for j in range(4):
                    n = 4 * i + j
                    for hf in range(2):
                        act.wait_ge(proj, UB_WQ + 2 * j + hf + 1 + 8 * i)
                        a(qn_peer[:, hf * HALF:(hf + 1) * HALF], pb[hf][:, 0:HALF]).then_inc(proj_free[hf], 1)
                    act.drain().then_inc(q_ok, 1)
                    act.wait_ge(sc_ps, n + 1)
                    a(s_all.rearrange("p t (n k) -> p n t k", k=NK)[:, bass.ds(n, 1), 0:QT, :],
                      pb[2][:, :].rearrange("p (o t k) -> p o t k", o=1, t=QT))
                    a(s_all[0:TS, QT, bass.ds(n * NK, NK)], pb[3][0:TS, 0:P])
                    act.drain().then_inc(sc_ok, 1)
            def dense_out(i):
                for j in range(4):
                    act.wait_ge(a_ps, 4 * i + j + 1)
                    if not (isinstance(i, int) and j < 2):
                        act.wait_ge(a_st[j % 2], 32 * i + 16 * (j // 2))
                    a(stage[:, j % 2, :], pb[j][:, 0:TD]).then_inc(a_free[j], 1)
                    act.wait_ge(a_free[j], i + 2)
                    act.dma_start(dots_dram[bass.ds(P * (4 * i + j), P), :], stage[:, j % 2, :]).then_inc(a_st[j % 2], 16)

            def to_sbuf(dst, banks, m):
                for c in range(4):
                    a(dst[0:m, c * 512:(c + 1) * 512], pb[banks + c][0:m, :])

            dense_out(0)
            with act.Fori(1, D0) as i:
                dense_out(i)
            act.wait_ge(smx_in, 1)
            a(gates[:, :], gates[:, :], ACT.Exp).then_inc(smx_ok, 1)
            act.wait_ge(g2_ps, 1)
            act.wait_ge(route_ok, 1)
            to_sbuf(g2b, 4, P)
            act.drain().then_inc(g2_ok, 1)
            act.wait_ge(ht_ps, 1)
            to_sbuf(h2_tok[0], 4, P)
            act.drain().then_inc(ht_ok, 1)
            act.wait_ge(ht_ps, 2)
            for g in range(4):
                for c in range(4):
                    a(h2_tok[1][32 * g:32 * g + TS, c * 512:(c + 1) * 512], pb[4 + c][0:TS, :])
            act.drain().then_inc(ht_ok, 1)
            with act.Fori(D0, D1) as i:
                dense_out(i)

            def gelu(n, t):
                act.wait_ge(dot_ok, n + 1)
                c0, w = t * SLOTS, (SLOTS if t < QT else TS)
                a(wts[:, c0:c0 + w], wts[:, c0:c0 + w], ACT.Gelu).then_inc(gelu_ok, 1)

            gelu(0, QT - 1)
            gelu(1, QT)
            with act.Fori(D1, NK // 4) as i:
                dense_out(i)

            def dots_in(t):
                with act.Fori(t * SLOTS // FB, (t + 1) * SLOTS // FB) as i:
                    for lap in range(2):
                        act.wait_ge(ss_in[lap], 16 * GR * (i + 1))
                        a(wts[:, bass.ds(FB * i + GR * lap, GR)], got[:, lap, :]).then_inc(ss_free[lap], 1)
                act.drain().then_inc(dot_ok, 1)

            def finish(n, t):
                m = rows(t)
                act.wait_ge(y_pre, n + 1)
                a(sq_junk[0:m, :], accs[n % 2][0:m, :], ACT.Square, accum_out=stat[0:m, 0, t:t + 1])
                act.drain().then_inc(y_ss, 1)
                act.wait_ge(y_rs, n + 1)
                a(stat[0:m, 1, t:t + 1], stat[0:m, 1, t:t + 1], ACT.Sqrt).then_inc(y_rs2, 1)
                act.wait_ge(y_ok, n + 1)
                dst = y_p[0, t * P:(t + 1) * P, :] if t < QT else y_s[0, :, :]
                act.dma_start(dst, accs[n % 2][0:m, :]).then_inc(y_out[n % 2], 16)

            dots_in(0)
            gelu(2, 0)
            for n, t in enumerate(ORDER):
                if 1 <= n < DN:
                    dots_in(t + 1)
                    gelu(2 + n, t + 1)
                if t == QT:
                    act.wait_ge(g2_ps, 2)
                    act.wait_ge(y_ok, NT - 1)
                    to_sbuf(g2b, 4, P)
                    act.drain().then_inc(g2_ok, 1)
                finish(n, t)
            act.wait_ge(y_out[0], 16 * ((NT + 1) // 2))
            act.wait_ge(y_out[1], 16 * (NT // 2))

        @block.vector
        def _(dve):
            v = nc.vector

            def square(src, n, gate):
                v.tensor_tensor(hreg[:, :, :], src[:, :, :], src[:, :, :], ALU.mult)
                dve.drain().then_inc(sq_ok, 1)

            def mod_out(n, batch, idx, ps):
                dve.wait_ge(col_ps, batch + 2)
                v.tensor_tensor(mod[:, bass.ds(idx, n), :], ps.rearrange("p (n g) -> p n g", g=2),
                                bad[:, bass.ds(idx, n)].rearrange("p (n o) -> p n o", o=1).to_broadcast([P, n, 2]),
                                ALU.add).then_inc(col_ok, 1)

            def norm(n, src, g, scale0):
                for hf in range(2):
                    dve.wait_ge(ssq_ok, 2 * n + hf + 1)
                    v.tensor_scalar(rstd[:, hf * HALF:(hf + 1) * HALF], pb[hf][:, 0:HALF], 1.0 / D, EPS, ALU.mult, ALU.add)
                dve.drain()
                v.reciprocal(rstd[:, :], rstd[:, :])
                dve.drain().then_inc(var_ok, 1)

            def norm2(n, src, g, scale0):
                dve.wait_ge(rstd_ok, n + 1)
                v.tensor_scalar(cf[:, :, :], mod[:, scale0:scale0 + KC, :], 1.0, None, ALU.add)
                dve.drain()
                v.tensor_tensor(cf[:, :, :], cf[:, :, :], g[:, :].rearrange("p (k o) -> p k o", o=1).to_broadcast([P, KC, 2]), ALU.mult)
                dve.drain().then_inc(cf_ok, 1)
                with dve.Fori(0, KC) as k:
                    v.tensor_tensor(hreg[:, bass.ds(k, 1), :].rearrange("p o t -> p (o t)"),
                                    src[:, bass.ds(k, 1), :].rearrange("p o t -> p (o t)"), rstd[:, :], ALU.mult).then_inc(hn_ok, 1)

            v.memset(stat[:, :, :], 1.0)
            v.memset(logf[:, 0:5, :], 0.0)
            v.memset(fw[:, :, :], 0.0)
            dve.wait_ge(x_in, 16)
            dve.wait_ge(small_in, 16 * NSMALL)
            square(oreg, 0, None)
            for t0 in (0, ADA_A // 8):
                with dve.Fori(t0, t0 + ADA_A // 8) as i:
                    mod_out(4, i, 4 * i, pb[6][:, 0:8])
                if t0 == 0:
                    norm(0, oreg, g1T, KC)
            dve.drain()
            norm2(0, oreg, g1T, KC)

            dve.wait_ge(lat_ss, 1)
            v.tensor_scalar(stat[:, 1, :], stat[:, 0, :], 1.0 / LORA, EPS, ALU.mult, ALU.add)
            dve.drain()
            v.reciprocal(stat[:, 1, :], stat[:, 1, :])
            dve.drain().then_inc(lat_rs, 1)

            def rotate(dst, hf, n):
                dve.wait_ge(rope_in, n)
                cols = slice(hf * HALF, (hf + 1) * HALF)
                v.tensor_tensor(rope_x, rope_x, cn["cos"][0:ROPE, cols], ALU.mult)
                v.tensor_tensor(rope_r, rope_r, cn["sin"][0:ROPE, cols], ALU.mult)
                dve.drain()
                v.tensor_tensor(dst[:, cols], rope_x, rope_r, ALU.add)
                dve.drain().then_inc(rope_ok, 1)

            for hf in range(2):
                rotate(krT, hf, hf + 1)
            dve.wait_ge(f_ps, 1)
            for t in range(NT):
                m = rows(t)
                v.tensor_tensor(fw[0:m, 0, t * NH:(t + 1) * NH], pb[7][0:m, t * NH:(t + 1) * NH], fb[0:m, :], ALU.add)
            dve.drain()
            v.tensor_scalar(fw[:, 1, :], fw[:, 0, :], -1.0, None, ALU.mult)
            v.tensor_scalar(fw[:, 4, :], fw[:, 0, :], 0.0, None, ALU.min)
            dve.drain()
            v.tensor_tensor(fw[:, 1, :], fw[:, 1, :], fw[:, 0, :], ALU.max)
            dve.drain().then_inc(f_z, 1)
            dve.wait_ge(lat_rs, 2)
            for t in range(NT):
                m = rows(t)
                v.scalar_tensor_tensor(lat_tok[0:m, t, :], pb[t][0:m, :], stat[0:m, 1, t:t + 1], kvgb[0:m, :],
                                       ALU.mult, ALU.mult).then_inc(lat_ok, 1)
            dve.wait_ge(f_l, 1)
            v.tensor_tensor(fw[:, 5, :], fw[:, 4, :], fw[:, 3, :], ALU.subtract)
            dve.drain()
            for t in range(NT):
                m = rows(t)
                v.tensor_copy(logf[0:m, t, :], fw[0:m, 5, t * NH:(t + 1) * NH])
            dve.drain().then_inc(logf_ok, 1)
            dve.wait_ge(cum_ps, 1)
            for a_, b_, src in ((0, TP, pb[5][0:NH, 0:TP]), (TP, T, pb[6][0:NH, PAST:PAST + TS]), (T, NKEY, pb[6][0:NH, 0:PAST])):
                v.tensor_copy(frow[:, 0, a_:b_], src)
            dve.drain()
            v.tensor_scalar(frow[:, 1, :], frow[:, 0, :], -1.0, None, ALU.mult)
            dve.drain().then_inc(frow_ok, 1)

            def row_max(g, mask, scale):
                dve.wait_ge(s_ok, g + 1)
                for t in range(QT):
                    b, c = S_AT[t]
                    d = pb[b][:, c + t * P:c + (t + 1) * P]
                    v.tensor_tensor(d, d, mask, ALU.add)
                if scale == 1.0:
                    b, c = S_AT[QT]
                    d = pb[b][0:TS, c:c + TS]
                    v.tensor_tensor(d, d, mask[0:TS, 0:TS], ALU.add)
                dve.drain()
                for t in range(NT):
                    m, (b, c) = rows(t), S_AT[t]
                    v.reduce_max(stat[0:m, 2, t:t + 1], pb[b][0:m, c:c + S_W[t]], AX.X)
                dve.drain()
                v.tensor_scalar(stat[:, 2, :], stat[:, 2, :], -scale, None, ALU.mult)
                dve.drain().then_inc(mx_ok, 1)

            def divide(g):
                dve.wait_ge(exp_ok, g + 1)
                v.reciprocal(stat[:, 3, :], stat[:, 3, :])
                dve.drain()
                for t in range(NT):
                    m = rows(t)
                    pr = prob[0:m, P_AT[t]:P_AT[t] + S_W[t]]
                    v.tensor_scalar(pr, pr, stat[0:m, 3, t:t + 1], None, ALU.mult)
                dve.drain().then_inc(prob_ok, 1)

            with dve.Fori(0, NH) as i:
                for hf in range(2):
                    rotate(qr, hf, 2 + 2 * i + hf + 1)
                mod_out(2, AD_A + i, 2 * KC + 2 * i, pb[7][:, 256:260])
                row_max(i, cn["mask_mla"], SC_MLA)
                divide(i)
            with dve.Fori(0, NH) as i:
                mod_out(2, AD_A + NH + i, 3 * KC + 2 * i, pb[7][:, 256:260])
                row_max(NH + i, cn["mask_fox"], 1.0)
                divide(NH + i)

            dve.wait_ge(o_ok, 2 * NH)
            dve.wait_ge(kt_out, 32 * NH)
            with dve.Fori(0, KC) as i:
                for hf in range(2):
                    if hf:
                        mod_out(1, AD_A + 2 * NH + i, 4 * KC + i, pb[4][:, 256:258])
                    dve.wait_ge(sig_ok, 2 * i + hf + 1)
                    s0, s1 = sg[:, 2 * hf, :], sg[:, 2 * hf + 1, :]
                    v.tensor_tensor(s0, s0, pb[4 * hf + 2][:, 0:HALF], ALU.mult)
                    v.tensor_tensor(s1, s1, pb[4 * hf + 3][:, 0:HALF], ALU.mult)
                    dve.drain()
                    v.tensor_tensor(merged[:, bass.ds(i, 1), hf * HALF:(hf + 1) * HALF].rearrange("p o t -> p (o t)"), s0, s1, ALU.add)
                    dve.drain().then_inc(mg_free[hf], 1)
            dve.wait_ge(x_in2, 16)
            with dve.Fori(0, KC // 2) as i:
                for j in range(2):
                    for hf in range(2):
                        dve.wait_ge(proj, UB_OUT + 2 * j + hf + 1 + 4 * i)
                        parts = [(0, HALF, 0)] if hf == 0 else [(HALF, TP, 0), (TP, T, 1)]
                        for a_, b_, g in parts:
                            xr = oreg[:, bass.ds(2 * i + j, 1), a_:b_].rearrange("p o t -> p (o t)")
                            v.scalar_tensor_tensor(xr, pb[hf][:, a_ - hf * HALF:b_ - hf * HALF],
                                                   mod[:, bass.ds(2 * KC + 2 * i + j, 1), g:g + 1].rearrange("p o g -> p (o g)"),
                                                   xr, ALU.mult, ALU.add)
                        dve.drain().then_inc(proj_free[hf], 1)
                    if j == 0:
                        mod_out(2, AD_A + 2 * NH + KC + i, 5 * KC + 2 * i, pb[4][:, 0:4])
            dve.drain()
            square(oreg, 1, None)
            norm(1, oreg, g2T, 4 * KC)
            norm2(1, oreg, g2T, 4 * KC)

            dve.wait_ge(proj_free[1], UB_WQ // 2)
            v.memset(s_all[:, QT, :], 0.0)
            dve.drain().then_inc(s_clear, 1)
            dve.wait_ge(sc_ok, KC + 1)
            with dve.Fori(0, NT) as t:
                v.tensor_copy(wk[:, 0:D], s_all[:, bass.ds(t, 1), :].rearrange("p o n -> p (o n)"))
                dve.drain()

                def top16(src, rep, val, ind):
                    n = len(src)
                    for q in range(n):
                        v.max(val[q][:, 0:8], src[q])
                    dve.drain()
                    for q in range(n):
                        v.max_index(ind[q][:, 0:8], val[q][:, 0:8], src[q])
                        v.match_replace(rep[q], val[q][:, 0:8], src[q], -3.0e38)
                    dve.drain()
                    for q in range(n):
                        v.max(val[q][:, 8:16], rep[q])
                    dve.drain()
                    for q in range(n):
                        v.max_index(ind[q][:, 8:16], val[q][:, 8:16], rep[q])
                    dve.drain()

                src = [wk[:, q * NK:(q + 1) * NK] for q in range(2 * PH)]
                rep = [wk[:, D + q * NK:D + (q + 1) * NK] for q in range(2 * PH)]
                top16(src, rep, [top_v[:, q, :] for q in range(2 * PH)], [top_i[:, q, :] for q in range(2 * PH)])
                v1 = top_v.rearrange("p (h s) k -> p h s k", s=2)
                cand = wk[:, 0:D].rearrange("p (h a b) -> p h a b", h=PH, a=TOPK)
                va = v1[:, :, 0, :].rearrange("p h (k o) -> p h k o", o=1).to_broadcast([P, PH, TOPK, TOPK])
                vb = v1[:, :, 1, :].rearrange("p h (o k) -> p h o k", o=1).to_broadcast([P, PH, TOPK, TOPK])
                v.tensor_tensor(cand, va, vb, ALU.add)
                v.tensor_copy(top_if[:, :, :], top_i[:, :, :])
                dve.drain()
                src = [wk[:, h * 256:(h + 1) * 256] for h in range(PH)]
                rep = [wk[:, D + h * 256:D + (h + 1) * 256] for h in range(PH)]
                top16(src, rep, [sc_v[:, h, :] for h in range(PH)], [sel[:, h, :] for h in range(PH)])
                v.tensor_tensor(gates[:, bass.ds(t * SLOTS, SLOTS)].rearrange("p (h k) -> p h k", h=PH), sc_v[:, :, :],
                                sc_v[:, :, 0:1].to_broadcast([P, PH, TOPK]), ALU.subtract)
                v.tensor_scalar(sel_a[:, :, :], sel[:, :, :], 4, None, ALU.logical_shift_right)
                v.tensor_scalar(sel_b[:, :, :], sel[:, :, :], 15, None, ALU.bitwise_and)
                dve.drain()
                v.tensor_copy(sel_f[:, 0], sel_a[:, :, :])
                v.tensor_copy(sel_f[:, 1], sel_b[:, :, :])
                dve.drain()
                i1 = top_if.rearrange("p (h s) k -> p h s k", s=2)
                iota = cn["iota"].rearrange("p (a b j) -> p a b j", a=1, b=1).to_broadcast([P, PH, TOPK, TOPK])
                for s in range(2):
                    hot = wk[:, s * D:(s + 1) * D].rearrange("p (h k j) -> p h k j", h=PH, k=TOPK)
                    v.tensor_tensor(hot, sel_f[:, s].rearrange("p h (k o) -> p h k o", o=1).to_broadcast([P, PH, TOPK, TOPK]),
                                    iota, ALU.is_equal)
                dve.drain()
                for s in range(2):
                    hot = wk[:, s * D:(s + 1) * D].rearrange("p (h k j) -> p h k j", h=PH, k=TOPK)
                    v.tensor_tensor(hot, hot, i1[:, :, s, :].rearrange("p h (o j) -> p h o j", o=1).to_broadcast([P, PH, TOPK, TOPK]), ALU.mult)
                dve.drain()
                for s in range(2):
                    v.reduce_sum(sel_f[:, s], wk[:, s * D:(s + 1) * D].rearrange("p (h k j) -> p h k j", h=PH, k=TOPK), AX.X)
                dve.drain()
                v.scalar_tensor_tensor(ex_f, sel_f[:, 0], float(NK), sel_f[:, 1], ALU.mult, ALU.add)
                dve.drain()
                v.tensor_copy(experts[:, bass.ds(t * SLOTS, SLOTS)].rearrange("p (h k) -> p h k", h=PH), ex_f)
                v.tensor_scalar(at_dot[:, bass.ds(t * SLOTS, SLOTS)].rearrange("p (h k) -> p h k", h=PH), ex_f, float(TD),
                                cn["token"][:, bass.ds(t, 1)], ALU.mult, ALU.add)
                dve.drain()
            dve.drain().then_inc(smx_in, 1)
            dve.wait_ge(smx_ok, 1)
            g16 = gates[:, :].rearrange("p (h k) -> p h k", k=TOPK)
            v.reduce_sum(gsum[:, :], g16, AX.X)
            dve.drain()
            v.reciprocal(gsum[:, :], gsum[:, :])
            dve.drain()
            v.tensor_tensor(g16, g16, gsum[:, :].rearrange("p (h o) -> p h o", o=1).to_broadcast([P, NT * PH, TOPK]), ALU.mult)
            dve.drain()
            c0 = QT * SLOTS
            for g in range(1, 4):
                v.tensor_copy(experts[32 * g:32 * g + 32, c0:c0 + 32], experts[0:TS, c0 + 32 * g:c0 + 32 * g + 32])
                v.tensor_copy(gates[32 * g:32 * g + 32, c0:c0 + 32], gates[0:TS, c0 + 32 * g:c0 + 32 * g + 32])
            dve.drain().then_inc(route_ok, 1)

            def dot_products(n, t, q0, trips, off):
                dve.wait_ge(ht_ok, n + 1)
                with dve.Fori(q0, q0 + trips) as i:
                    for e in range(FB):
                        r, lap = e % GR, e // GR
                        dve.wait_ge(g_in[r], 32 * i + 16 * (lap + 1))
                        v.tensor_tensor_reduce(out=vring[:, r, :], in0=vring[:, r, :], in1=h2_tok[n], scale=1.0, scalar=0.0,
                                               op0=ALU.mult, op1=ALU.add, accum_out=dots[:, e:e + 1]).then_inc(g_used[r], 1)
                    dve.drain()
                    v.tensor_copy(wts[:, bass.ds(FB * (i + off), FB)], dots[:, :])
                    dve.drain()
                dve.drain().then_inc(dot_ok, 1)

            def weights(n, t):
                dve.wait_ge(gelu_ok, n + 1)
                c0, w = t * SLOTS, (SLOTS if t < QT else TS)
                v.tensor_tensor(wts[:, c0:c0 + w], wts[:, c0:c0 + w], gates[:, c0:c0 + w], ALU.mult)
                dve.drain()

            def values(n, q0, trips, off):
                acc = accs[n % 2]
                if n >= 2:
                    dve.wait_ge(y_out[n % 2], 16 * (n // 2))
                v.memset(acc, 0.0)
                dve.drain()
                with dve.Fori(q0, q0 + trips) as i:
                    for e in range(FB):
                        r, lap = e % GR, e // GR
                        dve.wait_ge(g_in[r], 32 * i + 16 * (lap + 1))
                        v.scalar_tensor_tensor(acc, vring[:, r, :], wts[:, bass.ds(FB * (i + off) + e, 1)], acc, ALU.mult, ALU.add)
                        dve.drain().then_inc(g_used[r], 1)

            def finish(n, t):
                m = rows(t)
                y = accs[n % 2]
                dve.wait_ge(x2t_ps, n + 1)
                if t == QT:
                    dve.drain().then_inc(acc_ok, 1)
                    dve.wait_ge(sum_ps, 1)
                    dve.wait_ge(g2_ok, 2)
                    for c in range(4):
                        cc = slice(c * 512, (c + 1) * 512)
                        v.tensor_tensor(y[0:m, cc], pb[c][0:m, :], g2b[0:m, cc], ALU.mult)
                else:
                    v.tensor_tensor(y[0:m, :], y[0:m, :], g2b[0:m, :], ALU.mult)
                dve.drain()
                for c in range(4):
                    cc = slice(c * 512, (c + 1) * 512)
                    v.tensor_tensor(y[0:m, cc], y[0:m, cc], pb[4 + c][0:m, :], ALU.add)
                dve.drain().then_inc(acc_free, 1)
                dve.drain().then_inc(y_pre, 1)
                dve.wait_ge(y_ss, n + 1)
                st = stat[0:m, 1, t:t + 1]
                v.tensor_scalar(st, stat[0:m, 0, t:t + 1], 1.0 / D, EPS, ALU.mult, ALU.add)
                dve.drain()
                v.reciprocal(st, st)
                dve.drain().then_inc(y_rs, 1)
                dve.wait_ge(y_rs2, n + 1)
                v.scalar_tensor_tensor(y[0:m, :], y[0:m, :], st, fgb[0:m, :], ALU.mult, ALU.mult).then_inc(y_ok, 1)

            dot_products(0, QT - 1, 0, TRIP, (QT - 1) * TRIP)
            weights(0, QT - 1)
            dot_products(1, QT, TRIP, TRIP_S, (QT - 1) * TRIP)
            weights(1, QT)
            q = TRIP + TRIP_S
            values(0, q, TRIP, (QT - 1) * TRIP - q)
            finish(0, QT - 1)
            for n in range(1, 1 + DN):
                q += TRIP
                weights(1 + n, n - 1)
                values(n, q, TRIP, (n - 1) * TRIP - q)
                finish(n, n - 1)
            q += TRIP
            values(NT - 1, q, TRIP_S, QT * TRIP - q)
            finish(NT - 1, QT)

        @block.gpsimd
        def _(pool):
            g = nc.gpsimd
            for s in w_used + mg_free + g_used + a_free + ss_free + [sc_ok, col_ps, col_ok]:
                pool.sem_inc(s, 1)
            pool.wait_ge(lat_ok, NT)
            pool.dma_start(lat_p[0, 0].rearrange("(t p) c -> p t c", p=P), lat_tok[:, 0:QT, :]).then_inc(lat_out, 16)
            pool.dma_start(lat_s[0, 0], lat_tok[0:TS, QT, :]).then_inc(lat_out, 16)
            pool.wait_ge(logf_ok, 1)
            pool.dma_start(lf_p[0, 0].rearrange("(t p) h -> p t h", p=P), logf[:, 0:QT, :]).then_inc(out_s, 16)
            pool.dma_start(lf_s[0, 0], logf[0:TS, QT, :]).then_inc(out_s, 16)
            pool.wait_ge(frow_ok, 1)
            pool.dma_start(aug_q_dram[:, 0, :], frow[:, 0, 0:T]).then_inc(aug_st, 16)
            pool.dma_start(aug_k_dram[:, 1, :], frow[:, 1, :]).then_inc(aug_st, 16)
            pool.dma_start(aug_q_dram[:, 1, :], aug_ones[:, 0:T]).then_inc(aug_st, 16)
            pool.dma_start(aug_k_dram[:, 0, :], aug_ones).then_inc(aug_st, 16)
            pool.wait_ge(krt_ok, 1)
            pool.dma_start(kr_p[0, 0].rearrange("(t p) d -> p t d", p=P), ktok[:, 0:QT, 0:ROPE]).then_inc(out_s, 16)
            pool.dma_start(kr_s[0, 0], ktok[0:TS, QT, 0:ROPE]).then_inc(out_s, 16)

            def head_values(gh, h):
                pool.wait_ge(pv_ok, gh)
                for t in range(6):
                    m = rows(t) if t < 5 else P
                    g.tensor_copy(vh[0:m, t, :], v_tok[0:m, t, bass.ds(h * HD, HD)])
                pool.drain().then_inc(vh_ok, 1)

            pool.wait_ge(tokm_ev, 12)
            head_values(0, 0)
            with pool.Fori(1, NH) as i:
                head_values(i, i)
            pool.wait_ge(s_ok, NH)
            pool.dma_start(kf_past, kf_cache).then_inc(kfp_in, 16)
            pool.dma_start(v_tok[:, 5, :], vf_cache).then_inc(vfp_in, 16)
            pool.wait_ge(tokm_ev, 12 + 2 * NT)
            pool.dma_start(vf_p[0, 0].rearrange("(t p) h d -> p t (h d)", p=P), v_tok[:, 0:QT, :]).then_inc(v_out, 16)
            pool.dma_start(vf_s[0, 0].rearrange("s h d -> s (h d)"), v_tok[0:TS, QT, :]).then_inc(v_out, 16)
            pool.wait_ge(vfp_in, 16)
            pool.wait_ge(aug_st, 64)
            kfp_o = kf_p[0, 0].rearrange("(t p) h d -> p t h d", p=P)
            with pool.Fori(0, NH) as i:
                pool.wait_ge(s_ok, NH + i)
                pool.sem_inc(pool_on, 1)
                pool.dma_start(aug_q, aug_q_dram[bass.ds(i, 1)].rearrange("o r t -> (o r) t")).then_inc(aug_in, 16)
                pool.dma_start(aug_k, aug_k_dram[bass.ds(i, 1)].rearrange("o r t -> (o r) t")).then_inc(aug_in, 16)
                head_values(NH + i, i)
                pool.wait_ge(kt_ok, i + 1)
                pool.sem_inc(pool_on, 1)
                pool.dma_start(kfp_o[:, :, bass.ds(i, 1), :].rearrange("p t o d -> p t (o d)"), ktok[:, 0:QT, :]).then_inc(kt_out, 16)
                pool.dma_start(kf_s[0, 0, :, bass.ds(i, 1), :].rearrange("s o d -> s (o d)"), ktok[0:TS, QT, :]).then_inc(kt_out, 16)

            pool.wait_ge(route_ok, 1)

            def rows_of(table, q, off):
                for lap in range(2):
                    idx = idx8[:, lap, :]
                    g.tensor_copy(idx, experts[:, bass.ds(FB * (q + off) + GR * lap, GR)]).then_inc(idx_ok[0], 1)
                    pool.wait_ge(idx_ok[0], 2 * q + lap + 1)
                    for r in range(GR):
                        pool.wait_ge(g_used[r], 2 * q + lap + 1)
                        pool.sem_inc(pool_on, 1)
                        g.indirect_dma_start(out=vring[:, r, :], out_offset=None, in_=table,
                                             in_offset=bass.IndirectOffsetOnAxis(ap=idx[:, r:r + 1], axis=0)).then_inc(g_in[r], 16)

            def dots_of(i):
                for lap in range(2):
                    idx = idx8[:, 2 + lap, :]
                    pool.wait_ge(ss_free[lap], i + 1)
                    pool.sem_inc(pool_on, 1)
                    g.tensor_copy(idx, at_dot[:, bass.ds(FB * i + GR * lap, GR)]).then_inc(idx_ok[1], 1)
                    pool.wait_ge(idx_ok[1], 2 * i + lap + 1)
                    pool.sem_inc(pool_on, 1)
                    for r in range(GR):
                        g.indirect_dma_start(out=got[:, lap, r:r + 1], out_offset=None, in_=dots_dram.rearrange("e (t o) -> (e t) o", o=1),
                                             in_offset=bass.IndirectOffsetOnAxis(ap=idx[:, r:r + 1], axis=0)).then_inc(ss_in[lap], 16)

            c_late = (QT - 1) * TRIP
            with pool.Fori(0, TRIP + TRIP_S) as q:
                rows_of(peer_u, q, c_late)
            q0 = TRIP + TRIP_S
            with pool.Fori(q0, q0 + TRIP) as q:
                rows_of(peer_v, q, c_late - q0)
            for j in range(2):
                pool.wait_ge(a_st[j], 16 * NK // 2)
            with pool.Fori(0, TRIP) as i:
                dots_of(i)
            q0 += TRIP
            with pool.Fori(0, (DN - 1) * TRIP) as i:
                rows_of(peer_v, i + q0, -q0)
                dots_of(i + TRIP)
            with pool.Fori((DN - 1) * TRIP, DN * TRIP) as i:
                rows_of(peer_v, i + q0, -q0)
            q0 += DN * TRIP
            with pool.Fori(q0, q0 + TRIP_S) as q:
                rows_of(peer_v, q, QT * TRIP - q0)
            pool.wait_ge(out_s, 64)
            pool.wait_ge(v_out, 32)
            pool.wait_ge(kt_out, 32 * NH)
            pool.wait_ge(lat_out, 32)


def kernel(**inp):
    import concourse.bacc as bacc
    from concourse.bass_utils import run_bass_kernel_spmd

    x = {k: np.ascontiguousarray(v) for k, v in inp.items()}

    def feat(a):
        return np.ascontiguousarray(a.T.reshape(-1, P, a.shape[0]).transpose(1, 0, 2))

    def cols(v):
        return np.ascontiguousarray(v.reshape(-1, P).T)

    def block(w):
        return w.reshape(-1, P, w.shape[1]).transpose(1, 0, 2).reshape(P, -1)

    def pad(*parts):
        b = np.zeros((P, D), np.float32)
        at = 0
        for p_ in parts:
            b[:, at:at + p_.shape[1]] = p_
            at += p_.shape[1]
        return b

    w_in, w_ada, ukv = x["w_in"][0], x["w_ada"][0], x["w_ukv"][0]
    q_w = HD + ROPE
    o_lat = NH * q_w
    o_kr = o_lat + LORA
    o_fox = o_kr + ROPE
    o_f = o_fox + 3 * NH * HD
    o_gm = o_f + NH
    o_gf = o_gm + D

    def ada(n):
        return block(w_ada[:, n * P:(n + 1) * P])

    stream = np.empty((NB, P, D), np.float32)
    n = [0]

    def put(b):
        stream[n[0]] = b
        n[0] += 1

    for j in range(ADA_A):
        put(ada(j))
    for c in range(CKV):
        put(block(w_in[c * 512:(c + 1) * 512, o_lat:o_kr]))
    put(pad(block(w_in[:, o_kr:o_fox]), block(w_in[:, o_f:o_gm])))
    ukv_h = ukv.reshape(LORA, NH, 2, HD)
    for c in range(MLAV):
        put(block(ukv_h[:, 4 * c:4 * c + 4, 1].reshape(LORA, 512)))
    for h in range(NH):
        put(ada(2 * KC + 2 * h))
        put(ada(2 * KC + 2 * h + 1))
        put(block(w_in[:, h * q_w:h * q_w + HD]))
        put(pad(block(w_in[:, h * q_w + HD:(h + 1) * q_w]), block(ukv_h[:, h, 0])))
    for c in range(2):
        for r in range(4):
            a = o_fox + 2 * NH * HD + c * 512
            put(block(w_in[r * 512:(r + 1) * 512, a:a + 512]))
    for h in range(NH):
        put(ada(3 * KC + 2 * h))
        put(ada(3 * KC + 2 * h + 1))
        put(block(w_in[:, o_fox + h * HD:o_fox + (h + 1) * HD]))
        put(block(w_in[:, o_fox + (NH + h) * HD:o_fox + (NH + h + 1) * HD]))
    for j in range(KC):
        c = slice(j * P, (j + 1) * P)
        put(block(w_in[:, o_gm + j * P:o_gm + (j + 1) * P]))
        put(block(w_in[:, o_gf + j * P:o_gf + (j + 1) * P]))
        put(pad(block(x["w_o_mla"][0][:, c]), block(x["w_o_fox"][0][:, c])))
        put(ada(4 * KC + j))
    for j in range(KC // 2):
        for q in range(2):
            put(ada(5 * KC + 2 * j + q))
        for q in range(2):
            put(block(x["w_out"][0][:, (2 * j + q) * P:(2 * j + q + 1) * P]))
    for j in range(KC):
        put(block(x["peer_wq"][0][:, j * P:(j + 1) * P]))
    for j in range(NK * NK // P):
        put(block(x["peer_u"][0][j * P:(j + 1) * P].T))
    assert n[0] == NB

    lay, cw = const_layout()
    cst = np.zeros((P, cw), np.float32)

    def const(name, a):
        cst[:a.shape[0], lay[name][0]:lay[name][0] + a.shape[1]] = a

    i = np.arange(P)
    const("ident", np.eye(P, dtype=np.float32))
    const("stack", (i[:, None] % TS == i[None, :]).astype(np.float32))
    const("band", (i[:, None] <= np.arange(TP)[None, :]).astype(np.float32))
    const("mask_mla", np.where(i[:, None] // CHUNK >= i[None, :] // CHUNK, 0.0, NEG).astype(np.float32))
    const("mask_fox", np.where(i[:, None] >= i[None, :], 0.0, NEG).astype(np.float32))
    const("iota", np.broadcast_to(np.arange(TOPK, dtype=np.float32), (P, TOPK)))
    const("ones", np.ones((P, P), np.float32))
    const("token", (np.arange(NT)[None, :] * P + i[:, None]).astype(np.float32))
    inv = (1.0 / (np.float32(10000.0) ** (np.arange(0, ROPE, 2, dtype=np.float32) / ROPE))).astype(np.float32)
    pos = np.concatenate([np.arange(TP), PAST + np.arange(TS)]).astype(np.float32)
    ang = (inv[:, None] * pos[None, :]).astype(np.float32)
    const("cos", np.concatenate([np.cos(ang), np.cos(ang)]))
    const("sin", np.concatenate([-np.sin(ang), np.sin(ang)]))

    arrays = {
        "wstream": stream,
        "x_t": feat(np.concatenate([x["x_prompt"][0], x["x_sample"][0]])),
        "c_t": feat(np.concatenate([x["c_prompt"], x["c_sample"]])),
        "b_ada": cols(x["b_ada"][0]),
        "g1": cols(x["norm1_g"][0]),
        "g2": cols(x["norm2_g"][0]),
        "kvg": x["kv_norm_g"],
        "final_g": x["final_g"][None],
        "fbias": x["fox_fbias"],
        "lat_cache": feat(x["cache_mla_latent"][0, 0]),
        "kr_cache": np.ascontiguousarray(x["cache_mla_krope"][0, 0].T),
        "kf_cache": np.ascontiguousarray(x["cache_fox_k"][0, 0].transpose(2, 1, 0)),
        "vf_cache": x["cache_fox_v"][0, 0].reshape(PAST, NH * HD),
        "logf_cache": x["cache_fox_logf"][0, 0],
        "keys": np.ascontiguousarray(np.stack([x["peer_keys1"][0].T, x["peer_keys2"][0].T], 1)),
        "peer_u": x["peer_u"][0],
        "peer_v": x["peer_v"][0],
        "aug_ones": np.ones((NH, NKEY), np.float32),
        "consts": cst,
    }
    shapes = [(1, TP, D), (1, TS, D)]
    for s in (TP, TS):
        shapes += [(1, 1, s, LORA), (1, 1, s, ROPE), (1, 1, s, NH, HD), (1, 1, s, NH, HD), (1, 1, s, NH)]
    f32 = mybir.dt.float32
    nc = bacc.Bacc("TRN2", target_bir_lowering=False, num_devices=1)
    args = {k: nc.dram_tensor(k, a.shape, f32, kind="ExternalInput").ap() for k, a in arrays.items()}
    outs = [nc.dram_tensor(f"out{j}", s, f32, kind="ExternalOutput").ap() for j, s in enumerate(shapes)]
    build(nc, outs=outs, **args)
    r = run_bass_kernel_spmd(nc, [arrays], core_ids=[0])
    return tuple(r.results[0][f"out{j}"] for j in range(len(shapes)))
```

```python
import numpy as np
import concourse.bass as bass
from concourse import mybir
from contextlib import ExitStack

D, TP, TS, PAST = 2048, 512, 32, 128
T = TP + TS
P = 128
KC = D // P
NH, HD, ROPE, LORA = 8, 128, 64, 512
NKEY = T + PAST
QT = TP // P
NT = QT + 1
HALF = T // 2
KHALF = NKEY // 2
CHUNK = 64
EPS = 1e-6
NEG = -1e30
SC_MLA = float(HD + ROPE) ** -0.5
SC_FOX = float(HD) ** -0.5
PH, NK, TOPK = 8, 128, 16
SLOTS = PH * TOPK
RING = 4
FB = 8
GR = 4

N_MOD = 6 * KC
ADA_A = 2 * KC
CKV, KRF, FOXV, MLAV = 4, 1, 8, 2
B_CKV = ADA_A
B_KRF = B_CKV + CKV
B_MLAV = B_KRF + KRF
B_MLA = B_MLAV + MLAV
B_FOXV = B_MLA + 4 * NH
B_FOX = B_FOXV + FOXV
B_MERGE = B_FOX + 4 * NH
B_OUT = B_MERGE + 4 * KC
B_WQ = B_OUT + 2 * KC
B_UT = B_WQ + KC
DN = 3
TD = DN * P
NB = B_UT + NK * NK // P

S_AT = [(2, 0), (3, 0), (2, 128), (4, 0), (3, 256)]
S_W = [128 * (t + 1) for t in range(QT)] + [TS + PAST]
P_AT = [0, 128, 384, 768, 1280]
P_W = P_AT[-1] + S_W[-1]
PT_AT = [0, 512, 896, 1152]
PT_S = 1280
PT_W = PT_S + 2 * TS


def rows(t):
    return P if t < QT else TS


def const_layout():
    names = [("ident", P), ("stack", P), ("band", TP), ("mask_mla", P), ("mask_fox", P), ("iota", TOPK),
             ("cos", T), ("sin", T), ("ones", P), ("token", NT)]
    at, out = 0, {}
    for n, w in names:
        out[n] = (at, w)
        at += w
    return out, at


def build(nc, wstream, x_t, c_t, c_rows, b_ada, g1, g2, kvg, final_g, fbias, lat_cache, kr_cache, kf_cache, vf_cache,
          logf_cache, keys, peer_u, peer_v, aug_ones, consts, outs):
    F32, U32 = mybir.dt.float32, mybir.dt.uint32
    ACT, ALU, AX = mybir.ActivationFunctionType, mybir.AluOpType, mybir.AxisListType
    (y_p, y_s, lat_p, kr_p, kf_p, vf_p, lf_p, lat_s, kr_s, kf_s, vf_s, lf_s) = outs
    clay, cw = const_layout()
    aug_q_dram = nc.dram_tensor("aug_q", (NH, 2, T), F32).ap()
    dots_dram = nc.dram_tensor("dots_dram", (NK * NK, TD), F32).ap()
    aug_k_dram = nc.dram_tensor("aug_k", (NH, 2, NKEY), F32).ap()

    with ExitStack() as ctx:
        def sb(name, shape, dt=F32):
            return ctx.enter_context(nc.sbuf_tensor(name, shape, dt))

        def sem(name):
            return ctx.enter_context(nc.semaphore(name))

        ring = sb("ring", [P, RING, D])
        hreg = sb("hreg", [P, KC, T])
        oreg = sb("oreg", [P, KC, T])
        CW_A = 6 * NH * HD
        offs = {}
        at = 0
        for n, w in [("v", CW_A), ("latT", 4 * NKEY), ("qn", T), ("qr", T), ("kn", NKEY), ("rope_x", NKEY),
                     ("vh", 6 * HD), ("prob", P_W), ("probT", PT_W), ("ktok", NT * HD)]:
            offs[n] = at
            at += w
        arena_w = 8 * D
        assert at <= arena_w
        arena = sb("arena", [P, arena_w])

        def area(name, w, p=P):
            return arena[0:p, offs[name]:offs[name] + w]

        v_tok = area("v", CW_A).rearrange("p (t c) -> p t c", t=6)
        lat_tok = arena[:, 0:NT * LORA].rearrange("p (t c) -> p t c", t=NT)
        latT = area("latT", 4 * NKEY).rearrange("p (k t) -> p k t", k=4)
        kf_past = area("latT", NH * PAST).rearrange("p (h t) -> p h t", h=NH)
        qn = area("qn", T)
        qr = area("qr", T, ROPE)
        kn = area("kn", NKEY)
        rope_x = area("rope_x", HALF, ROPE)
        rope_r = arena[0:ROPE, offs["rope_x"] + HALF:offs["rope_x"] + 2 * HALF]
        aug_q = area("qr", T, 2)
        aug_k = area("rope_x", NKEY, 2)
        vh = area("vh", 6 * HD).rearrange("p (t d) -> p t d", t=6)
        prob = area("prob", P_W)
        probT = area("probT", PT_W)
        ktok = area("ktok", NT * HD).rearrange("p (t d) -> p t d", t=NT)
        merged = arena[:, 0:KC * T].rearrange("p (k t) -> p k t", k=KC)
        sg = arena[:, KC * T:KC * T + 4 * HALF].rearrange("p (n t) -> p n t", n=4)
        vring = arena[:, 0:GR * D].rearrange("p (r n) -> p r n", r=GR)
        g2b = arena[:, 4 * D:5 * D]
        h2_tok = [arena[:, 5 * D:6 * D], arena[:, 6 * D:7 * D]]
        ACC = [0, 2, 1, 0, 1]
        accs = [arena[:, (7 - j) * D:(8 - j) * D] for j in ACC]
        h_flat = hreg.rearrange("p k t -> p (k t)")
        sq_junk = h_flat[:, 0:D]
        g2b_s = h_flat[:, D:2 * D]
        deep = [vring[:, r, :] for r in range(GR)] + [ring[:, r, :] for r in range(RING)]
        roff = [0]

        def route(w, pat, dt=None, **kw):
            x = arena[:, roff[0]:roff[0] + w]
            roff[0] += w
            assert roff[0] <= GR * D
            return (x if dt is None else x.bitcast(dt)).rearrange(pat, **kw)

        NL, NC = 2 * NT, TOPK * TOPK
        qn_peer = route(T, "p t -> p t")
        s_head = route(2 * NL * NK, "p (b t s n) -> p b t s n", b=2, t=NT, s=2)
        s_rest = route(NL * NK, "p (t s n) -> p t s n", t=NT, s=2)
        cand = route(NT * NC, "p (t n) -> p t n", t=NT)
        top_v = route(NL * TOPK, "p (t s k) -> p t s k", t=NT, s=2)
        top_i = route(NL * TOPK, "p (t s k) -> p t s k", U32, t=NT, s=2)
        top_if = route(NL * TOPK, "p (t s k) -> p t s k", t=NT, s=2)
        sel_f = route(2 * NT * TOPK, "p (s t k) -> p s t k", s=2, t=NT)
        sc_v = route(NT * TOPK, "p (t k) -> p t k", t=NT)
        ex_f = route(NT * TOPK, "p (t k) -> p t k", t=NT)
        sel = route(NT * TOPK, "p (t k) -> p t k", U32, t=NT)
        sel_a = route(NT * TOPK, "p (t k) -> p t k", U32, t=NT)
        sel_b = route(NT * TOPK, "p (t k) -> p t k", U32, t=NT)
        cand_rest = s_rest.rearrange("p t s n -> p t (s n)")
        hots = [cand.rearrange("p t (k j) -> p t k j", k=TOPK), cand_rest.rearrange("p t (k j) -> p t k j", k=TOPK)]
        late = sb("late", [P, 2 * D])
        crow = late.rearrange("p (g n) -> p g n", g=2)
        fgb = late[:, 0:D]

        krT = sb("krT", [ROPE, NKEY])
        cst = sb("cst", [P, cw])
        cn = {n: cst[:, a:a + w] for n, (a, w) in clay.items()}
        ident = cn["ident"]
        kvgb = sb("kvgb", [P, LORA])
        keyT = sb("keyT", [P, 2, NK])
        cT = sb("cT", [P, KC, 2])
        bad = sb("bad", [P, N_MOD])
        g1T = sb("g1T", [P, KC])
        g2T = sb("g2T", [P, KC])
        mod = sb("mod", [P, N_MOD, 2])
        cf = sb("cf", [P, KC, 2])
        rstd = sb("rstd", [P, T])
        stat = sb("stat", [P, 4, NT])
        fb = sb("fb", [P, NH])
        fw = sb("fw", [P, 6, NT * NH])
        logf = sb("logf", [P, 6, NH])
        fT = area("prob", T, NH)
        frow = area("probT", 2 * NKEY, NH).rearrange("p (r t) -> p r t", r=2)
        mrow = sb("mrow", [2, 4, P])
        dots = sb("dots", [P, FB])
        idx8 = sb("idx8", [P, 4, GR], U32)
        got = sb("got", [P, 2, GR])
        stage = sb("stage", [P, 2, TD])
        prod = stage.rearrange("p a b -> p (a b)")[:, 0:512]
        part = sb("part", [P, 2, 4])
        msum = sb("msum", [P, 2, 2])
        NS = TP * SLOTS // P + TS * SLOTS // P
        SL = NT * SLOTS
        experts = late[:, D:D + SL].bitcast(U32)
        at_dot = late[:, D + SL:D + 2 * SL].bitcast(U32)
        gates = late[:, D + 2 * SL:D + 3 * SL]
        gsum = sb("gsum", [P, NT * PH])
        wts = sb("wts", [P, NS])
        pb = [ctx.enter_context(nc.psum_tensor(f"pb{i}", [P, 512], F32)) for i in range(8)]

        w_in = [sem(f"w_in{r}") for r in range(RING)]
        w_used = [sem(f"w_used{r}") for r in range(RING)]
        small_in = sem("small_in")
        c_in, cst_in, bada_in = sem("c_in"), sem("cst_in"), sem("bada_in")
        crow_in, crow_ok, fg_in = sem("crow_in"), sem("crow_ok"), sem("fg_in")
        x_in = [sem(f"x_in{k}") for k in range(4)]
        x_in2 = [sem(f"x_in2_{j}") for j in range(2)]
        cache_in = sem("cache_in")
        kfp_in = sem("kfp_in")
        vfp_in = sem("vfp_in")
        out_s = sem("out_s")
        sq_ok, ssq_ok, var_ok, rstd_ok = sem("sq_ok"), sem("ssq_ok"), sem("var_ok"), sem("rstd_ok")
        silu_ok = sem("silu_ok")
        ada_ok, row_ok, col_ps, col_ok = sem("ada_ok"), sem("row_ok"), sem("col_ps"), sem("col_ok")
        cf_ok, hn_ok, h_ok = sem("cf_ok"), sem("hn_ok"), sem("h_ok")
        tokm = sem("tokm")
        tokm_ev = sem("tokm_ev")
        lat_ss, lat_rs, lat_ok = sem("lat_ss"), sem("lat_rs"), sem("lat_ok")
        latT_ps, latT_ok = sem("latT_ps"), sem("latT_ok")
        lat_out = sem("lat_out")
        v_out = sem("v_out")
        f_in, f_ps, f_z, f_l, logf_ok, cum_ps, frow_ok, aug_st = (sem("f_in"), sem("f_ps"), sem("f_z"), sem("f_l"), sem("logf_ok"),
                                                            sem("cum_ps"), sem("frow_ok"), sem("aug_st"))
        proj = sem("proj")
        proj_free = [sem(f"proj_free{b}") for b in range(2)]
        rope_in, rope_ok = sem("rope_in"), sem("rope_ok")
        krt_ps, krt_ok = sem("krt_ps"), sem("krt_ok")
        s_ok, mx_ok, exp_ok, prob_ok = sem("s_ok"), sem("mx_ok"), sem("exp_ok"), sem("prob_ok")
        pt_ps, pt_ok, pv_ok, o_ok, vh_ok = sem("pt_ps"), sem("pt_ok"), sem("pv_ok"), sem("o_ok"), sem("vh_ok")
        aug_in, kt_ps, kt_ok, kt_out = sem("aug_in"), sem("kt_ps"), sem("kt_ok"), sem("kt_out")
        mg_ps, sig_ok = sem("mg_ps"), sem("sig_ok")
        mg_free = [sem(f"mg_free{b}") for b in range(2)]
        q_ok, sc_ps, sc_ok = sem("q_ok"), sem("sc_ps"), sem("sc_ok")
        rt_used = sem("rt_used")
        smx_in, smx_ok, route_ok = sem("smx_in"), sem("smx_ok"), sem("route_ok")
        g_in = [sem(f"g_in{r}") for r in range(FB)]
        g_used = [sem(f"g_used{r}") for r in range(FB)]
        a_ps = sem("a_ps")
        a_free = [sem(f"a_free{j}") for j in range(4)]
        a_st = [sem(f"a_st{j}") for j in range(2)]
        ss_in = [sem(f"ss_in{j}") for j in range(2)]
        ss_free = [sem(f"ss_free{j}") for j in range(2)]
        idx_ok = [sem("idx_row_ok"), sem("idx_dot_ok")]
        s_clear = sem("s_clear")
        pool_on, dve_on = sem("pool_on"), sem("dve_on")
        ht_ps, ht_ok = sem("ht_ps"), sem("ht_ok")
        dot_ok, gelu_ok = sem("dot_ok"), sem("gelu_ok")
        g2_ps, g2_ok, sum_ps = sem("g2_ps"), sem("g2_ok"), sem("sum_ps")
        acc_ok, acc_free, x2t_ps, y_pre, y_ss, y_rs, y_ok, y_out, y_rs2 = (
            sem("acc_ok"), sem("acc_free"), sem("x2t_ps"), sem("y_pre"), sem("y_ss"), sem("y_rs"), sem("y_ok"), [sem(f"y_out{j}") for j in range(3)], sem("y_rs2"))
        block = ctx.enter_context(nc.Block())

        UB_MLA = 2
        UB_FOX = UB_MLA + 6 * NH
        UB_OUT = UB_FOX + 4 * NH
        UB_WQ = UB_OUT + 2 * KC
        NSMALL = 7
        A_PARTS = ((0, ADA_A // 4 - 2), (ADA_A // 4 - 2, ADA_A // 4))

        def later(i):
            return not isinstance(i, int) or i > 0

        ORDER = [QT - 1, QT] + list(range(DN))
        D0, D1 = 2, 16
        AHEAD = 1
        TRIP, TRIP_S = SLOTS // FB, TS * SLOTS // P // FB
        SHALLOW = 2 * (TRIP + TRIP_S)

        def landed_deep(r, i):
            return 16 * i + (32 * SHALLOW if r < GR else 0) + 16

        def free_deep(r, i):
            return i + (2 * SHALLOW if r < GR else 0) + 1

        @block.sync
        def _(sp):
            with sp.Fori(0, NB // RING) as i:
                for r in range(RING):
                    sp.wait_ge(w_used[r], i + 1)
                    sp.dma_start(ring[:, r, :], wstream[i * RING + r]).then_inc(w_in[r], 16)
            for b in range(NB // RING * RING, NB):
                sp.wait_ge(w_used[b % RING], b // RING + 1)
                sp.dma_start(ring[:, b % RING, :], wstream[b]).then_inc(w_in[b % RING], 16)

        @block.tensor
        def _(pe):
            def mm(out, lhsT, rhs, start=True, stop=True):
                return nc.tensor.matmul(out, lhsT, rhs, start=start, stop=stop)

            def tr(out, in_):
                p = in_.shape[0]
                return nc.tensor.transpose(out, in_, ident[0:p, 0:p])

            def blk(base, j, i=0, per=4):
                b = base + j
                pe.wait_ge(w_in[b % RING], 16 * (b // RING + 1) + 16 * (per // RING) * i)
                return b % RING

            def used(ins, slot):
                ins.then_inc(w_used[slot], 1)

            def ada_row(base, j, i, ps):
                s = blk(base, j, i)
                for k in range(KC):
                    last = mm(ps, cT[:, k, :], ring[:, s, k * P:(k + 1) * P], k == 0, k == KC - 1)
                last.then_inc(ada_ok, 1)
                pe.drain().then_inc(w_used[s], 1)

            def ada_cols(n, blocks, batch, ps):
                pe.wait_ge(row_ok, blocks)
                pe.wait_ge(col_ok, batch)
                for j in range(n):
                    last = mm(ps[:, 2 * j:2 * j + 2], mrow[:, j, :], ident[0:2, 0:2])
                last.then_inc(col_ps, 1)

            def sumsq():
                for hf in range(2):
                    mm(pb[hf][:, 0:HALF], cn["ones"], rstd[:, hf * HALF:(hf + 1) * HALF]).then_inc(ssq_ok, 1)

            pe.wait_ge(silu_ok, 1)
            for t0, t1 in A_PARTS:
                with pe.Fori(t0, t1) as i:
                    for j in range(4):
                        ada_row(0, j, i, pb[2 + j][0:2, 0:P])
                    pe.wait_ge(cst_in, 16)
                    ada_cols(4, 4 * i + 4, i + 1, pb[6])
                if t0 == 0:
                    pe.wait_ge(sq_ok, 1)
                    sumsq()

            def token_major(base, nblk, bank0, tiles, lhs, kper):
                for c in range(nblk):
                    s = blk(base, c)
                    for kk in range(kper):
                        k = c * kper + kk
                        if base == B_CKV:
                            pe.wait_ge(h_ok, k + 1)
                        for t in tiles:
                            m = rows(t) if t < 5 else P
                            last = mm(pb[bank0 + t][0:m, :], lhs(k, t), ring[:, s, kk * 512:(kk + 1) * 512],
                                      k == 0, k == nblk * kper - 1)
                    used(last, s)

            def h_tile(k, t):
                return hreg[:, k, t * P:t * P + rows(t)]

            token_major(B_CKV, CKV, 0, range(NT), h_tile, 4)
            pe.drain().then_inc(tokm, 1)
            s = blk(B_KRF, 0)
            kf_w = ROPE + NH
            for hf in range(2):
                for k in range(KC):
                    last = mm(pb[5 + hf][0:kf_w, 0:HALF], ring[:, s, k * kf_w:(k + 1) * kf_w],
                              hreg[:, k, hf * HALF:(hf + 1) * HALF], k == 0, k == KC - 1)
                last.then_inc(proj, 1)
            pe.drain().then_inc(w_used[s], 1)
            pe.wait_ge(f_in, 1)
            for t in range(NT):
                last = tr(pb[7][0:rows(t), t * NH:(t + 1) * NH], fT[:, t * P:t * P + rows(t)])
            last.then_inc(f_ps, 1)
            for t in range(NT):
                pe.wait_ge(lat_ok, t + 1)
                m = rows(t)
                for c in range(4):
                    last = tr(pb[t][:, c * P:c * P + m], lat_tok[0:m, t, c * P:(c + 1) * P])
                last.then_inc(latT_ps, 1)
            pe.wait_ge(logf_ok, 1)
            band = cn["band"]
            pe.wait_ge(rope_in, 2)
            for t in range(QT):
                mm(pb[5][0:NH, t * P:TP], logf[:, t, :], band[:, 0:TP - t * P], t == 0, t == QT - 1)
            mm(pb[6][0:NH, 0:PAST + TS], logf[:, 5, :], band[:, 0:PAST + TS], True, False)
            mm(pb[6][0:NH, PAST:PAST + TS], logf[0:TS, 4, :], band[0:TS, 0:TS], False, True).then_inc(cum_ps, 1)
            pe.wait_ge(latT_ok, NT)
            pe.wait_ge(cache_in, 16)
            pe.wait_ge(frow_ok, 1)

            def lat_tile(k, t):
                a = t * P if t < 5 else T
                return latT[:, k, a:a + (rows(t) if t < 5 else P)]

            for n in range(MLAV):
                if n:
                    pe.wait_ge(tokm_ev, 6)
                token_major(B_MLAV + n, 1, 0, range(6), lat_tile, 4)
                pe.drain().then_inc(tokm, 1)
            pe.wait_ge(rope_ok, 2)
            pe.wait_ge(f_z, 1)
            for t in range(NT):
                last = tr(pb[7][0:rows(t), t * ROPE:(t + 1) * ROPE], krT[:, t * P:t * P + rows(t)])
            last.then_inc(krt_ps, 1)
            pe.wait_ge(tokm_ev, 12)
            pe.wait_ge(krt_ok, 1)

            def project(s, lhs, m, src, width, unit0, i, per, ready=False):
                for hf in range(2):
                    u = unit0 + hf
                    pe.wait_ge(proj_free[hf], u // 2 + (per // 2) * i)
                    for k in range(src.shape[1]):
                        if ready and hf == 0:
                            pe.wait_ge(h_ok, KC + k + 1)
                        last = mm(pb[hf][0:m, 0:width], lhs(k), src[:, k, hf * width:(hf + 1) * width],
                                  k == 0, k == src.shape[1] - 1)
                    last.then_inc(proj, 1)
                return last

            def scores_mla(g):
                pe.wait_ge(rope_ok, 2 + 2 * (g + 1))
                pe.wait_ge(proj_free[1], UB_MLA // 2 + 3 * (g + 1))
                pe.wait_ge(proj_free[0], UB_MLA // 2 + 3 * (g + 1))
                for t in range(NT):
                    m, (b, c) = rows(t), S_AT[t]
                    q = slice(t * P, t * P + m)
                    ks = slice(0, S_W[t]) if t < QT else slice(TP, NKEY)
                    mm(pb[b][0:m, c:c + S_W[t]], qn[:, q], kn[:, ks], True, False)
                    last = mm(pb[b][0:m, c:c + S_W[t]], qr[:, q], krT[:, ks], False, True)
                last.then_inc(s_ok, 1)

            def scores_fox(g, h):
                pe.wait_ge(proj_free[1], UB_FOX // 2 + 2 * (h + 1))
                pe.wait_ge(proj_free[0], UB_FOX // 2 + 2 * (h + 1))
                pe.wait_ge(aug_in, 32 * (h + 1))
                for t in range(NT):
                    m, (b, c) = rows(t), S_AT[t]
                    q = slice(t * P, t * P + m)
                    if t < QT:
                        mm(pb[b][0:m, c:c + S_W[t]], qn[:, q], kn[:, 0:S_W[t]], True, False)
                        last = mm(pb[b][0:m, c:c + S_W[t]], aug_q[:, q], aug_k[:, 0:S_W[t]], False, True)
                    else:
                        mm(pb[b][0:m, c:c + TS], qn[:, q], kn[:, TP:T], True, False)
                        mm(pb[b][0:m, c:c + TS], aug_q[:, q], aug_k[:, TP:T], False, True)
                        mm(pb[b][0:m, c + TS:c + TS + PAST], qn[:, q], kf_past[:, h, :], True, False)
                        last = mm(pb[b][0:m, c + TS:c + TS + PAST], aug_q[:, q], aug_k[:, T:NKEY], False, True)
                last.then_inc(s_ok, 1)

            def weighted_values(g):
                pe.wait_ge(prob_ok, g + 1)
                pe.wait_ge(o_ok, g + 1)

                def pt(bank, col, kt):
                    for t in range(kt, QT):
                        last = tr(pb[bank][:, col + (t - kt) * P:col + (t - kt + 1) * P],
                                  prob[:, P_AT[t] + kt * P:P_AT[t] + (kt + 1) * P])
                    return last
                pt(5, 0, 0).then_inc(pt_ps, 1)
                pt(6, 0, 1)
                pt(6, 384, 3).then_inc(pt_ps, 1)
                pe.wait_ge(pt_ok, 3 * g + 1)
                pt(5, 0, 2)
                a = P_AT[QT]
                tr(pb[5][0:TS, 256:256 + TS], prob[0:TS, a:a + TS])
                tr(pb[5][:, 256 + TS:256 + 2 * TS], prob[0:TS, a + TS:a + TS + PAST]).then_inc(pt_ps, 1)
                pe.wait_ge(vh_ok, g + 1)
                pe.wait_ge(pt_ok, 3 * g + 3)
                for kt in range(QT):
                    mm(pb[7][:, kt * P:TP], vh[:, kt, :], probT[:, PT_AT[kt]:PT_AT[kt] + TP - kt * P],
                       kt == 0, kt == QT - 1)
                so = pb[5][:, 440:440 + TS]
                mm(so, vh[0:TS, 4, :], probT[0:TS, PT_S:PT_S + TS], True, False)
                mm(so, vh[:, 5, :], probT[:, PT_S + TS:PT_S + 2 * TS], False, True).then_inc(pv_ok, 1)

            def proj_mla(i):
                s = blk(B_MLA, 2, i)
                last = project(s, lambda k: ring[:, s, k * P:(k + 1) * P], P, hreg, HALF, UB_MLA, i, 6)
                pe.drain().then_inc(w_used[s], 1)
                s2 = blk(B_MLA, 3, i)
                project(s2, lambda k: ring[:, s2, k * ROPE:(k + 1) * ROPE], ROPE, hreg, HALF, UB_MLA + 2, i, 6)
                project(s2, lambda k: ring[:, s2, KC * ROPE + k * P:KC * ROPE + (k + 1) * P], P, latT, KHALF, UB_MLA + 4, i, 6)
                pe.drain().then_inc(w_used[s2], 1)

            proj_mla(0)
            scores_mla(0)
            with pe.Fori(1, NH) as i:
                proj_mla(i)
                weighted_values(i - 1)
                scores_mla(i)
            weighted_values(NH - 1)

            pe.wait_ge(mx_ok, NH)
            pe.wait_ge(exp_ok, NH)
            pe.wait_ge(o_ok, NH + 1)
            for n in range(2):
                if n:
                    pe.wait_ge(tokm_ev, 12 + NT)
                token_major(B_FOXV + 4 * n, 4, 0, range(NT), h_tile, 4)
                pe.drain().then_inc(tokm, 1)
            pe.wait_ge(tokm_ev, 12 + 2 * NT)
            pe.wait_ge(kfp_in, 16)

            def proj_fox(i):
                s = blk(B_FOX, 2, i)
                project(s, lambda k: ring[:, s, k * P:(k + 1) * P], P, hreg, HALF, UB_FOX, i, 4)
                pe.drain().then_inc(w_used[s], 1)
                s2 = blk(B_FOX, 3, i)
                project(s2, lambda k: ring[:, s2, k * P:(k + 1) * P], P, hreg, HALF, UB_FOX + 2, i, 4)
                pe.drain().then_inc(w_used[s2], 1)

            def keys_out(h):
                pe.wait_ge(o_ok, NH + h + 1)
                for t in range(NT):
                    m = rows(t)
                    o = pb[5][0:m, t * P:(t + 1) * P] if t < QT else pb[6][0:m, 0:P]
                    last = tr(o, kn[:, t * P:t * P + m])
                last.then_inc(kt_ps, 1)

            proj_fox(0)
            scores_fox(NH, 0)
            pe.wait_ge(pt_ok, 3 * NH)
            keys_out(0)
            with pe.Fori(1, NH) as i:
                proj_fox(i)
                pe.wait_ge(kt_ok, i)
                weighted_values(NH - 1 + i)
                scores_fox(NH + i, i)
                pe.wait_ge(pt_ok, 3 * NH + 3 * i)
                keys_out(i)
            pe.wait_ge(kt_ok, NH)
            weighted_values(2 * NH - 1)
            pe.wait_ge(exp_ok, 2 * NH)
            pe.wait_ge(o_ok, 2 * NH + 1)

            with pe.Fori(0, KC) as i:
                def unit(hf, q, s, off, src, k0, n):
                    for k in range(n):
                        last = mm(pb[4 * hf + q][:, 0:HALF], ring[:, s, off + k * P:off + (k + 1) * P],
                                  src[:, k0 + k, hf * HALF:(hf + 1) * HALF], k == 0, k == n - 1)
                    return last

                sf = blk(B_MERGE, 0, i)
                for hf in range(2):
                    pe.wait_ge(mg_free[hf], i + 1)
                    unit(hf, 1, sf, 0, hreg, 0, KC)
                pe.drain().then_inc(w_used[sf], 1)
                so = blk(B_MERGE, 2, i)
                for hf in range(2):
                    unit(hf, 2, so, 0, oreg, 0, NH)
                    unit(hf, 3, so, NH * P, oreg, NH, NH)
                pe.drain().then_inc(w_used[so], 1)
                sm = blk(B_MERGE, 3, i)
                for hf in range(2):
                    unit(hf, 0, sm, 0, hreg, 0, KC).then_inc(mg_ps, 1)
                pe.drain().then_inc(w_used[sm], 1)
            for b in range(2):
                pe.wait_ge(mg_free[b], KC + 1)
            with pe.Fori(0, KC // 2) as i:
                for j in range(2):
                    s = blk(B_OUT, 2 + j, i)
                    project(s, lambda k: ring[:, s, k * P:(k + 1) * P], P, merged, HALF, UB_OUT + 2 * j, i, 4)
                    pe.drain().then_inc(w_used[s], 1)
            pe.wait_ge(sq_ok, 2)
            for b in range(2):
                pe.wait_ge(proj_free[b], UB_WQ // 2)
            sumsq()
            pe.wait_ge(small_in, 16 * NSMALL)
            with pe.Fori(0, KC // 4) as i:
                for j in range(4):
                    s = blk(B_WQ, j, i)
                    project(s, lambda k: ring[:, s, k * P:(k + 1) * P], P, hreg, HALF, UB_WQ + 2 * j, i, 8, j == 0)
                    pe.drain().then_inc(w_used[s], 1)
                    pe.wait_ge(q_ok, 4 * i + j + 1)
                    pe.wait_ge(sc_ok, 4 * i + j + 1)
                    for t in range(NT):
                        m = rows(t)
                        o = pb[2][0:m, t * P:(t + 1) * P] if t < QT else pb[3][0:m, 0:P]
                        last = mm(o, qn_peer[:, t * P:t * P + m], keyT[:, j % 2, :])
                    last.then_inc(sc_ps, 1)

            def gate2_rows(g):
                for k in range(KC):
                    c = 4 + k // 4
                    last = mm(pb[c][:, (k % 4) * P:(k % 4 + 1) * P],
                              mod[:, 5 * KC + k, g:g + 1].to_broadcast([P, P]), ident)
                last.then_inc(g2_ps, 1)

            def tokens_of(src, t, m, s):
                for k in range(KC):
                    last = tr(pb[4 + k // 4][0:m, (k % 4) * P:(k % 4 + 1) * P], src[:, k, t * P:t * P + m])
                last.then_inc(s, 1)

            def dense(t0, t1):
                with pe.Fori(t0, t1) as i:
                    for j in range(4):
                        s = blk(B_UT, j, i)
                        pe.wait_ge(a_free[j], i + 1)
                        for k in range(KC):
                            last = mm(pb[j][:, 0:TD], ring[:, s, k * P:(k + 1) * P], hreg[:, k, 0:TD], k == 0, k == KC - 1)
                        last.then_inc(a_ps, 1)
                        pe.drain().then_inc(w_used[s], 1)

            gate2_rows(0)
            pe.wait_ge(sc_ok, KC + 1)
            dense(0, 1)
            pe.wait_ge(g2_ok, 1)
            tokens_of(hreg, QT - 1, P, ht_ps)
            dense(1, D0)
            pe.wait_ge(ht_ok, 1)
            tokens_of(hreg, QT, TS, ht_ps)
            dense(D0, D0 + 1)
            pe.wait_ge(ht_ok, 2)
            tokens_of(oreg, QT - 1, P, x2t_ps)
            dense(D0 + 1, NK // 4)
            for n, t in enumerate(ORDER):
                if n == 0:
                    continue
                if t == QT:
                    pe.wait_ge(acc_ok, 1)
                    for c in range(4):
                        pe.wait_ge(a_free[c], NK // 4 + 1)
                        last = mm(pb[c][0:TS, :], cn["stack"][:, 0:TS], accs[n][:, c * 512:(c + 1) * 512])
                    last.then_inc(sum_ps, 1)
                pe.wait_ge(acc_free, n)
                if t == QT:
                    gate2_rows(1)
                    pe.wait_ge(g2_ok, 2)
                tokens_of(oreg, t, rows(t), x2t_ps)

        @block.scalar
        def _(act):
            def a(out, in_, fn=ACT.Copy, **kw):
                return nc.scalar.activation(out, in_, fn, **kw)

            act.dma_start(cT[:, :, :], c_t).then_inc(c_in, 16)
            act.dma_start(cst[:, :], consts).then_inc(cst_in, 16)
            act.dma_start(bad[:, :], b_ada).then_inc(bada_in, 16)
            act.wait_ge(c_in, 16)
            a(cT[:, :, :], cT[:, :, :], ACT.Silu).then_inc(silu_ok, 1)

            def root(n):
                act.wait_ge(var_ok, n + 1)
                a(rstd[:, :], rstd[:, :], ACT.Sqrt).then_inc(rstd_ok, 1)

            def norm(n, scale0):
                with act.Fori(0, KC) as k:
                    act.wait_ge(hn_ok, n * KC + k + 1)
                    act.wait_ge(cf_ok, n + 1)
                    for g, cols in enumerate((slice(0, TP), slice(TP, T))):
                        last = a(hreg[:, k, cols], hreg[:, k, cols], ACT.Identity, scale=cf[:, k, g:g + 1],
                                 bias=mod[:, scale0 + k, g:g + 1])
                    last.then_inc(h_ok, 1)

            def copy_rows(n, blocks, batch, src):
                act.wait_ge(col_ps, batch)
                for j in range(n):
                    act.wait_ge(ada_ok, blocks - n + j + 1 if len(src) > 1 else blocks)
                    a(mrow[:, j, :], src[j] if len(src) > 1 else src[0][:, j * P:(j + 1) * P]).then_inc(row_ok, 1)

            def rows_trip(i):
                copy_rows(4, 4 * i + 4, i + 1, [pb[2 + j][0:2, 0:P] for j in range(4)])

            for i in range(4):
                rows_trip(i)
                act.dma_start(oreg[:, 4 * i:4 * i + 4, :], x_t[:, 4 * i:4 * i + 4, :]).then_inc(x_in[i], 16)
            for dst, src in ((g1T[:, :], g1), (g2T[:, :], g2), (kvgb[:, :], kvg.to_broadcast([P, LORA])),
                             (fb[:, :], fbias.to_broadcast([P, NH])), (keyT[:, :, :], keys), (logf[:, 5, :], logf_cache),
                             (krT[:, T:NKEY], kr_cache)):
                act.dma_start(dst, src).then_inc(small_in, 16)
            rows_trip(4)
            act.dma_start(latT[:, :, T:NKEY], lat_cache).then_inc(cache_in, 16)
            act.dma_start(late[:, :], c_rows.to_broadcast([P, 2 * D])).then_inc(crow_in, 16)
            rows_trip(5)
            root(0)
            with act.Fori(*A_PARTS[1]) as i:
                rows_trip(i)
            norm(0, 0)
            act.wait_ge(crow_in, 16)
            a(late[:, :], late[:, :], ACT.Silu).then_inc(crow_ok, 1)
            act.wait_ge(tokm, 1)
            for t in range(NT):
                m = rows(t)
                a(lat_tok[0:m, t, :], pb[t][0:m, :], ACT.Square, accum_out=stat[0:m, 0, t:t + 1])
            act.drain().then_inc(lat_ss, 1)

            def rope_copy(bank, unit, kf, u):
                act.wait_ge(proj, u)
                if later(kf):
                    act.wait_ge(rope_ok, kf)
                a(rope_x, pb[bank][0:ROPE, 0:HALF])
                a(rope_r[0:32, :], pb[bank][32:64, 0:HALF])
                a(rope_r[32:64, :], pb[bank][0:32, 0:HALF])
                return act.drain()

            for hf in range(2):
                rope_copy(5 + hf, hf, hf, hf + 1)
                a(fT[:, hf * HALF:(hf + 1) * HALF], pb[5 + hf][ROPE:ROPE + NH, 0:HALF])
                act.drain().then_inc(rope_in, 1)
            act.drain().then_inc(f_in, 1)
            act.wait_ge(lat_rs, 1)
            a(stat[:, 1, :], stat[:, 1, :], ACT.Sqrt)
            act.drain().then_inc(lat_rs, 1)
            act.wait_ge(f_z, 1)
            a(fw[:, 2, :], fw[:, 1, :], ACT.Exp, scale=-1.0)
            act.drain()
            a(fw[:, 3, :], fw[:, 2, :], ACT.Ln, bias=1.0)
            act.drain().then_inc(f_l, 1)
            for t in range(NT):
                act.wait_ge(latT_ps, t + 1)
                m = rows(t)
                a(latT[:, :, t * P:t * P + m], pb[t][:, :].rearrange("p (c t) -> p c t", c=4)[:, :, 0:m]).then_inc(latT_ok, 1)
            act.wait_ge(lat_out, 32)
            for n in range(2):
                act.wait_ge(tokm, 2 + n)
                for t in range(6):
                    m = rows(t) if t < 5 else P
                    a(v_tok[0:m, t, n * 512:(n + 1) * 512], pb[t][0:m, :]).then_inc(tokm_ev, 1)
            act.wait_ge(krt_ps, 1)
            a(ktok[:, 0:QT, 0:ROPE], pb[7][:, 0:QT * ROPE].rearrange("p (t d) -> p t d", d=ROPE))
            a(ktok[0:TS, QT, 0:ROPE], pb[7][0:TS, QT * ROPE:NT * ROPE])
            act.drain().then_inc(krt_ok, 1)
            act.sem_inc(proj_free[0], 1)
            act.sem_inc(proj_free[1], 1)

            def softmax_exp(g, scale):
                act.wait_ge(mx_ok, g + 1)
                for t in range(NT):
                    m, (b, c) = rows(t), S_AT[t]
                    a(prob[0:m, P_AT[t]:P_AT[t] + S_W[t]], pb[b][0:m, c:c + S_W[t]], ACT.Exp,
                      bias=stat[0:m, 2, t:t + 1], scale=scale, accum_out=stat[0:m, 3, t:t + 1])
                act.drain().then_inc(exp_ok, 1)

            def copy_pt(g):
                act.wait_ge(pt_ps, 3 * g + 1)
                act.wait_ge(pv_ok, g + 1)
                act.wait_ge(aug_st, 64)
                a(probT[:, 0:512], pb[5][:, :]).then_inc(pt_ok, 1)
                act.wait_ge(pt_ps, 3 * g + 2)
                a(probT[:, PT_AT[1]:PT_AT[1] + 384], pb[6][:, 0:384])
                a(probT[:, PT_AT[3]:PT_AT[3] + 128], pb[6][:, 384:512]).then_inc(pt_ok, 1)
                act.wait_ge(pt_ps, 3 * g + 3)
                a(probT[:, PT_AT[2]:PT_AT[2] + 256], pb[5][:, 0:256])
                a(probT[0:TS, PT_S:PT_S + TS], pb[5][0:TS, 256:256 + TS])
                a(probT[:, PT_S + TS:PT_S + 2 * TS], pb[5][:, 256 + TS:256 + 2 * TS]).then_inc(pt_ok, 1)

            def copy_o(g):
                act.wait_ge(pv_ok, g + 2)
                a(oreg[:, bass.ds(g, 1), 0:TP], pb[7][:, :].rearrange("p (o t) -> p o t", o=1))
                a(oreg[:, bass.ds(g, 1), TP:T], pb[5][:, 440:440 + TS].rearrange("p (o t) -> p o t", o=1))
                act.drain().then_inc(o_ok, 1)

            def evict_mla(i):
                if later(i):
                    act.wait_ge(s_ok, i)
                for hf in range(2):
                    act.wait_ge(proj, UB_MLA + hf + 1 + 6 * i)
                    a(qn[:, hf * HALF:(hf + 1) * HALF], pb[hf][:, 0:HALF]).then_inc(proj_free[hf], 1)
                for hf in range(2):
                    rope_copy(hf, 0, 2 + 2 * i + hf, UB_MLA + 2 + hf + 1 + 6 * i)
                    act.drain().then_inc(proj_free[hf], 1)
                    act.drain().then_inc(rope_in, 1)
                for hf in range(2):
                    act.wait_ge(proj, UB_MLA + 4 + hf + 1 + 6 * i)
                    a(kn[:, hf * KHALF:(hf + 1) * KHALF], pb[hf][:, 0:KHALF]).then_inc(proj_free[hf], 1)

            evict_mla(0)
            softmax_exp(0, SC_MLA)
            with act.Fori(1, NH) as i:
                evict_mla(i)
                copy_pt(i - 1)
                copy_o(i - 1)
                softmax_exp(i, SC_MLA)
            copy_pt(NH - 1)
            copy_o(NH - 1)
            act.wait_ge(vh_ok, NH)
            for n in range(2):
                act.wait_ge(tokm, 4 + n)
                for t in range(NT):
                    m = rows(t)
                    a(v_tok[0:m, t, n * 512:(n + 1) * 512], pb[t][0:m, :]).then_inc(tokm_ev, 1)

            def evict_fox(i):
                act.wait_ge(s_ok, NH + i)
                if later(i):
                    act.wait_ge(kt_ps, i)
                for hf in range(2):
                    act.wait_ge(proj, UB_FOX + hf + 1 + 4 * i)
                    a(qn[:, hf * HALF:(hf + 1) * HALF], pb[hf][:, 0:HALF], scale=SC_FOX).then_inc(proj_free[hf], 1)
                for hf in range(2):
                    act.wait_ge(proj, UB_FOX + 2 + hf + 1 + 4 * i)
                    a(kn[:, hf * HALF:(hf + 1) * HALF], pb[hf][:, 0:HALF]).then_inc(proj_free[hf], 1)

            def copy_keys(i):
                act.wait_ge(kt_ps, i + 1)
                if later(i):
                    act.wait_ge(kt_out, 32 * i)
                act.wait_ge(out_s, 16 * 4)
                a(ktok[:, 0:QT, :], pb[5][:, :].rearrange("p (t d) -> p t d", t=QT))
                a(ktok[0:TS, QT, :], pb[6][0:TS, 0:P])
                act.drain().then_inc(kt_ok, 1)

            evict_fox(0)
            softmax_exp(NH, 1.0)
            copy_keys(0)
            with act.Fori(1, NH) as i:
                evict_fox(i)
                copy_pt(NH - 1 + i)
                copy_o(NH - 1 + i)
                softmax_exp(NH + i, 1.0)
                copy_keys(i)
            copy_pt(2 * NH - 1)
            copy_o(2 * NH - 1)
            act.wait_ge(vh_ok, 2 * NH)
            act.wait_ge(kt_out, 32 * NH)
            act.wait_ge(v_out, 32)
            with act.Fori(0, KC) as i:
                for hf in range(2):
                    act.wait_ge(mg_ps, 2 * i + hf + 1)
                    act.wait_ge(mg_free[hf], i + 1)
                    a(sg[:, 2 * hf, :], pb[4 * hf][:, 0:HALF], ACT.Sigmoid)
                    a(sg[:, 2 * hf + 1, :], pb[4 * hf + 1][:, 0:HALF], ACT.Sigmoid)
                    act.drain().then_inc(sig_ok, 1)
            act.wait_ge(mg_ps, 2 * KC)
            act.dma_start(oreg[:, 0:4, :], x_t[:, 0:4, :]).then_inc(x_in2[0], 16)
            act.dma_start(oreg[:, 4:KC, :], x_t[:, 4:KC, :]).then_inc(x_in2[1], 16)
            root(1)
            norm(1, 3 * KC)
            act.dma_start(fgb, final_g.to_broadcast([P, D])).then_inc(fg_in, 16)
            act.wait_ge(s_clear, 1)
            with act.Fori(0, KC // 4) as i:
                for j in range(4):
                    n = 4 * i + j
                    for hf in range(2):
                        act.wait_ge(proj, UB_WQ + 2 * j + hf + 1 + 8 * i)
                        a(qn_peer[:, hf * HALF:(hf + 1) * HALF], pb[hf][:, 0:HALF]).then_inc(proj_free[hf], 1)
                    act.drain().then_inc(q_ok, 1)
                    act.wait_ge(sc_ps, n + 1)
                    act.wait_ge(rt_used, 2 * i + j // 2 + 1)
                    a(s_head[:, j // 2, 0:QT, j % 2, :], pb[2][:, :].rearrange("p (t k) -> p t k", t=QT))
                    a(s_head[0:TS, j // 2, QT, j % 2, :], pb[3][0:TS, 0:P])
                    act.drain().then_inc(sc_ok, 1)
            def dense_out(i, first=False):
                for j in range(4):
                    act.wait_ge(a_ps, 4 * i + j + 1)
                    if not first or j >= 2:
                        act.wait_ge(a_st[j % 2], 32 * i + 16 * (j // 2))
                    a(stage[:, j % 2, :], pb[j][:, 0:TD]).then_inc(a_free[j], 1)
                    act.wait_ge(a_free[j], i + 2)
                    act.dma_start(dots_dram[bass.ds(P * (4 * i + j), P), :], stage[:, j % 2, :]).then_inc(a_st[j % 2], 16)

            def to_sbuf(dst, banks, m):
                for c in range(4):
                    a(dst[0:m, c * 512:(c + 1) * 512], pb[banks + c][0:m, :])

            act.wait_ge(g2_ps, 1)
            to_sbuf(g2b, 4, P)
            act.drain().then_inc(g2_ok, 1)
            act.wait_ge(smx_in, 1)
            a(gates[:, :], gates[:, :], ACT.Exp).then_inc(smx_ok, 1)
            dense_out(0, True)
            act.wait_ge(ht_ps, 1)
            to_sbuf(h2_tok[0], 4, P)
            act.drain().then_inc(ht_ok, 1)
            with act.Fori(1, D0) as i:
                dense_out(i)
            act.wait_ge(ht_ps, 2)
            for g in range(4):
                for c in range(4):
                    a(h2_tok[1][32 * g:32 * g + TS, c * 512:(c + 1) * 512], pb[4 + c][0:TS, :])
            act.drain().then_inc(ht_ok, 1)
            with act.Fori(D0, D1) as i:
                dense_out(i)

            def gelu(n, c0, w):
                act.wait_ge(dot_ok, n + 1)
                a(wts[:, c0:c0 + w], wts[:, c0:c0 + w], ACT.Gelu).then_inc(gelu_ok, 1)

            gelu(0, (QT - 1) * SLOTS, SLOTS)
            gelu(1, QT * SLOTS, TS)
            with act.Fori(D1, NK // 4) as i:
                dense_out(i)

            def dots_in(i):
                for lap in range(2):
                    act.wait_ge(ss_in[lap], 16 * GR * (i + 1))
                    a(wts[:, bass.ds(FB * i + GR * lap, GR)], got[:, lap, :]).then_inc(ss_free[lap], 1)
                act.drain()
                w = wts[:, bass.ds(FB * i, FB)]
                a(w, w, ACT.Gelu).then_inc(gelu_ok, 1)

            def finish(n, t):
                m = rows(t)
                act.wait_ge(y_pre, n + 1)
                a(sq_junk[0:m, :], accs[n][0:m, :], ACT.Square, accum_out=stat[0:m, 0, t:t + 1])
                act.drain().then_inc(y_ss, 1)
                act.wait_ge(y_rs, n + 1)
                a(stat[0:m, 1, t:t + 1], stat[0:m, 1, t:t + 1], ACT.Sqrt).then_inc(y_rs2, 1)
                act.wait_ge(y_ok, n + 1)
                dst = y_p[0, t * P:(t + 1) * P, :] if t < QT else y_s[0, :, :]
                act.dma_start(dst, accs[n][0:m, :]).then_inc(y_out[ACC[n]], 16)

            dots_in(0)
            for n, t in enumerate(ORDER):
                if t == QT:
                    act.wait_ge(g2_ps, 2)
                    to_sbuf(g2b_s, 4, P)
                    act.drain().then_inc(g2_ok, 1)
                    dots_in(1)
                if t < DN:
                    with act.Fori(max(2, TRIP * t + 1), min(TRIP * (t + 1), TRIP * DN - 1) + 1) as i:
                        dots_in(i)
                finish(n, t)
            for j in range(3):
                act.wait_ge(y_out[j], 16 * ACC.count(j))

        @block.vector
        def _(dve):
            v = nc.vector


            def mod_out(n, batch, idx, ps):
                dve.wait_ge(col_ps, batch + 2)
                v.tensor_tensor(mod[:, bass.ds(idx, n), :], ps.rearrange("p (n g) -> p n g", g=2),
                                bad[:, bass.ds(idx, n)].rearrange("p (n o) -> p n o", o=1).to_broadcast([P, n, 2]),
                                ALU.add).then_inc(col_ok, 1)

            def mod_blocks(base, js, i, idx):
                for q, j in enumerate(js):
                    b = base + j
                    sl = b % RING
                    dve.wait_ge(w_in[sl], 16 * (b // RING + 1) + 16 * i)
                    for c in range(4):
                        cc = slice(c * 512, (c + 1) * 512)
                        v.tensor_tensor_reduce(out=prod, in0=ring[:, sl, cc], in1=crow[:, 0, cc], scale=1.0, scalar=0.0,
                                               op0=ALU.mult, op1=ALU.add, accum_out=part[:, q, c:c + 1])
                        dve.drain()
                    v.tensor_tensor_reduce(out=ring[:, sl, :], in0=ring[:, sl, :], in1=crow[:, 1, :], scale=1.0, scalar=0.0,
                                           op0=ALU.mult, op1=ALU.add, accum_out=msum[:, q, 1:2]).then_inc(w_used[sl], 1)
                dve.drain()
                n = len(js)
                v.reduce_sum(msum[:, 0:n, 0:1].rearrange("p n o -> p (n o)"), part[:, 0:n, :], AX.X)
                dve.drain()
                v.tensor_tensor(mod[:, bass.ds(idx, n), :], msum[:, 0:n, :],
                                bad[:, bass.ds(idx, n)].rearrange("p (n o) -> p n o", o=1).to_broadcast([P, n, 2]), ALU.add)
                dve.drain()

            def norm(n):
                for hf in range(2):
                    dve.wait_ge(ssq_ok, 2 * n + hf + 1)
                    v.tensor_scalar(rstd[:, hf * HALF:(hf + 1) * HALF], pb[hf][:, 0:HALF], 1.0 / D, EPS, ALU.mult, ALU.add)
                dve.drain()
                v.reciprocal(rstd[:, :], rstd[:, :])
                dve.drain().then_inc(var_ok, 1)

            def scaled(n):
                dve.wait_ge(rstd_ok, n + 1)
                with dve.Fori(0, KC) as k:
                    v.tensor_tensor(hreg[:, bass.ds(k, 1), :].rearrange("p o t -> p (o t)"),
                                    oreg[:, bass.ds(k, 1), :].rearrange("p o t -> p (o t)"), rstd[:, :], ALU.mult).then_inc(hn_ok, 1)

            def coefs(g, scale0):
                v.tensor_scalar(cf[:, :, :], mod[:, scale0:scale0 + KC, :], 1.0, None, ALU.add)
                dve.drain()
                v.tensor_tensor(cf[:, :, :], cf[:, :, :], g[:, :].rearrange("p (k o) -> p k o", o=1).to_broadcast([P, KC, 2]), ALU.mult)
                dve.drain().then_inc(cf_ok, 1)

            v.memset(stat[:, :, :], 1.0)
            v.memset(logf[:, 0:5, :], 0.0)
            v.memset(fw[:, :, :], 0.0)
            def squares(k):
                dve.wait_ge(x_in[k], 16)
                v.tensor_tensor(hreg[:, 4 * k:4 * k + 4, :], oreg[:, 4 * k:4 * k + 4, :], oreg[:, 4 * k:4 * k + 4, :], ALU.mult)

            for t0, t1 in A_PARTS:
                if t0 == 0:
                    for i in range(t1):
                        if i == 0:
                            dve.wait_ge(bada_in, 16)
                        if 1 <= i <= 4:
                            squares(i - 1)
                        if i == 5:
                            dve.drain()
                            v.reduce_sum(rstd[:, :], hreg[:, :, :].rearrange("p k t -> p t k"), AX.X)
                            dve.drain().then_inc(sq_ok, 1)
                        mod_out(4, i, 4 * i, pb[6][:, 0:8])
                    norm(0)
                    scaled(0)
                else:
                    with dve.Fori(t0, t1) as i:
                        mod_out(4, i, 4 * i, pb[6][:, 0:8])
            dve.drain()
            dve.wait_ge(small_in, 16 * NSMALL)
            coefs(g1T, KC)

            dve.wait_ge(lat_ss, 1)
            v.tensor_scalar(stat[:, 1, :], stat[:, 0, :], 1.0 / LORA, EPS, ALU.mult, ALU.add)
            dve.drain()
            v.reciprocal(stat[:, 1, :], stat[:, 1, :])
            dve.drain().then_inc(lat_rs, 1)

            def rotate(dst, hf, n):
                dve.wait_ge(rope_in, n)
                cols = slice(hf * HALF, (hf + 1) * HALF)
                v.tensor_tensor(rope_x, rope_x, cn["cos"][0:ROPE, cols], ALU.mult)
                v.tensor_tensor(rope_r, rope_r, cn["sin"][0:ROPE, cols], ALU.mult)
                dve.drain()
                v.tensor_tensor(dst[:, cols], rope_x, rope_r, ALU.add)
                dve.drain().then_inc(rope_ok, 1)

            for hf in range(2):
                rotate(krT, hf, hf + 1)
            dve.wait_ge(f_ps, 1)
            for t in range(NT):
                m = rows(t)
                v.tensor_tensor(fw[0:m, 0, t * NH:(t + 1) * NH], pb[7][0:m, t * NH:(t + 1) * NH], fb[0:m, :], ALU.add)
            dve.drain()
            v.tensor_scalar(fw[:, 1, :], fw[:, 0, :], -1.0, None, ALU.mult)
            v.tensor_scalar(fw[:, 4, :], fw[:, 0, :], 0.0, None, ALU.min)
            dve.drain()
            v.tensor_tensor(fw[:, 1, :], fw[:, 1, :], fw[:, 0, :], ALU.max)
            dve.drain().then_inc(f_z, 1)
            dve.wait_ge(lat_rs, 2)
            for t in range(NT):
                m = rows(t)
                v.scalar_tensor_tensor(lat_tok[0:m, t, :], pb[t][0:m, :], stat[0:m, 1, t:t + 1], kvgb[0:m, :],
                                       ALU.mult, ALU.mult).then_inc(lat_ok, 1)
            dve.wait_ge(f_l, 1)
            v.tensor_tensor(fw[:, 5, :], fw[:, 4, :], fw[:, 3, :], ALU.subtract)
            dve.drain()
            for t in range(NT):
                m = rows(t)
                v.tensor_copy(logf[0:m, t, :], fw[0:m, 5, t * NH:(t + 1) * NH])
            dve.drain().then_inc(logf_ok, 1)
            dve.wait_ge(cum_ps, 1)
            for a_, b_, src in ((0, TP, pb[5][0:NH, 0:TP]), (TP, T, pb[6][0:NH, PAST:PAST + TS]), (T, NKEY, pb[6][0:NH, 0:PAST])):
                v.tensor_copy(frow[:, 0, a_:b_], src)
            dve.drain()
            v.tensor_scalar(frow[:, 1, :], frow[:, 0, :], -1.0, None, ALU.mult)
            dve.drain().then_inc(frow_ok, 1)

            def row_max(g, mask, scale):
                dve.wait_ge(s_ok, g + 1)
                for t in range(QT):
                    b, c = S_AT[t]
                    d = pb[b][:, c + t * P:c + (t + 1) * P]
                    v.tensor_tensor(d, d, mask, ALU.add)
                if scale == 1.0:
                    b, c = S_AT[QT]
                    d = pb[b][0:TS, c:c + TS]
                    v.tensor_tensor(d, d, mask[0:TS, 0:TS], ALU.add)
                dve.drain()
                for t in range(NT):
                    m, (b, c) = rows(t), S_AT[t]
                    v.reduce_max(stat[0:m, 2, t:t + 1], pb[b][0:m, c:c + S_W[t]], AX.X)
                dve.drain()
                v.tensor_scalar(stat[:, 2, :], stat[:, 2, :], -scale, None, ALU.mult)
                dve.drain().then_inc(mx_ok, 1)

            def divide(g):
                dve.wait_ge(exp_ok, g + 1)
                v.reciprocal(stat[:, 3, :], stat[:, 3, :])
                dve.drain()
                for t in range(NT):
                    m = rows(t)
                    pr = prob[0:m, P_AT[t]:P_AT[t] + S_W[t]]
                    v.tensor_scalar(pr, pr, stat[0:m, 3, t:t + 1], None, ALU.mult)
                dve.drain().then_inc(prob_ok, 1)

            dve.wait_ge(crow_ok, 1)
            with dve.Fori(0, NH) as i:
                mod_blocks(B_MLA, (0, 1), i, 2 * KC + 2 * i)
                for hf in range(2):
                    rotate(qr, hf, 2 + 2 * i + hf + 1)
                row_max(i, cn["mask_mla"], SC_MLA)
                divide(i)
            with dve.Fori(0, NH) as i:
                mod_blocks(B_FOX, (0, 1), i, 3 * KC + 2 * i)
                row_max(NH + i, cn["mask_fox"], 1.0)
                divide(NH + i)

            dve.wait_ge(o_ok, 2 * NH + 1)
            dve.wait_ge(kt_out, 32 * NH)
            with dve.Fori(0, KC) as i:
                mod_blocks(B_MERGE, (1,), i, 4 * KC + i)
                for hf in range(2):
                    dve.wait_ge(sig_ok, 2 * i + hf + 1)
                    s0, s1 = sg[:, 2 * hf, :], sg[:, 2 * hf + 1, :]
                    v.tensor_tensor(s0, s0, pb[4 * hf + 2][:, 0:HALF], ALU.mult)
                    v.tensor_tensor(s1, s1, pb[4 * hf + 3][:, 0:HALF], ALU.mult)
                    dve.drain()
                    v.tensor_tensor(merged[:, bass.ds(i, 1), hf * HALF:(hf + 1) * HALF].rearrange("p o t -> p (o t)"), s0, s1, ALU.add)
                    dve.drain().then_inc(mg_free[hf], 1)
            v.memset(rstd[:, :], 0.0)

            def add_out(i):
                mod_blocks(B_OUT, (0, 1), i, 5 * KC + 2 * i)
                for j in range(2):
                    for hf in range(2):
                        dve.wait_ge(proj, UB_OUT + 2 * j + hf + 1 + 4 * i)
                        parts = [(0, HALF, 0)] if hf == 0 else [(HALF, TP, 0), (TP, T, 1)]
                        for a_, b_, g in parts:
                            xr = oreg[:, bass.ds(2 * i + j, 1), a_:b_].rearrange("p o t -> p (o t)")
                            v.scalar_tensor_tensor(xr, pb[hf][:, a_ - hf * HALF:b_ - hf * HALF],
                                                   mod[:, bass.ds(2 * KC + 2 * i + j, 1), g:g + 1].rearrange("p o g -> p (o g)"),
                                                   xr, ALU.mult, ALU.add)
                        dve.drain().then_inc(proj_free[hf], 1)
                    xr = oreg[:, bass.ds(2 * i + j, 1), :].rearrange("p o t -> p (o t)")
                    v.tensor_tensor(hreg[:, 0, :], xr, xr, ALU.mult)
                    dve.drain()
                    v.tensor_tensor(rstd[:, :], rstd[:, :], hreg[:, 0, :], ALU.add)

            dve.wait_ge(x_in2[0], 16)
            with dve.Fori(0, 2) as i:
                add_out(i)
            dve.wait_ge(x_in2[1], 16)
            with dve.Fori(2, KC // 2) as i:
                add_out(i)
            dve.drain().then_inc(sq_ok, 1)
            norm(1)
            coefs(g2T, 4 * KC)
            scaled(1)

            dve.wait_ge(proj_free[1], UB_WQ // 2)
            v.memset(s_head[:, :, QT, :, :], 0.0)
            dve.drain().then_inc(s_clear, 1)

            def top16(src, rest, val, ind):
                n = len(src)
                for q in range(n):
                    v.max(val[q][:, 0:8], src[q])
                dve.drain()
                for q in range(n):
                    v.max_index(ind[q][:, 0:8], val[q][:, 0:8], src[q])
                    v.match_replace(rest[q], val[q][:, 0:8], src[q], -3.0e38)
                dve.drain()
                for q in range(n):
                    v.max(val[q][:, 8:16], rest[q])
                dve.drain()
                for q in range(n):
                    v.max_index(ind[q][:, 8:16], val[q][:, 8:16], rest[q])
                dve.drain()

            full = [P, NT, TOPK, TOPK]
            lists = [(t, s) for t in range(NT) for s in range(2)]
            with dve.Fori(0, PH // 2) as i:
                for b in range(2):
                    h = 2 * i + b
                    dve.wait_ge(sc_ok, 4 * i + 2 * b + 3)
                    dve.sem_inc(dve_on, 1)
                    top16([s_head[:, b, t, s, :] for t, s in lists], [s_rest[:, t, s, :] for t, s in lists],
                          [top_v[:, t, s, :] for t, s in lists], [top_i[:, t, s, :] for t, s in lists])
                    dve.drain().then_inc(rt_used, 1)
                    va = top_v[:, :, 0, :].rearrange("p t (k o) -> p t k o", o=1).to_broadcast(full)
                    vb = top_v[:, :, 1, :].rearrange("p t (o k) -> p t o k", o=1).to_broadcast(full)
                    v.tensor_tensor(hots[0], va, vb, ALU.add)
                    v.tensor_copy(top_if, top_i)
                    dve.drain()
                    top16([cand[:, t, :] for t in range(NT)], [cand_rest[:, t, :] for t in range(NT)],
                          [sc_v[:, t, :] for t in range(NT)], [sel[:, t, :] for t in range(NT)])
                    v.tensor_tensor(gates[:, :].rearrange("p (t h k) -> p t h k", t=NT, h=PH)[:, :, bass.ds(h, 1), :].rearrange("p t o k -> p t (o k)"),
                                    sc_v, sc_v[:, :, 0:1].to_broadcast([P, NT, TOPK]), ALU.subtract)
                    v.tensor_scalar(sel_a, sel, 4, None, ALU.logical_shift_right)
                    v.tensor_scalar(sel_b, sel, 15, None, ALU.bitwise_and)
                    dve.drain()
                    v.tensor_copy(sel_f[:, 0], sel_a)
                    v.tensor_copy(sel_f[:, 1], sel_b)
                    dve.drain()
                    iota = cn["iota"].rearrange("p (a b j) -> p a b j", a=1, b=1).to_broadcast(full)
                    for s in range(2):
                        v.tensor_tensor(hots[s], sel_f[:, s].rearrange("p t (k o) -> p t k o", o=1).to_broadcast(full),
                                        iota, ALU.is_equal)
                    dve.drain()
                    for s in range(2):
                        v.tensor_tensor(hots[s], hots[s], top_if[:, :, s, :].rearrange("p t (o j) -> p t o j", o=1).to_broadcast(full), ALU.mult)
                    dve.drain()
                    for s in range(2):
                        v.reduce_sum(sel_f[:, s], hots[s], AX.X)
                    dve.drain()
                    v.scalar_tensor_tensor(ex_f, sel_f[:, 0], float(NK), sel_f[:, 1], ALU.mult, ALU.add)
                    dve.drain()
                    v.tensor_copy(experts[:, :].rearrange("p (t h k) -> p t h k", t=NT, h=PH)[:, :, bass.ds(h, 1), :].rearrange("p t o k -> p t (o k)"), ex_f)
                    v.scalar_tensor_tensor(at_dot[:, :].rearrange("p (t h k) -> p t h k", t=NT, h=PH)[:, :, bass.ds(h, 1), :].rearrange("p t o k -> p t (o k)"),
                                           ex_f, float(TD), cn["token"].rearrange("p (t o) -> p t o", o=1).to_broadcast([P, NT, TOPK]), ALU.mult, ALU.add)
                    dve.drain()
            dve.drain().then_inc(smx_in, 1)
            dve.wait_ge(smx_ok, 1)
            g16 = gates[:, :].rearrange("p (h k) -> p h k", k=TOPK)
            v.reduce_sum(gsum[:, :], g16, AX.X)
            dve.drain()
            v.reciprocal(gsum[:, :], gsum[:, :])
            dve.drain()
            v.tensor_tensor(g16, g16, gsum[:, :].rearrange("p (h o) -> p h o", o=1).to_broadcast([P, NT * PH, TOPK]), ALU.mult)
            dve.drain()
            c0 = QT * SLOTS
            for g in range(1, 4):
                v.tensor_copy(experts[32 * g:32 * g + 32, c0:c0 + 32], experts[0:TS, c0 + 32 * g:c0 + 32 * g + 32])
                v.tensor_copy(gates[32 * g:32 * g + 32, c0:c0 + 32], gates[0:TS, c0 + 32 * g:c0 + 32 * g + 32])
            dve.drain().then_inc(route_ok, 1)

            def dot_products(n, t, q0, trips, off):
                dve.wait_ge(ht_ok, n + 1)
                with dve.Fori(q0, q0 + trips) as i:
                    for e in range(FB):
                        r, lap = e % GR, e // GR
                        dve.wait_ge(g_in[r], 32 * i + 16 * (lap + 1))
                        v.tensor_tensor_reduce(out=vring[:, r, :], in0=vring[:, r, :], in1=h2_tok[n], scale=1.0, scalar=0.0,
                                               op0=ALU.mult, op1=ALU.add, accum_out=dots[:, e:e + 1]).then_inc(g_used[r], 1)
                    dve.drain()
                    v.tensor_copy(wts[:, bass.ds(FB * (i + off), FB)], dots[:, :])
                    dve.drain()
                dve.drain().then_inc(dot_ok, 1)

            def weights(n, c0, w):
                dve.wait_ge(gelu_ok, n + 1)
                v.tensor_tensor(wts[:, c0:c0 + w], wts[:, c0:c0 + w], gates[:, c0:c0 + w], ALU.mult)
                dve.drain()

            def clear(n):
                if n > 2:
                    dve.wait_ge(y_out[ACC[n]], 16)
                v.memset(accs[n], 0.0)
                dve.drain()

            def add_row(n, row, r, landed, col):
                dve.wait_ge(g_in[r], landed)
                v.scalar_tensor_tensor(accs[n], row, wts[:, bass.ds(col, 1)], accs[n], ALU.mult, ALU.add)
                dve.drain().then_inc(g_used[r], 1)

            def values(n, q0, trips, off):
                with dve.Fori(q0, q0 + trips) as i:
                    for e in range(FB):
                        add_row(n, vring[:, e % GR, :], e % GR, 32 * i + 16 * (e // GR + 1), FB * (i + off) + e)

            def values_deep(n, i):
                dve.wait_ge(gelu_ok, i + 3)
                w = wts[:, bass.ds(FB * i, FB)]
                v.tensor_tensor(w, w, gates[:, bass.ds(FB * i, FB)], ALU.mult)
                dve.drain()
                for e in range(FB):
                    add_row(n, deep[e], e, landed_deep(e, i), FB * i + e)

            def finish(n, t):
                dve.wait_ge(fg_in, 16)
                m = rows(t)
                y = accs[n]
                dve.wait_ge(x2t_ps, n + 1)
                if t == QT:
                    dve.wait_ge(sum_ps, 1)
                    dve.wait_ge(g2_ok, 2)
                    for c in range(4):
                        cc = slice(c * 512, (c + 1) * 512)
                        v.tensor_tensor(y[0:m, cc], pb[c][0:m, :], g2b_s[0:m, cc], ALU.mult)
                else:
                    v.tensor_tensor(y[0:m, :], y[0:m, :], g2b[0:m, :], ALU.mult)
                dve.drain()
                for c in range(4):
                    cc = slice(c * 512, (c + 1) * 512)
                    v.tensor_tensor(y[0:m, cc], y[0:m, cc], pb[4 + c][0:m, :], ALU.add)
                dve.drain().then_inc(acc_free, 1)
                dve.drain().then_inc(y_pre, 1)
                dve.wait_ge(y_ss, n + 1)
                st = stat[0:m, 1, t:t + 1]
                v.tensor_scalar(st, stat[0:m, 0, t:t + 1], 1.0 / D, EPS, ALU.mult, ALU.add)
                dve.drain()
                v.reciprocal(st, st)
                dve.drain().then_inc(y_rs, 1)
                dve.wait_ge(y_rs2, n + 1)
                v.scalar_tensor_tensor(y[0:m, :], y[0:m, :], st, fgb[0:m, :], ALU.mult, ALU.mult).then_inc(y_ok, 1)

            late = (QT - 1) * TRIP
            dot_products(0, QT - 1, 0, TRIP, late)
            dot_products(1, QT, TRIP, TRIP_S, late)
            weights(0, (QT - 1) * SLOTS, SLOTS)
            q, h = TRIP + TRIP_S, TRIP - AHEAD
            clear(0)
            values(0, q, h, late - q)
            weights(1, QT * SLOTS, TS)
            clear(1)
            values(1, q + h, TRIP_S, late + TRIP - q - h)
            dve.drain().then_inc(acc_ok, 1)
            values(0, q + h + TRIP_S, AHEAD, late - q - TRIP_S)
            finish(0, QT - 1)
            for t in range(DN):
                clear(2 + t)
                if t == 0:
                    values_deep(2, 0)
                    finish(1, QT)
                with dve.Fori(max(1, TRIP * t), TRIP * (t + 1)) as i:
                    values_deep(2 + t, i)
                finish(2 + t, t)

        @block.gpsimd
        def _(pool):
            g = nc.gpsimd
            pool.sem_inc(rt_used, 2)
            for s in w_used + mg_free + g_used + a_free + ss_free + [sc_ok, col_ps, col_ok, o_ok, pv_ok]:
                pool.sem_inc(s, 1)
            pool.wait_ge(lat_ok, NT)
            pool.dma_start(lat_p[0, 0].rearrange("(t p) c -> p t c", p=P), lat_tok[:, 0:QT, :]).then_inc(lat_out, 16)
            pool.dma_start(lat_s[0, 0], lat_tok[0:TS, QT, :]).then_inc(lat_out, 16)
            pool.wait_ge(logf_ok, 1)
            pool.dma_start(lf_p[0, 0].rearrange("(t p) h -> p t h", p=P), logf[:, 0:QT, :]).then_inc(out_s, 16)
            pool.dma_start(lf_s[0, 0], logf[0:TS, QT, :]).then_inc(out_s, 16)
            pool.wait_ge(frow_ok, 1)
            pool.dma_start(aug_q_dram[:, 0, :], frow[:, 0, 0:T]).then_inc(aug_st, 16)
            pool.dma_start(aug_k_dram[:, 1, :], frow[:, 1, :]).then_inc(aug_st, 16)
            pool.dma_start(aug_q_dram[:, 1, :], aug_ones[:, 0:T]).then_inc(aug_st, 16)
            pool.dma_start(aug_k_dram[:, 0, :], aug_ones).then_inc(aug_st, 16)
            pool.wait_ge(krt_ok, 1)
            pool.dma_start(kr_p[0, 0].rearrange("(t p) d -> p t d", p=P), ktok[:, 0:QT, 0:ROPE]).then_inc(out_s, 16)
            pool.dma_start(kr_s[0, 0], ktok[0:TS, QT, 0:ROPE]).then_inc(out_s, 16)

            def head_values(gh, h):
                pool.wait_ge(pv_ok, gh + 1)
                for t in range(6):
                    m = rows(t) if t < 5 else P
                    g.tensor_copy(vh[0:m, t, :], v_tok[0:m, t, bass.ds(h * HD, HD)])
                pool.drain().then_inc(vh_ok, 1)

            pool.wait_ge(tokm_ev, 12)
            head_values(0, 0)
            with pool.Fori(1, NH) as i:
                head_values(i, i)
            pool.wait_ge(s_ok, NH)
            pool.dma_start(kf_past, kf_cache).then_inc(kfp_in, 16)
            pool.dma_start(v_tok[:, 5, :], vf_cache).then_inc(vfp_in, 16)
            pool.wait_ge(tokm_ev, 12 + 2 * NT)
            pool.dma_start(vf_p[0, 0].rearrange("(t p) h d -> p t (h d)", p=P), v_tok[:, 0:QT, :]).then_inc(v_out, 16)
            pool.dma_start(vf_s[0, 0].rearrange("s h d -> s (h d)"), v_tok[0:TS, QT, :]).then_inc(v_out, 16)
            pool.wait_ge(vfp_in, 16)
            pool.wait_ge(aug_st, 64)
            kfp_o = kf_p[0, 0].rearrange("(t p) h d -> p t h d", p=P)
            with pool.Fori(0, NH) as i:
                pool.wait_ge(s_ok, NH + i)
                pool.sem_inc(pool_on, 1)
                pool.dma_start(aug_q, aug_q_dram[bass.ds(i, 1)].rearrange("o r t -> (o r) t")).then_inc(aug_in, 16)
                pool.dma_start(aug_k, aug_k_dram[bass.ds(i, 1)].rearrange("o r t -> (o r) t")).then_inc(aug_in, 16)
                head_values(NH + i, i)
                pool.wait_ge(kt_ok, i + 1)
                pool.sem_inc(pool_on, 1)
                pool.dma_start(kfp_o[:, :, bass.ds(i, 1), :].rearrange("p t o d -> p t (o d)"), ktok[:, 0:QT, :]).then_inc(kt_out, 16)
                pool.dma_start(kf_s[0, 0, :, bass.ds(i, 1), :].rearrange("s o d -> s (o d)"), ktok[0:TS, QT, :]).then_inc(kt_out, 16)

            pool.wait_ge(route_ok, 1)

            def index(src, c, place, s, n, free=None):
                idx = idx8[:, place, :]
                if free is not None:
                    pool.wait_ge(*free)
                    pool.sem_inc(pool_on, 1)
                g.tensor_copy(idx, src[:, bass.ds(c, GR)]).then_inc(s, 1)
                pool.wait_ge(s, n)
                pool.sem_inc(pool_on, 1)
                return idx

            def gather_row(table, idx, r, place):
                g.indirect_dma_start(out=deep[place], out_offset=None, in_=table,
                                     in_offset=bass.IndirectOffsetOnAxis(ap=idx[:, r:r + 1], axis=0)).then_inc(g_in[place], 16)

            def gather_dot(idx, lap, r):
                g.indirect_dma_start(out=got[:, lap, r:r + 1], out_offset=None, in_=dots_dram.rearrange("e (t o) -> (e t) o", o=1),
                                     in_offset=bass.IndirectOffsetOnAxis(ap=idx[:, r:r + 1], axis=0)).then_inc(ss_in[lap], 16)

            def gathers(table, q, off, dots=(), is_deep=False):
                for lap in range(2):
                    if is_deep:
                        for r in range(GR):
                            pool.wait_ge(g_used[GR * lap + r], free_deep(GR * lap + r, q))
                        pool.sem_inc(pool_on, 1)
                    rows_ = index(experts, FB * (q + off) + GR * lap, lap, idx_ok[0], 2 * (q + (SHALLOW if is_deep else 0)) + lap + 1)
                    share = [(i, l2) for i in dots for l2 in range(2)]
                    share = share[len(dots) * lap:len(dots) * (lap + 1)]
                    at = [(index(at_dot, FB * i + GR * l2, 2 + l2, idx_ok[1], 2 * i + l2 + 1, (ss_free[l2], i + 1)), l2)
                          for i, l2 in share]
                    for r in range(GR):
                        if not is_deep:
                            pool.wait_ge(g_used[r], 2 * q + lap + 1)
                            pool.sem_inc(pool_on, 1)
                        gather_row(table, rows_, r, GR * lap + r if is_deep else r)
                        for idx, l2 in at:
                            gather_dot(idx, l2, r)

            late = (QT - 1) * TRIP
            with pool.Fori(0, TRIP + TRIP_S) as q:
                gathers(peer_u, q, late)
            q0 = TRIP + TRIP_S
            with pool.Fori(q0, q0 + TRIP - AHEAD) as q:
                gathers(peer_v, q, late - q0)
            q1 = q0 + TRIP - AHEAD
            with pool.Fori(q1, q1 + TRIP_S) as q:
                gathers(peer_v, q, late + TRIP - q1)
            for j in range(2):
                pool.wait_ge(a_st[j], 16 * NK // 2)
            q1 += TRIP_S
            with pool.Fori(0, AHEAD) as i:
                gathers(peer_v, i + q1, late - q0 - TRIP_S, [i])
            with pool.Fori(0, DN * TRIP - AHEAD) as i:
                gathers(peer_v, i, 0, [i + AHEAD], True)
            with pool.Fori(DN * TRIP - AHEAD, DN * TRIP) as i:
                gathers(peer_v, i, 0, (), True)
            pool.wait_ge(out_s, 64)
            pool.wait_ge(v_out, 32)
            pool.wait_ge(kt_out, 32 * NH)
            pool.wait_ge(lat_out, 32)


def kernel(**inp):
    import concourse.bacc as bacc
    from concourse.bass_utils import run_bass_kernel_spmd

    x = {k: np.ascontiguousarray(v) for k, v in inp.items()}

    def feat(a):
        return np.ascontiguousarray(a.T.reshape(-1, P, a.shape[0]).transpose(1, 0, 2))

    def cols(v):
        return np.ascontiguousarray(v.reshape(-1, P).T)

    def block(w):
        return w.reshape(-1, P, w.shape[1]).transpose(1, 0, 2).reshape(P, -1)

    def pad(*parts):
        b = np.zeros((P, D), np.float32)
        at = 0
        for p_ in parts:
            b[:, at:at + p_.shape[1]] = p_
            at += p_.shape[1]
        return b

    w_in, w_ada, ukv = x["w_in"][0], x["w_ada"][0], x["w_ukv"][0]
    q_w = HD + ROPE
    o_lat = NH * q_w
    o_kr = o_lat + LORA
    o_fox = o_kr + ROPE
    o_f = o_fox + 3 * NH * HD
    o_gm = o_f + NH
    o_gf = o_gm + D

    def ada(n):
        return block(w_ada[:, n * P:(n + 1) * P])

    def ada_t(n):
        return w_ada[:, n * P:(n + 1) * P].T

    stream = np.empty((NB, P, D), np.float32)
    n = [0]

    def put(b):
        stream[n[0]] = b
        n[0] += 1

    for j in range(ADA_A):
        put(ada(j))
    for c in range(CKV):
        put(block(w_in[c * 512:(c + 1) * 512, o_lat:o_kr]))
    put(pad(block(np.concatenate([w_in[:, o_kr:o_fox], w_in[:, o_f:o_gm]], axis=1))))
    ukv_h = ukv.reshape(LORA, NH, 2, HD)
    for c in range(MLAV):
        put(block(ukv_h[:, 4 * c:4 * c + 4, 1].reshape(LORA, 512)))
    for h in range(NH):
        put(ada_t(2 * KC + 2 * h))
        put(ada_t(2 * KC + 2 * h + 1))
        put(block(w_in[:, h * q_w:h * q_w + HD]))
        put(pad(block(w_in[:, h * q_w + HD:(h + 1) * q_w]), block(ukv_h[:, h, 0])))
    for c in range(2):
        for r in range(4):
            a = o_fox + 2 * NH * HD + c * 512
            put(block(w_in[r * 512:(r + 1) * 512, a:a + 512]))
    for h in range(NH):
        put(ada_t(3 * KC + 2 * h))
        put(ada_t(3 * KC + 2 * h + 1))
        put(block(w_in[:, o_fox + h * HD:o_fox + (h + 1) * HD]))
        put(block(w_in[:, o_fox + (NH + h) * HD:o_fox + (NH + h + 1) * HD]))
    for j in range(KC):
        c = slice(j * P, (j + 1) * P)
        put(block(w_in[:, o_gf + j * P:o_gf + (j + 1) * P]))
        put(ada_t(4 * KC + j))
        put(pad(block(x["w_o_mla"][0][:, c]), block(x["w_o_fox"][0][:, c])))
        put(block(w_in[:, o_gm + j * P:o_gm + (j + 1) * P]))
    for j in range(KC // 2):
        for q in range(2):
            put(ada_t(5 * KC + 2 * j + q))
        for q in range(2):
            put(block(x["w_out"][0][:, (2 * j + q) * P:(2 * j + q + 1) * P]))
    for j in range(KC):
        put(block(x["peer_wq"][0][:, j * P:(j + 1) * P]))
    for j in range(NK * NK // P):
        put(block(x["peer_u"][0][j * P:(j + 1) * P].T))
    assert n[0] == NB

    lay, cw = const_layout()
    cst = np.zeros((P, cw), np.float32)

    def const(name, a):
        cst[:a.shape[0], lay[name][0]:lay[name][0] + a.shape[1]] = a

    i = np.arange(P)
    const("ident", np.eye(P, dtype=np.float32))
    const("stack", (i[:, None] % TS == i[None, :]).astype(np.float32))
    const("band", (i[:, None] <= np.arange(TP)[None, :]).astype(np.float32))
    const("mask_mla", np.where(i[:, None] // CHUNK >= i[None, :] // CHUNK, 0.0, NEG).astype(np.float32))
    const("mask_fox", np.where(i[:, None] >= i[None, :], 0.0, NEG).astype(np.float32))
    const("iota", np.broadcast_to(np.arange(TOPK, dtype=np.float32), (P, TOPK)))
    const("ones", np.ones((P, P), np.float32))
    const("token", (np.arange(NT)[None, :] * P + i[:, None]).astype(np.float32))
    inv = (1.0 / (np.float32(10000.0) ** (np.arange(0, ROPE, 2, dtype=np.float32) / ROPE))).astype(np.float32)
    pos = np.concatenate([np.arange(TP), PAST + np.arange(TS)]).astype(np.float32)
    ang = (inv[:, None] * pos[None, :]).astype(np.float32)
    const("cos", np.concatenate([np.cos(ang), np.cos(ang)]))
    const("sin", np.concatenate([-np.sin(ang), np.sin(ang)]))

    arrays = {
        "wstream": stream,
        "x_t": feat(np.concatenate([x["x_prompt"][0], x["x_sample"][0]])),
        "c_t": feat(np.concatenate([x["c_prompt"], x["c_sample"]])),
        "c_rows": np.concatenate([x["c_prompt"], x["c_sample"]]).reshape(1, 2 * D),
        "b_ada": cols(x["b_ada"][0]),
        "g1": cols(x["norm1_g"][0]),
        "g2": cols(x["norm2_g"][0]),
        "kvg": x["kv_norm_g"],
        "final_g": x["final_g"][None],
        "fbias": x["fox_fbias"],
        "lat_cache": feat(x["cache_mla_latent"][0, 0]),
        "kr_cache": np.ascontiguousarray(x["cache_mla_krope"][0, 0].T),
        "kf_cache": np.ascontiguousarray(x["cache_fox_k"][0, 0].transpose(2, 1, 0)),
        "vf_cache": x["cache_fox_v"][0, 0].reshape(PAST, NH * HD),
        "logf_cache": x["cache_fox_logf"][0, 0],
        "keys": np.ascontiguousarray(np.stack([x["peer_keys1"][0].T, x["peer_keys2"][0].T], 1)),
        "peer_u": x["peer_u"][0],
        "peer_v": x["peer_v"][0],
        "aug_ones": np.ones((NH, NKEY), np.float32),
        "consts": cst,
    }
    shapes = [(1, TP, D), (1, TS, D)]
    for s in (TP, TS):
        shapes += [(1, 1, s, LORA), (1, 1, s, ROPE), (1, 1, s, NH, HD), (1, 1, s, NH, HD), (1, 1, s, NH)]
    f32 = mybir.dt.float32
    nc = bacc.Bacc("TRN2", target_bir_lowering=False, num_devices=1)
    args = {k: nc.dram_tensor(k, a.shape, f32, kind="ExternalInput").ap() for k, a in arrays.items()}
    outs = [nc.dram_tensor(f"out{j}", s, f32, kind="ExternalOutput").ap() for j, s in enumerate(shapes)]
    build(nc, outs=outs, **args)
    r = run_bass_kernel_spmd(nc, [arrays], core_ids=[0])
    return tuple(r.results[0][f"out{j}"] for j in range(len(shapes)))
```
